# Optimizing a Trainium2 kernel written in Bass

```python
import jax, jax.numpy as jnp
from jax import lax
import numpy as np

D_MODEL = 1024
BATCH = 1
SEQ = 256
DEPTH = 2
DEC_BATCH = 8
DEC_SEQ = 8
PAST_LEN = 1024
PAGE_SIZE = 128

SSD_EXPAND = 2
D_INNER = SSD_EXPAND * D_MODEL
SSD_HEAD_DIM = 64
SSD_HEADS = D_INNER // SSD_HEAD_DIM
SSD_GROUPS = 4
SSD_HEADS_PER_GROUP = SSD_HEADS // SSD_GROUPS
SSD_STATE = 128
SSD_CONV = 4
SSD_CHUNK = 128
CONV_DIM = D_INNER + 2 * SSD_GROUPS * SSD_STATE
D_IN_PROJ = D_INNER + CONV_DIM + SSD_HEADS
MLA_HEADS = 8
Q_LORA = 384
KV_LORA = 256
QK_NOPE = 128
QK_ROPE = 64
V_HEAD = 128
ROPE_THETA = 10000.0
ATTN_Q_BLOCK = 128
MOE_GROUPS = 4
EXPERTS_PER_GROUP = 8
N_EXPERTS = MOE_GROUPS * EXPERTS_PER_GROUP
EXPERT_FF = 256
GROUP_TOPK_SCORE = 2
EXPERT_TOPK = 2
N_SSD_LAYERS = (DEPTH + 1) // 2
N_MLA_LAYERS = DEPTH // 2
DEEPNORM_ALPHA = (2.0 * DEPTH) ** 0.25
DEEPNORM_BETA = (8.0 * DEPTH) ** -0.25
LN_EPS = 1e-5
RMS_EPS = 1e-6

kernel_name = 'hybrid_ssd_mla_hmoe_step'

def layer_norm(x, g, b):
    xf = x.astype(jnp.float32)
    mu = jnp.mean(xf, axis=-1, keepdims=True)
    var = jnp.mean(jnp.square(xf - mu), axis=-1, keepdims=True)
    return ((xf - mu) * lax.rsqrt(var + LN_EPS) * g.astype(jnp.float32) + b.astype(jnp.float32)).astype(x.dtype)

def rms_norm(x, g):
    xf = x.astype(jnp.float32)
    out = xf * lax.rsqrt(jnp.mean(jnp.square(xf), axis=-1, keepdims=True) + RMS_EPS) * g.astype(jnp.float32)
    return out.astype(x.dtype)

def rope_tables(pos):
    half = QK_ROPE // 2
    inv_freq = ROPE_THETA ** (-jnp.arange(half, dtype=jnp.float32) / half)
    ang = pos.astype(jnp.float32)[:, None] * inv_freq[None, :]
    return jnp.cos(ang), jnp.sin(ang)

def apply_rope(x, cos, sin):
    x1, x2 = jnp.split(x.astype(jnp.float32), 2, axis=-1)
    return jnp.concatenate([x1 * cos - x2 * sin, x2 * cos + x1 * sin], axis=-1).astype(x.dtype)

def causal_conv(xbc, conv_state, w, b):
    t = xbc.shape[1]
    xp = jnp.concatenate([conv_state.astype(xbc.dtype), xbc], axis=1)
    out = b
    for k in range(SSD_CONV):
        out = out + xp[:, k:k + t] * w[k]
    return jax.nn.silu(out), xp[:, t:]

def ssd_scan(xs, dt, a_neg, bm, cm, h0):
    bsz, t = xs.shape[:2]
    lc = min(SSD_CHUNK, t)
    nc = -(-t // lc)
    pad = nc * lc - t

    def prep(a):
        a = a.astype(jnp.float32)
        a = jnp.pad(a, [(0, 0), (0, pad)] + [(0, 0)] * (a.ndim - 2))
        return jnp.moveaxis(a.reshape((bsz, nc, lc) + a.shape[2:]), 1, 0)

    causal = jnp.tril(jnp.ones((lc, lc), dtype=bool))[None, :, :, None, None]

    def chunk_step(h, inp):
        xc, dtc, bc, cc = inp
        cum = jnp.cumsum(dtc * a_neg, axis=1)
        seg = cum[:, :, None] - cum[:, None, :]
        decay = jnp.exp(jnp.where(causal, seg, -jnp.inf))
        cb = jnp.einsum('blgn,bsgn->blsg', cc, bc)
        xdt = xc * dtc[..., None]
        y = jnp.einsum('blsgj,bsgjp->blgjp', cb[..., None] * decay, xdt)
        y = y + jnp.einsum('blgn,bgjpn->blgjp', cc, h) * jnp.exp(cum)[..., None]
        last = cum[:, -1]
        w_s = jnp.exp(last[:, None] - cum)[..., None]
        h = h * jnp.exp(last)[..., None, None] + jnp.einsum('bsgn,bsgjp->bgjpn', bc, xdt * w_s)
        return h, y

    h_fin, y = lax.scan(chunk_step, h0.astype(jnp.float32), (prep(xs), prep(dt), prep(bm), prep(cm)))
    y = jnp.moveaxis(y, 0, 1).reshape((bsz, nc * lc) + xs.shape[2:])[:, :t]
    return y.astype(xs.dtype), h_fin.astype(h0.dtype)

def ssd_mixer(x, conv_state, ssm_state, w_in, conv_w, conv_b, dt_bias, a_log, d_skip, norm_w, w_out):
    bsz, t, _ = x.shape
    z, xbc, dt = jnp.split(x @ w_in, [D_INNER, D_INNER + CONV_DIM], axis=-1)
    xbc, new_conv = causal_conv(xbc, conv_state, conv_w, conv_b)
    xs, bm, cm = jnp.split(xbc, [D_INNER, D_INNER + SSD_GROUPS * SSD_STATE], axis=-1)
    xs = xs.reshape(bsz, t, SSD_GROUPS, SSD_HEADS_PER_GROUP, SSD_HEAD_DIM)
    bm = bm.reshape(bsz, t, SSD_GROUPS, SSD_STATE)
    cm = cm.reshape(bsz, t, SSD_GROUPS, SSD_STATE)
    dt = jax.nn.softplus(dt.astype(jnp.float32) + dt_bias.astype(jnp.float32))
    dt = dt.reshape(bsz, t, SSD_GROUPS, SSD_HEADS_PER_GROUP)
    a_neg = -jnp.exp(a_log.astype(jnp.float32)).reshape(SSD_GROUPS, SSD_HEADS_PER_GROUP)
    h0 = ssm_state.reshape(bsz, SSD_GROUPS, SSD_HEADS_PER_GROUP, SSD_HEAD_DIM, SSD_STATE)
    y, h = ssd_scan(xs, dt, a_neg, bm, cm, h0)
    y = y + d_skip.reshape(SSD_GROUPS, SSD_HEADS_PER_GROUP)[..., None] * xs
    gated = (y.reshape(bsz, t, D_INNER) * jax.nn.silu(z)).astype(jnp.float32)
    gated = gated.reshape(bsz, t, SSD_GROUPS, D_INNER // SSD_GROUPS)
    gated = gated * lax.rsqrt(jnp.mean(jnp.square(gated), axis=-1, keepdims=True) + RMS_EPS)
    y = (gated.reshape(bsz, t, D_INNER) * norm_w.astype(jnp.float32)).astype(x.dtype)
    return y @ w_out, new_conv, h.reshape(bsz, SSD_HEADS, SSD_HEAD_DIM, SSD_STATE)

def latent_attention(q_lat, q_rope, k_lat, k_rope):
    bsz, t = q_lat.shape[:2]
    s = k_lat.shape[1]
    qb = min(ATTN_Q_BLOCK, t)
    nb = -(-t // qb)
    pad = nb * qb - t
    q_lat = jnp.pad(q_lat, [(0, 0), (0, pad), (0, 0), (0, 0)])
    q_rope = jnp.pad(q_rope, [(0, 0), (0, pad), (0, 0), (0, 0)])
    q_pos = ((s - t) + jnp.arange(nb * qb)).reshape(nb, qb)
    k_pos = jnp.arange(s)
    scale = (QK_NOPE + QK_ROPE) ** -0.5
    qlb = jnp.swapaxes(q_lat.reshape(bsz, nb, qb, MLA_HEADS, KV_LORA), 0, 1)
    qrb = jnp.swapaxes(q_rope.reshape(bsz, nb, qb, MLA_HEADS, QK_ROPE), 0, 1)

    def block(args):
        ql, qr, qp = args
        sc = jnp.einsum('bqhc,bkc->bhqk', ql, k_lat, preferred_element_type=jnp.float32)
        sc = sc + jnp.einsum('bqhr,bkr->bhqk', qr, k_rope, preferred_element_type=jnp.float32)
        sc = jnp.where(k_pos[None, :] <= qp[:, None], sc * scale, -jnp.inf)
        p = jax.nn.softmax(sc, axis=-1)
        return jnp.einsum('bhqk,bkc->bqhc', p.astype(k_lat.dtype), k_lat)

    o = lax.map(block, (qlb, qrb, q_pos))
    return jnp.swapaxes(o, 0, 1).reshape(bsz, nb * qb, MLA_HEADS, KV_LORA)[:, :t]

def mla_mixer(x, pos, past_lat, past_krope, w_dqkv, q_norm, kv_norm, w_uq, w_uk, w_uv, w_o):
    bsz, t, _ = x.shape
    cq, ckv, kr = jnp.split(x @ w_dqkv, [Q_LORA, Q_LORA + KV_LORA], axis=-1)
    cq = rms_norm(cq, q_norm)
    ckv = rms_norm(ckv, kv_norm)
    q = jnp.einsum('btc,chd->bthd', cq, w_uq)
    q_nope, q_rope = jnp.split(q, [QK_NOPE], axis=-1)
    cos, sin = rope_tables(pos)
    q_rope = apply_rope(q_rope, cos[:, None, :], sin[:, None, :])
    kr = apply_rope(kr, cos, sin)
    q_lat = jnp.einsum('bthn,chn->bthc', q_nope, w_uk)
    if past_lat is None:
        k_lat, k_rope = ckv, kr
    else:
        k_lat = jnp.concatenate([past_lat.astype(ckv.dtype), ckv], axis=1)
        k_rope = jnp.concatenate([past_krope.astype(kr.dtype), kr], axis=1)
    o_lat = latent_attention(q_lat, q_rope, k_lat, k_rope)
    o = jnp.einsum('bthc,chv->bthv', o_lat, w_uv).reshape(bsz, t, MLA_HEADS * V_HEAD)
    return o @ w_o, ckv, kr

def hier_moe(x, router, router_bias, w_gate, w_up, w_down):
    bsz, t, d = x.shape
    xt = x.reshape(-1, d)
    n = xt.shape[0]
    aff = jax.nn.sigmoid((xt @ router).astype(jnp.float32))
    sel = (aff + router_bias.astype(jnp.float32)).reshape(n, MOE_GROUPS, EXPERTS_PER_GROUP)
    group_score = jnp.sum(lax.top_k(sel, GROUP_TOPK_SCORE)[0], axis=-1)
    grp = jnp.argmax(group_score, axis=-1)
    gidx = jnp.broadcast_to(grp[:, None, None], (n, 1, EXPERTS_PER_GROUP))
    sel_in = jnp.take_along_axis(sel, gidx, axis=1)[:, 0]
    _, loc = lax.top_k(sel_in, EXPERT_TOPK)
    eidx = grp[:, None] * EXPERTS_PER_GROUP + loc
    wts = jnp.take_along_axis(aff, eidx, axis=1)
    wts = wts / jnp.sum(wts, axis=-1, keepdims=True)
    gate = jnp.einsum('nk,nke->ne', wts, jax.nn.one_hot(eidx, N_EXPERTS, dtype=jnp.float32))
    out = jnp.zeros((n, d), jnp.float32)
    for g in range(MOE_GROUPS):
        sl = slice(g * EXPERTS_PER_GROUP, (g + 1) * EXPERTS_PER_GROUP)
        hg = jax.nn.silu(jnp.einsum('nd,edf->nef', xt, w_gate[sl])) * jnp.einsum('nd,edf->nef', xt, w_up[sl])
        hg = hg * gate[:, sl, None].astype(hg.dtype)
        out = out + jnp.einsum('nef,efd->nd', hg, w_down[sl], preferred_element_type=jnp.float32)
    return out.astype(x.dtype).reshape(bsz, t, d)

def setup_inputs(seed: int = 0) -> dict:
    key = jax.random.key(seed)
    ks = jax.random.split(key, 40)
    f32 = jnp.float32

    def nrm(i, shape, scale):
        return jax.random.normal(ks[i], shape, f32) * scale

    n_pages = PAST_LEN // PAGE_SIZE
    n_used = DEC_BATCH * n_pages
    n_pool = n_used + n_used // 4
    perm = jax.random.permutation(ks[0], n_pool)
    page_table = perm[:n_used].reshape(DEC_BATCH, n_pages).astype(jnp.int32)

    dt0 = jnp.exp(jax.random.uniform(ks[1], (N_SSD_LAYERS, SSD_HEADS), f32, minval=np.log(1e-3), maxval=np.log(1e-1)))
    ssd_dt_bias = dt0 + jnp.log(-jnp.expm1(-dt0))
    ssd_a_log = jnp.log(jax.random.uniform(ks[2], (N_SSD_LAYERS, SSD_HEADS), f32, minval=1.0, maxval=16.0))

    return {
        'x_prompt': nrm(3, (BATCH, SEQ, D_MODEL), 1.0),
        'x_sample': nrm(4, (DEC_BATCH, DEC_SEQ, D_MODEL), 1.0),
        'cache_mla_latent': nrm(5, (N_MLA_LAYERS, n_pool, PAGE_SIZE, KV_LORA), 1.0),
        'cache_mla_krope': nrm(6, (N_MLA_LAYERS, n_pool, PAGE_SIZE, QK_ROPE), 1.0),
        'state_ssd': nrm(7, (N_SSD_LAYERS, DEC_BATCH, SSD_HEADS, SSD_HEAD_DIM, SSD_STATE), 0.1),
        'state_conv': nrm(8, (N_SSD_LAYERS, DEC_BATCH, SSD_CONV - 1, CONV_DIM), 1.0),
        'page_table': page_table,
        'ln_mix_g': 1.0 + nrm(9, (DEPTH, D_MODEL), 0.02),
        'ln_mix_b': nrm(10, (DEPTH, D_MODEL), 0.02),
        'ln_ffn_g': 1.0 + nrm(11, (DEPTH, D_MODEL), 0.02),
        'ln_ffn_b': nrm(12, (DEPTH, D_MODEL), 0.02),
        'ssd_w_in': nrm(13, (N_SSD_LAYERS, D_MODEL, D_IN_PROJ), D_MODEL ** -0.5),
        'ssd_conv_w': nrm(14, (N_SSD_LAYERS, SSD_CONV, CONV_DIM), SSD_CONV ** -0.5),
        'ssd_conv_b': nrm(15, (N_SSD_LAYERS, CONV_DIM), 0.02),
        'ssd_dt_bias': ssd_dt_bias,
        'ssd_a_log': ssd_a_log,
        'ssd_d_skip': 1.0 + nrm(16, (N_SSD_LAYERS, SSD_HEADS), 0.02),
        'ssd_norm_w': 1.0 + nrm(17, (N_SSD_LAYERS, D_INNER), 0.02),
        'ssd_w_out': nrm(18, (N_SSD_LAYERS, D_INNER, D_MODEL), D_INNER ** -0.5 * DEEPNORM_BETA),
        'mla_w_dqkv': nrm(19, (N_MLA_LAYERS, D_MODEL, Q_LORA + KV_LORA + QK_ROPE), D_MODEL ** -0.5),
        'mla_q_norm': 1.0 + nrm(20, (N_MLA_LAYERS, Q_LORA), 0.02),
        'mla_kv_norm': 1.0 + nrm(21, (N_MLA_LAYERS, KV_LORA), 0.02),
        'mla_w_uq': nrm(22, (N_MLA_LAYERS, Q_LORA, MLA_HEADS, QK_NOPE + QK_ROPE), Q_LORA ** -0.5),
        'mla_w_uk': nrm(23, (N_MLA_LAYERS, KV_LORA, MLA_HEADS, QK_NOPE), KV_LORA ** -0.5),
        'mla_w_uv': nrm(24, (N_MLA_LAYERS, KV_LORA, MLA_HEADS, V_HEAD), KV_LORA ** -0.5),
        'mla_w_o': nrm(25, (N_MLA_LAYERS, MLA_HEADS * V_HEAD, D_MODEL), (MLA_HEADS * V_HEAD) ** -0.5 * DEEPNORM_BETA),
        'moe_router': nrm(26, (DEPTH, D_MODEL, N_EXPERTS), D_MODEL ** -0.5),
        'moe_router_bias': nrm(27, (DEPTH, N_EXPERTS), 0.01),
        'moe_w_gate': nrm(28, (DEPTH, N_EXPERTS, D_MODEL, EXPERT_FF), D_MODEL ** -0.5),
        'moe_w_up': nrm(29, (DEPTH, N_EXPERTS, D_MODEL, EXPERT_FF), D_MODEL ** -0.5),
        'moe_w_down': nrm(30, (DEPTH, N_EXPERTS, EXPERT_FF, D_MODEL), EXPERT_FF ** -0.5 * DEEPNORM_BETA),
    }

def reference(x_prompt, x_sample, cache_mla_latent, cache_mla_krope, state_ssd, state_conv, page_table,
              ln_mix_g, ln_mix_b, ln_ffn_g, ln_ffn_b,
              ssd_w_in, ssd_conv_w, ssd_conv_b, ssd_dt_bias, ssd_a_log, ssd_d_skip, ssd_norm_w, ssd_w_out,
              mla_w_dqkv, mla_q_norm, mla_kv_norm, mla_w_uq, mla_w_uk, mla_w_uv, mla_w_o,
              moe_router, moe_router_bias, moe_w_gate, moe_w_up, moe_w_down):
    bsz_p, t_p, _ = x_prompt.shape
    bsz_s, t_s, _ = x_sample.shape
    pos_p = jnp.arange(t_p)
    pos_s = PAST_LEN + jnp.arange(t_s)
    conv0 = jnp.zeros((bsz_p, SSD_CONV - 1, CONV_DIM), x_prompt.dtype)
    ssm0 = jnp.zeros((bsz_p, SSD_HEADS, SSD_HEAD_DIM, SSD_STATE), x_prompt.dtype)

    p_lat, p_kr, p_ssm, p_conv = [], [], [], []
    s_lat, s_kr, s_ssm, s_conv = [], [], [], []
    xp, xs = x_prompt, x_sample
    for i in range(DEPTH):
        j = i // 2
        if i % 2 == 0:
            hp, cp, sp = ssd_mixer(xp, conv0, ssm0, ssd_w_in[j], ssd_conv_w[j], ssd_conv_b[j], ssd_dt_bias[j],
                                   ssd_a_log[j], ssd_d_skip[j], ssd_norm_w[j], ssd_w_out[j])
            hs, cs, ss = ssd_mixer(xs, state_conv[j], state_ssd[j], ssd_w_in[j], ssd_conv_w[j], ssd_conv_b[j],
                                   ssd_dt_bias[j], ssd_a_log[j], ssd_d_skip[j], ssd_norm_w[j], ssd_w_out[j])
            p_conv.append(cp)
            p_ssm.append(sp)
            s_conv.append(cs)
            s_ssm.append(ss)
        else:
            past_lat = jnp.take(cache_mla_latent[j], page_table, axis=0).reshape(bsz_s, -1, KV_LORA)
            past_kr = jnp.take(cache_mla_krope[j], page_table, axis=0).reshape(bsz_s, -1, QK_ROPE)
            hp, lp, kp = mla_mixer(xp, pos_p, None, None, mla_w_dqkv[j], mla_q_norm[j], mla_kv_norm[j],
                                   mla_w_uq[j], mla_w_uk[j], mla_w_uv[j], mla_w_o[j])
            hs, ls, kss = mla_mixer(xs, pos_s, past_lat, past_kr, mla_w_dqkv[j], mla_q_norm[j], mla_kv_norm[j],
                                    mla_w_uq[j], mla_w_uk[j], mla_w_uv[j], mla_w_o[j])
            p_lat.append(lp)
            p_kr.append(kp)
            s_lat.append(ls)
            s_kr.append(kss)
        xp = layer_norm(DEEPNORM_ALPHA * xp + hp, ln_mix_g[i], ln_mix_b[i])
        xs = layer_norm(DEEPNORM_ALPHA * xs + hs, ln_mix_g[i], ln_mix_b[i])
        fp = hier_moe(xp, moe_router[i], moe_router_bias[i], moe_w_gate[i], moe_w_up[i], moe_w_down[i])
        fs = hier_moe(xs, moe_router[i], moe_router_bias[i], moe_w_gate[i], moe_w_up[i], moe_w_down[i])
        xp = layer_norm(DEEPNORM_ALPHA * xp + fp, ln_ffn_g[i], ln_ffn_b[i])
        xs = layer_norm(DEEPNORM_ALPHA * xs + fs, ln_ffn_g[i], ln_ffn_b[i])

    return (xp, xs,
            jnp.stack(p_lat), jnp.stack(p_kr), jnp.stack(p_ssm), jnp.stack(p_conv),
            jnp.stack(s_lat), jnp.stack(s_kr), jnp.stack(s_ssm), jnp.stack(s_conv))


_drawn_inputs = setup_inputs


def setup_inputs(seed=0):
    import zlib

    import numpy as np

    out = dict(_drawn_inputs(seed))
    spreads = {}
    factors = {'ssd_norm_w': 3.173, 'mla_q_norm': 5.96, 'mla_kv_norm': 2.866}
    for name, (base, spread) in spreads.items():
        noise = np.random.default_rng([zlib.crc32(name.encode()), seed]).standard_normal(out[name].shape)
        drawn = base * np.exp(spread * noise) if base else spread * noise
        out[name] = __import__('jax').numpy.asarray(drawn.astype(out[name].dtype))
    for name, factor in factors.items():
        out[name] = (out[name] * factor).astype(out[name].dtype)
    return out
```

```python
from contextlib import ExitStack

import numpy as np

import concourse.bass as bass
from concourse import mybir

F32 = mybir.dt.float32
I32 = mybir.dt.int32
ALU = mybir.AluOpType
ACT = mybir.ActivationFunctionType
X_AXIS = mybir.AxisListType.X
ds = bass.ds

P = 128
D = 1024
KD = D // P
SEQ, DEC_B, DEC_T = 256, 8, 8
NT = 3
ROWS = [P, P, DEC_B * DEC_T]
OFF = [0, P, 2 * P]
TOK = SEQ + DEC_B * DEC_T
SAMPLE = slice(SEQ, TOK)
PAST, PAGE = 1024, 128
PAGES = PAST // PAGE

INNER = 2048
HEADS, HP, STATE, GROUPS = 32, 64, 128, 4
HG = HEADS // GROUPS
ZB = INNER // P
XBCB = 24
CONVO = 3 + 3 * DEC_B
RMS_EPS, LN_EPS = 1e-6, 1e-5

AH, QL, KL, NOPE, ROPE, VH = 8, 384, 256, 128, 64, 128
DQKV = QL + KL + ROPE
ATT_SCALE = float(NOPE + ROPE) ** -0.5
ALPHA = 4.0 ** 0.25

EXPERTS, MGROUPS, EG, FF = 32, 4, 8, 256
SLOTS = 64
NSLOT = EXPERTS * SLOTS
WEXP = 2 * KD * FF + 2 * D
MAX_WINDOWS = TOK // SLOTS
PHASE_SEMS = 64
NEG = -1e30

_WIDTHS = [("ident", P), ("tri", P), ("strict", P), ("ones", P), ("tri_s", 64), ("same_s", 64),
           ("bmask", DEC_B), ("desc4", MGROUPS), ("desc32", EXPERTS), ("ebase", EXPERTS),
           ("valid", NT), ("causal", 2 * P), ("smask", DEC_B * 64), ("eps", 2), ("cos", NT * 32), ("sin", NT * 32)]
CONST = {}
_at = 0
for _name, _w in _WIDTHS:
    CONST[_name] = slice(_at, _at + _w)
    _at += _w
CONST_W = _at


def constants():
    c = np.zeros((P, CONST_W), np.float32)
    i = np.arange(P)
    s = np.arange(64)
    c[:, CONST["ident"]] = np.eye(P)
    c[:, CONST["tri"]] = i[:, None] <= i[None, :]
    c[:, CONST["strict"]] = i[:, None] < i[None, :]
    c[:, CONST["ones"]] = 1.0
    same = s[:, None] // DEC_T == s[None, :] // DEC_T
    c[:64, CONST["tri_s"]] = same & (s[:, None] <= s[None, :])
    c[:64, CONST["same_s"]] = same
    c[:64, CONST["bmask"]] = s[:, None] // DEC_T == np.arange(DEC_B)[None, :]
    c[:, CONST["desc4"]] = np.arange(MGROUPS, 0, -1)
    c[:, CONST["desc32"]] = np.arange(EXPERTS, 0, -1)
    c[:, CONST["ebase"]] = np.arange(EXPERTS) * SLOTS
    for t in range(NT):
        c[:ROWS[t], CONST["valid"].start + t] = 1.0
    c[:, CONST["causal"].start + P:CONST["causal"].stop] = np.where(i[None, :] <= i[:, None], 0.0, NEG)
    key_b, key_j = s // DEC_T, s % DEC_T
    t_of = s // AH
    ok = (key_b[None, None, :] == np.arange(DEC_B)[None, :, None]) & (key_j[None, None, :] <= t_of[:, None, None])
    c[:64, CONST["smask"]] = np.where(ok, 0.0, NEG).reshape(64, -1)
    c[:, CONST["eps"]] = [LN_EPS, RMS_EPS]
    half = ROPE // 2
    inv = 10000.0 ** (-np.arange(half, dtype=np.float32) / half)
    pos = np.zeros((NT, P), np.float32)
    pos[0], pos[1], pos[2, :64] = i, P + i, PAST + s % DEC_T
    ang = (pos[:, :, None] * inv.astype(np.float32)).transpose(1, 0, 2)
    c[:, CONST["cos"]] = np.cos(ang).reshape(P, -1)
    c[:, CONST["sin"]] = np.sin(ang).reshape(P, -1)
    return c


class Tally:

    def __init__(self, sem):
        self.sem, self.base, self.n = sem, 0, 0

    def mark(self, ins):
        ins.then_inc(self.sem, 1)
        self.n += 1

    def settle(self, eng):
        eng.wait_ge(self.sem, self.base + self.n)

    def loop(self, base):
        self.base, self.n = base, 0


def program(nc, a, o):
    ctx = ExitStack()
    with ctx:
        def sem(name):
            return ctx.enter_context(nc.semaphore(name))

        def sems(name, n):
            return [sem(f"{name}{i}") for i in range(n)]

        free = sorted(nc.free_semaphores)[-2 * PHASE_SEMS:]
        POOLS, turn = (free[:PHASE_SEMS], free[PHASE_SEMS:]), [0]

        def phase_semaphores(stack, tag=""):
            made = []
            stack.callback(nc.clear_and_free_semaphores, made)
            turn[0] ^= 1
            numbers = iter(POOLS[turn[0]])

            def make(name):
                names[name + tag] = names.get(name + tag, 0) + 1
                made.append(nc.alloc_semaphore(f"{name}{tag}_{names[name + tag]}", num=next(numbers)))
                return made[-1]

            return make

        names = {}

        def buf(stack, name, shape, dt=F32):
            names[name] = names.get(name, 0) + 1
            unique = name if names[name] == 1 else f"{name}_{names[name]}"
            return stack.enter_context(nc.sbuf_tensor(unique, shape, dt))

        ring = buf(ctx, "ring", [P, 4, WEXP])
        X = buf(ctx, "X", [P, NT, D])
        XT = buf(ctx, "XT", [P, KD, TOK])
        C = buf(ctx, "C", [P, CONST_W])
        lnp = buf(ctx, "lnp", [P, 2, D])
        ps = ctx.enter_context(nc.psum_tensor("ps", [P, 8, 512], F32))
        xs_dram = nc.dram_tensor("xs_dram", (NSLOT, D), F32).ap()
        ys_dram = nc.dram_tensor("ys_dram", (NSLOT, D), F32).ap()

        def const(name, rows=P):
            return C[0:rows, CONST[name]]

        def const3(name):
            return C[:, CONST[name]].rearrange("p (t i) -> p t i", t=NT)

        ident = const("ident")
        eps = const("eps")
        const_in, x_in, ln_in, cols_in, rows_in, conv_in, wdt_in = map(
            sem, ["const_in", "x_in", "ln_in", "cols_in", "rows_in", "conv_in", "wdt_in"])
        wout_in = sems("wout_in", 4)
        zero_made, zero_out = sem("zero_made"), sem("zero_out")
        state_in = sems("state_in", 2)
        key_in, wo_in = sems("key_in", 2), sem("wo_in")

        ssd = ExitStack()
        zT = buf(ssd, "zT", [P, ZB, TOK])
        xbcT = buf(ssd, "xbcT", [P, XBCB, TOK])
        cols = buf(ssd, "cols", [P, 152])
        dt = buf(ssd, "dt", [P, NT, HEADS])
        dtA = buf(ssd, "dtA", [P, NT, HEADS])
        convw, convb = cols[:, 0:96], cols[:, 96:120]
        normw, dskip = cols[:, 120:136], cols[:, 136:152]

        def in_projection():
            with ExitStack() as st:
                xpad = buf(st, "xpad", [P, 2, 3 + SEQ])
                spad = buf(st, "spad", [P, 2, DEC_B, 3 + DEC_T])
                conv = buf(st, "conv", [P, 2, TOK])
                cst = buf(st, "cst", [P, XBCB, DEC_B, 3])
                cvo = buf(st, "cvo", [P, XBCB, CONVO])
                wdt = buf(st, "wdt", [P, KD, HEADS])
                rows = buf(st, "rows", [P, 2, HEADS])
                nega = buf(st, "nega", [P, HEADS])
                soft = buf(st, "soft", [P, 3, NT * HEADS])
                zero = ring[:, 3, 0:D]

                s = phase_semaphores(st)

                chunk_in = [s("chunk_in0"), s("chunk_in1")]
                proj_done, dt_done, conv_done, kept, cvo_out = map(
                    s, ["proj_done", "dt_done", "conv_done", "kept", "cvo_out"])
                freed = [s(f"freed{q}") for q in range(4)]
                silu_done = [s("silu_done0"), s("silu_done1")]
                dve, soft_in, soft_out = map(s, ["dve_a", "soft_in", "soft_out"])
                block = st.enter_context(nc.Block())

                @block.sync
                def _(sp):
                    sp.dma_start(XT[:, :, :], a["xT"]).then_inc(x_in, 16)
                    for u in range(2):
                        sp.dma_start(ring[:, u, 0:KD * 512], a["w_in"][u]).then_inc(chunk_in[u], 16)
                    sp.dma_start(C[:, :], a["const"]).then_inc(const_in, 16)
                    sp.dma_start(cols[:, :], a["cols"]).then_inc(cols_in, 16)
                    sp.dma_start(cst[:, :, :, :], a["conv"]).then_inc(conv_in, 16)
                    sp.dma_start(wdt[:, :, :], a["w_dt"]).then_inc(wdt_in, 16)
                    sp.dma_start(rows[:, :, :], a["rows"]).then_inc(rows_in, 16)
                    with sp.Fori(0, 4) as it:
                        for u in range(2):
                            src = a["w_in"][ds(sp.snap(2 * it + 2 + u), 1)].rearrange("c p n -> (c p) n")
                            for q in range(1):
                                sp.wait_ge(proj_done, 8 * it + 4 * u + 4)
                            sp.dma_start(ring[:, u, 0:KD * 512], src).then_inc(chunk_in[u], 16)
                    for i in (2, 3):
                        if i == 3:
                            sp.wait_ge(zero_out, 16 * (NSLOT // P))
                        sp.dma_start(ring[:, i, 0:4 * D], a["w_out"][i]).then_inc(wout_in[i], 16)
                    sp.dma_start(X[:, :, :], a["x"]).then_inc(x_in, 16)
                    sp.dma_start(lnp[:, :, :], a["ln"][0]).then_inc(ln_in, 16)
                    for i in range(2):
                        sp.wait_ge(proj_done, 40)
                        sp.dma_start(ring[:, i, 0:4 * D], a["w_out"][i]).then_inc(wout_in[i], 16)
                    sp.wait_ge(kept, 2 * XBCB)
                    sp.dma_start(o["conv"], cvo[:, :, :]).then_inc(cvo_out, 16)
                    sp.wait_ge(cvo_out, 16)

                @block.tensor
                def _(pe):
                    pe.wait_ge(x_in, 16)
                    with pe.Fori(0, 5) as it:
                        for u in range(2):
                            pe.wait_ge(chunk_in[u], 16 * (it + 1))
                            for q in range(4):
                                pe.wait_ge(freed[q], 2 * it + u)
                                for k in range(KD):
                                    mm = pe.matmul(ps[:, q, 0:TOK],
                                                   ring[:, u, k * 512 + q * P:k * 512 + (q + 1) * P],
                                                   XT[:, k, :], start=(k == 0), stop=(k == KD - 1))
                                mm.then_inc(proj_done, 1)
                    pe.wait_ge(wdt_in, 16)
                    for t in range(NT):
                        r = ROWS[t]
                        for k in range(KD):
                            mm = pe.matmul(ps[0:r, 4, t * HEADS:(t + 1) * HEADS], XT[:, k, OFF[t]:OFF[t] + r],
                                           wdt[:, k, :], start=(k == 0), stop=(k == KD - 1))
                    mm.then_inc(dt_done, 1)

                @block.scalar
                def _(act):
                    with act.Fori(0, 2) as it:
                        for u in range(2):
                            for q in range(4):
                                blk = 8 * it + 4 * u + q
                                act.wait_ge(proj_done, blk + 1)
                                act.activation(zT[:, ds(blk, 1), :].rearrange("p a t -> p (a t)"),
                                               ps[:, q, 0:TOK], ACT.Silu).then_inc(freed[q], 1)
                    with act.Fori(0, 3) as it:
                        for u in range(2):
                            for q in range(4):
                                blk = 8 * it + 4 * u + q
                                act.wait_ge(conv_done, blk + 1)
                                act.activation(xbcT[:, ds(blk, 1), :].rearrange("p a t -> p (a t)"),
                                               conv[:, q % 2, :], ACT.Silu).then_inc(silu_done[q % 2], 1)
                    act.wait_ge(soft_in, 1)
                    act.activation(soft[:, 1, :], soft[:, 1, :], ACT.Exp).then_inc(soft_out, 1)
                    act.wait_ge(rows_in, 16)
                    act.activation(nega[:, :], rows[:, 1, :], ACT.Exp)
                    act.wait_ge(soft_out, 1)
                    act.activation(soft[:, 1, :], soft[:, 1, :], ACT.Ln, bias=1.0).then_inc(soft_out, 1)

                @block.gpsimd
                def _(pool):
                    pool.memset(zero, 0.0).then_inc(zero_made, 1)
                    pool.wait_ge(zero_made, 1)
                    for i in range(NSLOT // P):
                        pool.dma_start(xs_dram[i * P:(i + 1) * P, :], zero).then_inc(zero_out, 16)
                    with pool.Fori(0, 12) as it:
                        for v in range(2):
                            blk = 2 * it + v
                            pool.wait_ge(conv_done, blk + 1)
                            pool.tensor_copy(cvo[:, ds(blk, 1), 0:3].rearrange("p a t -> p (a t)"),
                                             xpad[:, v, SEQ:SEQ + 3]).then_inc(kept, 1)
                            pool.tensor_copy(
                                cvo[:, ds(blk, 1), 3:CONVO].rearrange("p a (b t) -> p (a b) t", b=DEC_B),
                                spad[:, v, :, DEC_T:DEC_T + 3]).then_inc(kept, 1)

                @block.vector
                def _(v):
                    step = Tally(dve)
                    step.mark(v.memset(xpad[:, :, 0:3], 0.0))
                    step.mark(v.memset(soft[:, 0, :], 0.0))
                    v.wait_ge(conv_in, 16)
                    v.wait_ge(cols_in, 16)
                    start = step.n
                    with v.Fori(0, 3) as it:
                        for u in range(2):
                            for q in range(4):
                                b = q % 2
                                m = 4 * u + q
                                blk = 8 * it + m
                                step.loop(start + blk * 4)
                                xo, so = conv[:, b, 0:SEQ], conv[:, b, SEQ:TOK].rearrange("p (b t) -> p b t", b=DEC_B)
                                v.wait_ge(kept, 2 * (blk - 1) if m > 1 else 2 * (blk - m))
                                v.wait_ge(proj_done, 16 + blk + 1)
                                v.tensor_copy(xpad[:, b, 3:3 + SEQ], ps[:, q, 0:SEQ])
                                v.tensor_copy(spad[:, b, :, 0:3], cst[:, ds(blk, 1), :, :].rearrange("p a b t -> p (a b) t"))
                                cp = v.tensor_copy(spad[:, b, :, 3:3 + DEC_T],
                                                   ps[:, q, SEQ:TOK].rearrange("p (b t) -> p b t", b=DEC_B))
                                cp.then_inc(freed[q], 1)
                                v.wait_ge(freed[q], 4 + 2 * it + u + 1)
                                v.wait_ge(silu_done[b], 4 * it + 2 * u + q // 2)
                                for k in range(4):
                                    w = convw[:, ds(4 * blk + k, 1)]
                                    xi, si = xpad[:, b, k:k + SEQ], spad[:, b, :, k:k + DEC_T]
                                    if k == 0:
                                        bias = convb[:, ds(blk, 1)]
                                        v.tensor_scalar(xo, xi, w, bias, ALU.mult, ALU.add)
                                        ins = v.tensor_scalar(so, si, w, bias, ALU.mult, ALU.add)
                                    else:
                                        v.scalar_tensor_tensor(out=xo, in0=xi, scalar=w, in1=xo, op0=ALU.mult, op1=ALU.add)
                                        ins = v.scalar_tensor_tensor(out=so, in0=si, scalar=w, in1=so,
                                                                     op0=ALU.mult, op1=ALU.add)
                                    if k < 3:
                                        step.mark(ins)
                                        step.settle(v)
                                    else:
                                        ins.then_inc(conv_done, 1)
                                step.mark(v.engine_nop() if False else v.memset(soft[:, 2, 0:1], 0.0))
                    step.loop(start + XBCB * 4)
                    v.wait_ge(dt_done, 1)
                    v.wait_ge(rows_in, 16)
                    v.tensor_copy(soft[:, 0, 0:64], ps[:, 4, 0:64])
                    step.mark(v.tensor_copy(soft[0:64, 0, 64:96], ps[0:64, 4, 64:96]))
                    step.settle(v)
                    raw = soft[:, 0, :].rearrange("p (t h) -> p t h", t=NT)
                    bias = rows[:, 0, :].unsqueeze(1).to_broadcast([P, NT, HEADS])
                    step.mark(v.tensor_tensor(raw, raw, bias, ALU.add))
                    step.settle(v)
                    v.scalar_tensor_tensor(out=soft[:, 1, :], in0=soft[:, 0, :], scalar=-1.0, in1=soft[:, 0, :],
                                           op0=ALU.mult, op1=ALU.min).then_inc(soft_in, 1)
                    v.wait_ge(soft_out, 2)
                    dtf = dt[:, :, :].rearrange("p t h -> p (t h)")
                    step.mark(v.scalar_tensor_tensor(out=dtf, in0=soft[:, 0, :], scalar=0.0, in1=soft[:, 1, :],
                                                     op0=ALU.max, op1=ALU.add))
                    step.settle(v)
                    v.scalar_tensor_tensor(out=dtA[:, :, :], in0=dt[:, :, :], scalar=-1.0,
                                           in1=nega[:, :].unsqueeze(1).to_broadcast([P, NT, HEADS]),
                                           op0=ALU.mult, op1=ALU.mult)

        h1 = buf(ssd, "h1", [P, INNER])
        Bt = buf(ssd, "Bt", [P, GROUPS * STATE])
        decS = buf(ssd, "decS", [P, DEC_B, HEADS])
        xdt = ring[:, 0, 4 * D:6 * D]
        xdtw = ring[:, 1, 4 * D:6 * D]
        h0 = [ring[:, 2, 4 * D:6 * D], ring[:, 3, 4 * D:6 * D]]

        def scan_chunk(c):
            r = ROWS[c]
            carried = c == 1
            mask = const("tri_s", 64) if c == 2 else const("tri")
            same = const("same_s", 64) if c == 2 else const("ones")
            TR, BC, CB, Y, M = (0, 1), (2, 3), 4, (5, 6), 7
            UNITS = 2 * GROUPS

            def by_channel(blk):
                return xbcT[:, blk, OFF[c]:OFF[c] + r]

            with ExitStack() as st:
                s = phase_semaphores(st, f"_c{c}")

                cums = buf(st, "cums", [P, HEADS])
                wS = buf(st, "wS", [P, HEADS])
                dec = buf(st, "dec", [P, HEADS])
                cbm = buf(st, "cbm", [P, 2, P])
                ec = buf(st, "ec", [P, 2, 4, P])
                seg = buf(st, "seg", [P, 2, 4, P])
                tmp = buf(st, "tmp", [P, 2, 2, P])
                (turned, xdt_done, bt_done, cum_done, cums_done, w_in, w_done, xw_done, bc_done, cb_done,
                 cbm_done, ec_done, seg_in, seg_done, mt_done, ct_done, y_done, tmp_done, gated,
                 h_mm, h1_done, h1_scaled, h2_out, dec_done) = map(s, [
                     "turned", "xdt_done", "bt_done", "cum_done", "cums_done", "w_in", "w_done", "xw_done",
                     "bc_done", "cb_done", "cbm_done", "ec_done", "seg_in", "seg_done", "mt_done", "ct_done",
                     "y_done", "tmp_done", "gated", "h_mm", "h1_done", "h1_scaled", "h2_out", "dec_done"])
                block = st.enter_context(nc.Block())

                if c != 0:
                    @block.sync
                    def _(sp):
                        if c == 1:
                            sp.wait_ge(h1_done, GROUPS)
                            sp.dma_start(o["ssdp"], h1[:, :]).then_inc(h2_out, 16)
                            sp.wait_ge(h2_out, 16)
                        else:
                            for b in range(2):
                                sp.dma_start(h0[b], a["state"][b]).then_inc(state_in[b], 16)

                @block.tensor
                def _(pe):
                    for f in range(5):
                        if f >= 2:
                            pe.wait_ge(xdt_done, f - 1)
                        for j in range(4):
                            tr = pe.transpose(ps[0:r, TR[f % 2], j * P:(j + 1) * P], by_channel(4 * f + j), ident)
                        tr.then_inc(turned, 1)
                    pe.matmul(ps[0:r, M, 0:HEADS], mask[0:r, 0:r], dtA[0:r, c, :], start=True, stop=True)
                    mm = pe.matmul(ps[0:P if c < 2 else r, M, HEADS:2 * HEADS], same[0:r, :], dtA[0:r, c, :],
                                   start=True, stop=True)
                    if c == 2:
                        for b in range(DEC_B):
                            at = CONST["bmask"].start + b
                            mm = pe.matmul(ps[:, M, P + b * HEADS:P + (b + 1) * HEADS],
                                           C[0:64, at:at + 1].to_broadcast([64, P]), dtA[0:64, 2, :],
                                           start=True, stop=True)
                    mm.then_inc(cum_done, 1)

                    def spread(u):
                        g, half = divmod(u, 2)
                        if u >= 2:
                            pe.wait_ge(seg_in, u - 1)
                            if c:
                                pe.wait_ge(ec_done, u - 1)
                        for j in range(4):
                            h = HG * g + 4 * half + j
                            mm = pe.matmul(ps[:, BC[u % 2], j * P:j * P + r],
                                           dtA[0:r, c, h:h + 1].to_broadcast([r, P]), mask[0:r, 0:r],
                                           start=True, stop=True)
                        mm.then_inc(bc_done, 1)
                        if half == 0:
                            if g:
                                pe.wait_ge(cbm_done, g)
                            pe.matmul(ps[0:r, CB, 0:r], by_channel(ZB + g), by_channel(ZB + GROUPS + g),
                                      start=True, stop=True).then_inc(cb_done, 1)

                    def output(u):
                        g, half = divmod(u, 2)
                        pe.wait_ge(mt_done, u + 1)
                        if carried:
                            pe.wait_ge(ct_done, u + 1)
                        if u >= 2:
                            pe.wait_ge(tmp_done, u - 1)
                        for j in range(4):
                            h = HG * g + 4 * half + j
                            at = HP * (j % 2)
                            out = ps[at:at + HP, Y[u % 2], (j // 2) * P:(j // 2) * P + r]
                            mm = pe.matmul(out, xdt[0:r, h * HP:(h + 1) * HP], seg[0:r, u % 2, j, 0:r],
                                           start=True, stop=not carried)
                            if carried:
                                mm = pe.matmul(out, h1[:, h * HP:(h + 1) * HP], ec[:, u % 2, j, 0:r],
                                               start=False, stop=True)
                        mm.then_inc(y_done, 1)

                    pe.wait_ge(xdt_done, 4)
                    for u in range(UNITS):
                        spread(u)
                        if u:
                            output(u - 1)
                    output(UNITS - 1)
                    if c < 2:
                        pe.wait_ge(xw_done, 1)
                        pe.wait_ge(bt_done, 1)
                        pe.wait_ge(seg_in, UNITS)
                        if c:
                            pe.wait_ge(ec_done, UNITS)
                        for g in range(GROUPS):
                            pe.matmul(ps[:, g, :], Bt[:, g * STATE:(g + 1) * STATE], xdtw[:, g * 512:(g + 1) * 512],
                                      start=True, stop=True).then_inc(h_mm, 1)

                @block.vector
                def _(v):
                    for f in range(4):
                        v.wait_ge(turned, f + 1)
                        v.tensor_tensor(
                            xdt[0:r, f * 512:(f + 1) * 512].rearrange("p (h e) -> p h e", e=HP),
                            ps[0:r, TR[f % 2], :].rearrange("p (h e) -> p h e", e=HP),
                            dt[0:r, c, HG * f:HG * (f + 1)].unsqueeze(2).to_broadcast([r, HG, HP]),
                            ALU.mult).then_inc(xdt_done, 1)
                    v.wait_ge(cum_done, 1)
                    v.tensor_copy(cums[0:r, :], ps[0:r, M, 0:HEADS]).then_inc(cums_done, 1)
                    v.wait_ge(cums_done, 1)
                    v.tensor_tensor(wS[0:r, :], ps[0:r, M, HEADS:2 * HEADS], cums[0:r, :],
                                    ALU.subtract).then_inc(w_in, 1)

                    def exponents(u):
                        g, half = divmod(u, 2)
                        v.wait_ge(bc_done, u + 1)
                        if u >= 2:
                            v.wait_ge(y_done, u - 1)
                        for j in range(4):
                            h = HG * g + 4 * half + j
                            ins = v.tensor_scalar(seg[0:r, u % 2, j, 0:r], ps[0:r, BC[u % 2], j * P:j * P + r],
                                                  cums[0:r, h:h + 1], 0.0, ALU.subtract, ALU.min)
                        ins.then_inc(seg_in, 1)
                        if half == 0:
                            v.wait_ge(cb_done, g + 1)
                            v.tensor_tensor(cbm[0:r, g % 2, 0:r], ps[0:r, CB, 0:r], mask[0:r, 0:r],
                                            ALU.mult).then_inc(cbm_done, 1)

                    def weights(u):
                        g = u // 2
                        v.wait_ge(seg_done, u + 1)
                        v.wait_ge(cbm_done, g + 1)
                        w = seg[0:r, u % 2, :, 0:r]
                        v.tensor_tensor(w, w, cbm[0:r, g % 2, 0:r].unsqueeze(1).to_broadcast([r, 4, r]),
                                        ALU.mult).then_inc(mt_done, 1)

                    def skip(u):
                        v.wait_ge(y_done, u + 1)
                        if c < 2 and u >= 2:
                            v.wait_ge(gated, u - 1)
                        for i in range(2):
                            blk = 2 * u + i
                            out = tmp[:, u % 2, i, 0:r] if c < 2 else by_channel(blk)
                            ins = v.scalar_tensor_tensor(out=out, in0=by_channel(blk), scalar=dskip[:, blk:blk + 1],
                                                         in1=ps[:, Y[u % 2], i * P:i * P + r], op0=ALU.mult, op1=ALU.add)
                        ins.then_inc(tmp_done, 1)

                    for u in range(UNITS + 2):
                        if u < UNITS:
                            exponents(u)
                        if 1 <= u <= UNITS:
                            weights(u - 1)
                        if u >= 2:
                            skip(u - 2)
                    if c == 1:
                        v.wait_ge(dec_done, 1)
                        hv = h1[:, :].rearrange("p (h e) -> p h e", e=HP)
                        v.tensor_tensor(hv, hv, dec[:, :].unsqueeze(2).to_broadcast([P, HEADS, HP]),
                                        ALU.mult).then_inc(h1_scaled, 1)
                        v.wait_ge(h1_scaled, 1)
                        for g in range(GROUPS):
                            v.wait_ge(h_mm, g + 1)
                            hg = h1[:, g * 512:(g + 1) * 512]
                            v.tensor_tensor(hg, hg, ps[:, g, :], ALU.add).then_inc(h1_done, 1)

                @block.scalar
                def _(act):
                    act.wait_ge(turned, 5)
                    act.activation(Bt[0:r, :], ps[0:r, TR[0], :], ACT.Copy).then_inc(bt_done, 1)
                    act.wait_ge(w_in, 1)
                    act.activation(wS[0:r, :], wS[0:r, :], ACT.Exp).then_inc(w_done, 1)
                    if c == 1:
                        act.activation(dec[:, :], ps[:, M, HEADS:2 * HEADS], ACT.Exp).then_inc(dec_done, 1)
                    if c == 2:
                        act.activation(decS[:, :, :].rearrange("p b h -> p (b h)"), ps[:, M, P:P + DEC_B * HEADS],
                                       ACT.Exp).then_inc(dec_done, 1)
                    for u in range(UNITS):
                        if c:
                            act.wait_ge(seg_in, u + 1)
                            if u >= 2:
                                act.wait_ge(y_done if c == 1 else ct_done, u - 1)
                            act.activation(ec[:, u % 2, :, 0:r],
                                           ps[:, BC[u % 2], :].rearrange("p (j l) -> p j l", j=4)[:, :, 0:r],
                                           ACT.Exp).then_inc(ec_done, 1)
                        act.wait_ge(seg_in, u + 1)
                        w = seg[0:r, u % 2, :, 0:r]
                        act.activation(w, w, ACT.Exp).then_inc(seg_done, 1)
                    if c == 0:
                        for g in range(GROUPS):
                            act.wait_ge(h_mm, g + 1)
                            act.activation(h1[:, g * 512:(g + 1) * 512], ps[:, g, :], ACT.Copy).then_inc(h1_done, 1)

                @block.gpsimd
                def _(pool):
                    def weigh_inputs():
                        pool.wait_ge(w_done, 1)
                        pool.wait_ge(xdt_done, 4)
                        pool.tensor_tensor(xdtw[0:r, :].rearrange("p (h e) -> p h e", e=HP),
                                           xdt[0:r, :].rearrange("p (h e) -> p h e", e=HP),
                                           wS[0:r, :].unsqueeze(2).to_broadcast([r, HEADS, HP]),
                                           ALU.mult).then_inc(xw_done, 1)

                    def gate(u):
                        z = zT[:, 2 * u:2 * u + 2, OFF[c]:OFF[c] + r]
                        pool.wait_ge(tmp_done, u + 1)
                        pool.tensor_tensor(z, z, tmp[:, u % 2, :, 0:r], ALU.mult).then_inc(gated, 1)

                    for u in range(UNITS + 2):
                        if c and u < UNITS:
                            cu = by_channel(ZB + GROUPS + u // 2).unsqueeze(1).to_broadcast([P, 4, r])
                            src = ec[:, u % 2, :, 0:r]
                            dst = src if c == 1 else h1[:, u * 256:(u + 1) * 256].rearrange("p (j l) -> p j l", j=4)
                            pool.wait_ge(ec_done, u + 1)
                            pool.tensor_tensor(dst, src, cu, ALU.mult).then_inc(ct_done, 1)
                        if c < 2 and u >= 2:
                            gate(u - 2)
                        if u == 3:
                            weigh_inputs()

        def sample_states():
            with ExitStack() as st:
                s = phase_semaphores(st)

                Bm = buf(st, "Bm", [64, 2, GROUPS * STATE])
                bm_done, ys_mm, ys_done, up_mm, scaled, updated = map(
                    s, ["bm_done", "ys_mm", "ys_done", "up_mm", "scaled", "updated"])
                state_out = [s("state_out0"), s("state_out1")]
                block = st.enter_context(nc.Block())
                cts = h1[:, :].rearrange("p (h l) -> p h l", l=64)
                YB, UP = 4, (0, 1, 2, 3)

                @block.sync
                def _(sp):
                    with sp.Fori(0, 3) as it:
                        for b in range(2):
                            nxt = a["state"][ds(sp.snap(2 * it + 2 + b), 1)].rearrange("a n h -> (a n) h")
                            out = o["ssds"][ds(sp.snap(2 * it + b), 1)].rearrange("a n h -> (a n) h")
                            sp.wait_ge(updated, GROUPS * (2 * it + b + 1))
                            sp.dma_start(out, h0[b]).then_inc(state_out[b], 16)
                            sp.wait_ge(state_out[b], 16 * (it + 1))
                            sp.dma_start(h0[b], nxt).then_inc(state_in[b], 16)
                    for b in range(2):
                        sp.wait_ge(updated, GROUPS * (7 + b))
                        sp.dma_start(o["ssds"][6 + b], h0[b]).then_inc(state_out[b], 16)
                    for b in range(2):
                        sp.wait_ge(state_out[b], 64)

                @block.tensor
                def _(pe):
                    with pe.Fori(0, 4) as it:
                        for b in range(2):
                            n = 2 * it + b
                            pe.wait_ge(state_in[b], 16 * (it + 1))
                            pe.wait_ge(ys_done, 2 * n)
                            for j in range(ZB):
                                mm = pe.matmul(ps[:, YB, j * 16:(j + 1) * 16], h0[b][:, j * P:(j + 1) * P],
                                               cts[:, 2 * j:2 * j + 2, ds(DEC_T * n, DEC_T)], start=True, stop=True)
                            mm.then_inc(ys_mm, 1)
                            pe.wait_ge(bm_done, n + 1)
                            for g in range(GROUPS):
                                pe.wait_ge(updated, GROUPS * n)
                                pe.matmul(ps[:, UP[g], :], Bm[:, b, g * STATE:(g + 1) * STATE],
                                          xdtw[0:64, g * 512:(g + 1) * 512], start=True, stop=True).then_inc(up_mm, 1)

                @block.gpsimd
                def _(pool):
                    with pool.Fori(0, 4) as it:
                        for b in range(2):
                            n = 2 * it + b
                            pool.wait_ge(up_mm, GROUPS * 2 * it)
                            own = C[0:64, ds(CONST["bmask"].start + n, 1)].to_broadcast([64, GROUPS * STATE])
                            pool.tensor_tensor(Bm[:, b, :], Bt[0:64, :], own, ALU.mult).then_inc(bm_done, 1)

                @block.vector
                def _(v):
                    with v.Fori(0, 4) as it:
                        for b in range(2):
                            n = 2 * it + b
                            v.wait_ge(ys_mm, n + 1)
                            y = ps[:, YB, 0:ZB * 16].rearrange("p (j e) -> p j e", e=16)
                            for half in range(2):
                                at = HP * half
                                ysm = xbcT[at:at + HP, 0:ZB, ds(SEQ + DEC_T * n, DEC_T)]
                                v.tensor_tensor(ysm, ysm, y[at:at + HP, :, DEC_T * half:DEC_T * (half + 1)],
                                                ALU.add).then_inc(ys_done, 1)
                            hv = h0[b].rearrange("p (h e) -> p h e", e=HP)
                            dv = decS[:, ds(n, 1), :].rearrange("p a h -> p (a h)").unsqueeze(2)
                            v.tensor_tensor(hv, hv, dv.to_broadcast([P, HEADS, HP]), ALU.mult).then_inc(scaled, 1)
                            v.wait_ge(scaled, n + 1)
                            for g in range(GROUPS):
                                v.wait_ge(up_mm, GROUPS * n + g + 1)
                                hg = h0[b][:, g * 512:(g + 1) * 512]
                                v.tensor_tensor(hg, hg, ps[:, UP[g], :], ALU.add).then_inc(updated, 1)

        def out_projection():
            with ExitStack() as st:
                s = phase_semaphores(st)

                sq = buf(st, "sq", [P, 2, 4, TOK])
                rstd = buf(st, "rstd", [P, 2, TOK])
                gate_done, sq_done, ms_done, std_done, rstd_done, scaled, wout_done = map(
                    s, ["gate_done", "sq_done", "ms_done", "std_done", "rstd_done", "scaled", "wout_done"])
                block = st.enter_context(nc.Block())
                ms = [6, 7]

                @block.vector
                def _(v):
                    z = zT[:, :, SAMPLE]
                    v.tensor_tensor(z, z, xbcT[:, 0:ZB, SAMPLE], ALU.mult).then_inc(gate_done, 1)
                    for g in range(GROUPS):
                        v.wait_ge(std_done, g + 1)
                        rs = rstd[:, g % 2, :]
                        v.reciprocal(rs, rs).then_inc(rstd_done, 1)
                        v.wait_ge(rstd_done, g + 1)
                        for i in range(4):
                            blk = 4 * g + i
                            v.scalar_tensor_tensor(out=zT[:, blk, :], in0=zT[:, blk, :], scalar=normw[:, blk:blk + 1],
                                                   in1=rs, op0=ALU.mult, op1=ALU.mult).then_inc(scaled, 1)

                @block.scalar
                def _(act):
                    act.wait_ge(gate_done, 1)
                    for g in range(GROUPS):
                        if g >= 2:
                            act.wait_ge(ms_done, g - 1)
                        act.activation(sq[:, g % 2, :, :], zT[:, 4 * g:4 * g + 4, :], ACT.Square).then_inc(sq_done, 1)
                    for g in range(GROUPS):
                        act.wait_ge(ms_done, g + 1)
                        if g >= 2:
                            act.wait_ge(scaled, 4 * (g - 1))
                        act.activation(rstd[:, g % 2, :], ps[:, ms[g % 2], 0:TOK], ACT.Sqrt,
                                       bias=eps[:, 1:2], scale=1.0 / (4 * P)).then_inc(std_done, 1)

                @block.tensor
                def _(pe):
                    for g in range(GROUPS):
                        pe.wait_ge(sq_done, g + 1)
                        if g >= 2:
                            pe.wait_ge(std_done, g - 1)
                        for i in range(4):
                            mm = pe.matmul(ps[:, ms[g % 2], 0:TOK], const("ones"), sq[:, g % 2, i, :],
                                           start=(i == 0), stop=(i == 3))
                        mm.then_inc(ms_done, 1)
                    for blk in range(ZB):
                        pe.wait_ge(wout_in[blk // 4], 16)
                        pe.wait_ge(scaled, blk + 1)
                        for t in range(NT):
                            for n in range(2):
                                at = (blk % 4) * D + n * 512
                                mm = pe.matmul(ps[0:ROWS[t], 2 * t + n, :], zT[:, blk, OFF[t]:OFF[t] + ROWS[t]],
                                               ring[:, blk // 4, at:at + 512], start=(blk == 0), stop=(blk == ZB - 1))
                    mm.then_inc(wout_done, 1)

        def layer_norm(tag, sub, ln_count):
            with ExitStack() as st:
                s = phase_semaphores(st, f"_{tag}")

                stats = buf(st, "stats", [P, NT, 2, 6])
                mv = buf(st, "mv", [P, NT, 2])
                var_done, std_done, norm_done, turned, copied, dve, stored = map(
                    s, ["var_done", "std_done", "norm_done", "turned", "copied", "dve", "stored"])
                block = st.enter_context(nc.Block())
                last = tag == "f1"

                @block.vector
                def _(v):
                    step = Tally(dve)
                    for t in range(NT):
                        r = ROWS[t]
                        xt = X[0:r, t, :]
                        step.mark(v.scalar_tensor_tensor(out=xt, in0=xt, scalar=ALPHA, in1=sub(t), op0=ALU.mult, op1=ALU.add))
                        step.settle(v)
                        for n in range(2):
                            ins = v.bn_stats(stats[0:r, t, n, :], X[0:r, t, n * 512:(n + 1) * 512])
                        step.mark(ins)
                        step.settle(v)
                        v.bn_aggr(mv[0:r, t, :], stats[0:r, t, :, :].rearrange("p n s -> p (n s)")).then_inc(var_done, 1)
                    v.wait_ge(ln_in, 16 * ln_count)
                    for t in range(NT):
                        r = ROWS[t]
                        xt = X[0:r, t, :]
                        v.wait_ge(std_done, t + 1)
                        step.mark(v.reciprocal(mv[0:r, t, 1:2], mv[0:r, t, 1:2]))
                        step.settle(v)
                        step.mark(v.tensor_scalar(xt, xt, mv[0:r, t, 0:1], mv[0:r, t, 1:2], ALU.subtract, ALU.mult))
                        step.settle(v)
                        step.mark(v.tensor_tensor(xt, xt, lnp[0:r, 0, :], ALU.mult))
                        step.settle(v)
                        v.tensor_tensor(xt, xt, lnp[0:r, 1, :], ALU.add).then_inc(norm_done, 1)

                @block.scalar
                def _(act):
                    for t in range(NT):
                        act.wait_ge(var_done, t + 1)
                        r = ROWS[t]
                        act.activation(mv[0:r, t, 1:2], mv[0:r, t, 1:2], ACT.Sqrt, bias=eps[0:r, 0:1]).then_inc(std_done, 1)
                    if not last:
                        for k in range(KD):
                            act.wait_ge(turned, k + 1)
                            act.activation(XT[:, k, :], ps[:, 6 + k % 2, 0:TOK], ACT.Copy).then_inc(copied, 1)

                if not last:
                    @block.tensor
                    def _(pe):
                        pe.wait_ge(norm_done, NT)
                        for k in range(KD):
                            if k >= 2:
                                pe.wait_ge(copied, k - 1)
                            for t in range(NT):
                                tr = pe.transpose(ps[:, 6 + k % 2, OFF[t]:OFF[t] + ROWS[t]],
                                                  X[0:ROWS[t], t, k * P:(k + 1) * P], ident[0:ROWS[t], 0:ROWS[t]])
                            tr.then_inc(turned, 1)

                @block.sync
                def _(sp):
                    sp.wait_ge(norm_done, NT)
                    if last:
                        sp.dma_start(o["y"], X[:, :, :]).then_inc(stored, 16)
                        sp.wait_ge(stored, 16)
                    else:
                        sp.dma_start(lnp[:, :, :], a["ln"][ln_count]).then_inc(ln_in, 16)

        def moe(layer, acc):
            with ExitStack() as st:
                s = phase_semaphores(st, f"_m{layer}")

                def wide(n, w=EXPERTS, dt_=F32):
                    return buf(st, n, [P, NT, w], dt_)

                router = buf(st, "router", [P, KD, EXPERTS])
                rbias = buf(st, "rbias", [P, EXPERTS])
                aff, sel, eq, pick1, pick2, took, pos = map(
                    wide, ["aff", "sel", "eq", "pick1", "pick2", "took", "pos"])
                top = buf(st, "top", [P, NT, MGROUPS, 8])
                gs, geq = wide("gs", MGROUPS), wide("geq", MGROUPS)
                mx = buf(st, "mx", [P, NT])
                rowb, rowp, wk, rowq, inw, gw = (buf(st, n, [P, 2, NT]) for n in
                                                 ["rowb", "rowp", "wk", "rowq", "inw", "gw"])
                to_slot = buf(st, "to_slot", [P, 2, NT], I32)
                from_slot = buf(st, "from_slot", [P, 2, NT], I32)
                count = buf(st, "count", [P, 1])
                windows = buf(st, "windows", [P, 1], I32)
                woff = buf(st, "woff", [P, 1])
                xs = buf(st, "xs", [P, 2, D])
                xsT = buf(st, "xsT", [P, 2, KD, P])
                sg = buf(st, "sg", [P, 2, 2 * SLOTS])
                hT = buf(st, "hT", [P, 2, 2 * SLOTS])
                ys = buf(st, "ys", [P, 2, D])
                got = buf(st, "got", [P, 2, D])

                (router_in, logit_done, logit_copied, aff_done, took_done, pos_done, windows_set, index_set, scattered,
                 turned, xs_act, xs_dve, gu_done, silu_done, h_done, y_act, y_dve, summed, passed, dve) = map(s, [
                     "router_in", "logit_done", "logit_copied", "aff_done", "took_done", "pos_done", "windows_set",
                     "index_set", "scattered", "turned", "xs_act", "xs_dve", "gu_done", "silu_done", "h_done",
                     "y_act", "y_dve", "summed", "passed", "dve"])
                w_in = [s(f"w_in{i}") for i in range(4)]
                w_used = [s(f"w_used{i}") for i in range(4)]
                xs_in = [s("xs_in0"), s("xs_in1")]
                ys_out = [s("ys_out0"), s("ys_out1")]
                got_in = [s("got_in0"), s("got_in1")]
                block = st.enter_context(nc.Block())

                LG = 0
                TP, GU, YB = (0, 1), (2, 3), ((4, 5), (6, 7))
                BODIES = EXPERTS // 4

                def load_windows(eng):
                    eng.wait_ge(windows_set, 1)
                    return eng.value_load(windows[0:1, 0:1], min_val=1, max_val=MAX_WINDOWS)

                @block.sync
                def _(sp):
                    sp.dma_start(router[:, :, :], a["router"][layer]).then_inc(router_in, 16)
                    sp.dma_start(rbias[:, :], a["rbias"][layer]).then_inc(router_in, 16)

                    def weights(i, e, n):
                        src = a["experts"][ds(sp.snap(layer * EXPERTS + e), 1)].rearrange("e p n -> (e p) n")
                        if n is not None:
                            sp.wait_ge(w_used[i], n)
                        sp.dma_start(ring[:, i, :], src).then_inc(w_in[i], 16)

                    for i in range(4):
                        sp.dma_start(ring[:, i, :], a["experts"][layer * EXPERTS + i]).then_inc(w_in[i], 16)
                    n_windows = load_windows(sp)
                    with sp.Fori(0, n_windows) as w:
                        base = sp.snap(BODIES * w)
                        n_scat = sp.snap(2 * NT * 16 * w + 2 * NT * 16)
                        sp.wait_ge(scattered, n_scat)
                        for p in range(2):
                            sp.dma_start(xs[:, p, :], xs_dram[p * P:(p + 1) * P, :]).then_inc(xs_in[p], 16)
                        with sp.Fori(0, BODIES - 1) as it:
                            for p in range(2):
                                src = xs_dram[ds(sp.snap((2 * it + 2 + p) * P), P), :]
                                n_t = sp.snap(2 * (base + it) + p + 1)
                                sp.wait_ge(turned, n_t)
                                sp.dma_start(xs[:, p, :], src).then_inc(xs_in[p], 16)
                                for e in range(2):
                                    i = 2 * p + e
                                    weights(i, 4 * it + 4 + i, sp.snap(base + it + 1))
                        n_u = sp.snap(base + BODIES)
                        with sp.If(w + 1 < n_windows):
                            for i in range(4):
                                sp.wait_ge(w_used[i], n_u)
                                sp.dma_start(ring[:, i, :], a["experts"][layer * EXPERTS + i]).then_inc(w_in[i], 16)

                @block.tensor
                def _(pe):
                    pe.wait_ge(router_in, 32)
                    for t in range(NT):
                        r = ROWS[t]
                        for k in range(KD):
                            mm = pe.matmul(ps[0:r, LG, t * EXPERTS:(t + 1) * EXPERTS], XT[:, k, OFF[t]:OFF[t] + r],
                                           router[:, k, :], start=(k == 0), stop=(k == KD - 1))
                    mm.then_inc(logit_done, 1)
                    pe.wait_ge(took_done, 1)
                    for t in range(NT):
                        out = ps[:, 1, t * EXPERTS:(t + 1) * EXPERTS]
                        for e in range(t):
                            pe.matmul(out, const("ones"), took[:, e, :], start=(e == 0), stop=False)
                        pe.matmul(out, const("strict"), took[:, t, :], start=(t == 0), stop=True)
                    for t in range(NT):
                        mm = pe.matmul(ps[:, 1, 128:128 + EXPERTS], const("ones"), took[:, t, :],
                                       start=(t == 0), stop=(t == NT - 1))
                    mm.then_inc(pos_done, 1)
                    with pe.Fori(0, load_windows(pe)) as w:
                        with pe.Fori(0, BODIES) as it:
                            n = pe.snap(BODIES * w + it)
                            for p in range(2):
                                j = 2 * n + p
                                pe.wait_ge(xs_in[p], 16 * n + 16)
                                pe.wait_ge(xs_act, j)
                                pe.wait_ge(xs_dve, j)
                                for k in range(KD):
                                    tr = pe.transpose(ps[:, TP[k // 4], (k % 4) * P:(k % 4 + 1) * P],
                                                      xs[:, p, k * P:(k + 1) * P], ident)
                                tr.then_inc(turned, 1)
                                pe.wait_ge(xs_act, j + 1)
                                pe.wait_ge(xs_dve, j + 1)
                                for e in range(2):
                                    i = 2 * p + e
                                    pe.wait_ge(w_in[i], 16 * n + 16)
                                    pe.wait_ge(h_done, 2 * j)
                                    for f in range(4):
                                        for k in range(KD):
                                            at = (f // 2) * KD * FF + k * FF + (f % 2) * P
                                            mm = pe.matmul(ps[:, GU[e], f * SLOTS:(f + 1) * SLOTS],
                                                           ring[:, i, at:at + P], xsT[:, p, k, e * SLOTS:(e + 1) * SLOTS],
                                                           start=(k == 0), stop=(k == KD - 1))
                                    mm.then_inc(gu_done, 1)
                                pe.wait_ge(y_act, 2 * n)
                                pe.wait_ge(y_dve, 2 * n)
                                for e in range(2):
                                    i = 2 * p + e
                                    pe.wait_ge(h_done, 2 * j + e + 1)
                                    for m in range(2):
                                        for f in range(2):
                                            at = 2 * KD * FF + f * D + m * 512
                                            mm = pe.matmul(ps[e * SLOTS:(e + 1) * SLOTS, YB[p][m], :],
                                                           hT[:, e, f * SLOTS:(f + 1) * SLOTS], ring[:, i, at:at + 512],
                                                           start=(f == 0), stop=(f == 1))
                                    mm.then_inc(w_used[i], 1)

                @block.scalar
                def _(act):
                    act.wait_ge(logit_copied, 1)
                    act.activation(aff[:, :, :], aff[:, :, :], ACT.Sigmoid).then_inc(aff_done, 1)
                    with act.Fori(0, load_windows(act)) as w:
                        with act.Fori(0, BODIES) as it:
                            n = act.snap(BODIES * w + it)
                            for p in range(2):
                                j = 2 * n + p
                                act.wait_ge(turned, j + 1)
                                act.activation(xsT[:, p, 0:4, :], ps[:, TP[0], :].rearrange("p (k s) -> p k s", k=4),
                                               ACT.Copy).then_inc(xs_act, 1)
                                for e in range(2):
                                    act.wait_ge(gu_done, 2 * j + e + 1)
                                    act.wait_ge(h_done, 2 * j)
                                    act.activation(sg[:, e, :], ps[:, GU[e], 0:2 * SLOTS], ACT.Silu).then_inc(silu_done, 1)
                                act.wait_ge(w_used[2 * p + 1], n + 1)
                                act.wait_ge(ys_out[p], 16 * n)
                                act.activation(ys[:, p, 0:512], ps[:, YB[p][0], :], ACT.Copy).then_inc(y_act, 1)

                @block.gpsimd
                def _(pool):
                    last_row = pool.to_reg(NSLOT - 1)
                    with pool.Fori(0, load_windows(pool)) as w:
                        pool.wait_ge(index_set, w + 1)
                        pool.sem_inc(passed, 1)
                        for k in range(2):
                            for t in range(NT):
                                r = ROWS[t]
                                pool.indirect_dma_start(
                                    out=xs_dram, out_offset=bass.IndirectOffsetOnAxis(ap=to_slot[0:r, k, t:t + 1], axis=0),
                                    in_=X[0:r, t, :], in_offset=None, bounds_check=last_row,
                                    oob_is_err=False).then_inc(scattered, 16)
                        with pool.Fori(0, BODIES) as it:
                            n = pool.snap(BODIES * w + it)
                            for p in range(2):
                                rows = ys_dram[ds(pool.snap((2 * it + p) * P), P), :]
                                pool.wait_ge(y_act, 2 * n + p + 1)
                                pool.wait_ge(y_dve, 2 * n + p + 1)
                                pool.dma_start(rows, ys[:, p, :]).then_inc(ys_out[p], 16)
                        for p in range(2):
                            pool.wait_ge(ys_out[p], 16 * BODIES * (w + 1))
                        for t in range(NT):
                            for k in range(2):
                                r = ROWS[t]
                                pool.wait_ge(summed, 2 * NT * w + max(0, 2 * t + k - 1))
                                pool.sem_inc(passed, 1)
                                pool.indirect_dma_start(
                                    out=got[0:r, k, :], out_offset=None, in_=ys_dram,
                                    in_offset=bass.IndirectOffsetOnAxis(ap=from_slot[0:r, k, t:t + 1], axis=0),
                                    bounds_check=last_row, oob_is_err=True).then_inc(got_in[k], 16)

                @block.vector
                def _(v):
                    step = Tally(dve)

                    def do(ins):
                        step.mark(ins)
                        step.settle(v)

                    def tt(out, x, y, op):
                        do(v.tensor_tensor(out, x, y, op))

                    def spread(x, w):
                        return x.unsqueeze(2).to_broadcast([P, NT, w])

                    v.memset(acc[:, :, :], 0.0)
                    do(v.memset(aff[:, :, :], 0.0))
                    v.wait_ge(logit_done, 1)
                    v.tensor_copy(aff[:, 0:2, :], ps[:, LG, 0:64].rearrange("p (t e) -> p t e", t=2))
                    v.tensor_copy(aff[0:64, 2, :], ps[0:64, LG, 64:96]).then_inc(logit_copied, 1)
                    v.wait_ge(aff_done, 1)
                    v.wait_ge(router_in, 32)
                    tt(sel[:, :, :], aff[:, :, :], rbias[:, :].unsqueeze(1).to_broadcast([P, NT, EXPERTS]), ALU.add)
                    for t in range(NT):
                        for g in range(MGROUPS):
                            ins = v.max(top[:, t, g, :], sel[:, t, g * EG:(g + 1) * EG])
                    do(ins)
                    tt(gs[:, :, :], top[:, :, :, 0], top[:, :, :, 1], ALU.add)

                    def first_best(out, values, desc, w):
                        do(v.tensor_reduce(mx[:, :], values, X_AXIS, ALU.max))
                        tt(out, values, spread(mx[:, :], w), ALU.is_ge)
                        tt(out, out, desc.unsqueeze(1).to_broadcast([P, NT, w]), ALU.mult)
                        do(v.tensor_reduce(mx[:, :], out, X_AXIS, ALU.max))
                        tt(out, out, spread(mx[:, :], w), ALU.is_ge)

                    first_best(geq[:, :, :], gs[:, :, :], const("desc4"), MGROUPS)
                    do(v.tensor_scalar(geq[:, :, :], geq[:, :, :], -1.0, -NEG, ALU.add, ALU.mult))
                    sel4 = sel[:, :, :].rearrange("p t (g e) -> p (t g) e", e=EG)
                    g4 = geq[:, :, :].rearrange("p t g -> p (t g)").unsqueeze(2).to_broadcast([P, NT * MGROUPS, EG])
                    tt(sel4, sel4, g4, ALU.add)
                    first_best(pick1[:, :, :], sel[:, :, :], const("desc32"), EXPERTS)
                    do(v.scalar_tensor_tensor(out=sel[:, :, :], in0=pick1[:, :, :], scalar=10 * NEG, in1=sel[:, :, :],
                                              op0=ALU.mult, op1=ALU.add))
                    first_best(pick2[:, :, :], sel[:, :, :], const("desc32"), EXPERTS)
                    tt(took[:, :, :], pick1[:, :, :], pick2[:, :, :], ALU.add)
                    v.tensor_tensor(took[:, :, :], took[:, :, :], spread(const("valid"), EXPERTS),
                                    ALU.mult).then_inc(took_done, 1)
                    picks = [pick1, pick2]

                    def picked(out, table):
                        for k in range(2):
                            tt(eq[:, :, :], picks[k][:, :, :], table, ALU.mult)
                            do(v.tensor_reduce(out[:, k, :], eq[:, :, :], X_AXIS, ALU.add))

                    picked(wk, aff[:, :, :])
                    tt(mx[:, :], wk[:, 0, :], wk[:, 1, :], ALU.add)
                    do(v.reciprocal(mx[:, :], mx[:, :]))
                    tt(wk[:, :, :], wk[:, :, :], mx[:, :].unsqueeze(1).to_broadcast([P, 2, NT]), ALU.mult)
                    picked(rowb, const("ebase").unsqueeze(1).to_broadcast([P, NT, EXPERTS]))
                    v.wait_ge(pos_done, 1)
                    do(v.tensor_copy(pos[:, :, :], ps[:, 1, 0:NT * EXPERTS].rearrange("p (t e) -> p t e", t=NT)))
                    do(v.tensor_reduce(count[:, :], ps[:, 1, 128:128 + EXPERTS], X_AXIS, ALU.max))
                    v.tensor_scalar(windows[:, :], count[:, :], 1.0 / SLOTS, 0.5 - 0.5 / SLOTS,
                                    ALU.mult, ALU.add).then_inc(windows_set, 1)
                    picked(rowp, pos[:, :, :])
                    do(v.memset(woff[:, :], 0.0))
                    total = step.n
                    PER_WINDOW = 9
                    with v.Fori(0, load_windows(v)) as w:
                        step.loop(v.snap(w * PER_WINDOW + total))
                        do(v.tensor_scalar(rowq[:, :, :], rowp[:, :, :], woff[:, 0:1], None, ALU.subtract))
                        do(v.tensor_scalar(inw[:, :, :], rowq[:, :, :], 0.0, None, ALU.is_ge))
                        do(v.scalar_tensor_tensor(out=inw[:, :, :], in0=rowq[:, :, :], scalar=float(SLOTS),
                                                  in1=inw[:, :, :], op0=ALU.is_lt, op1=ALU.mult))
                        tt(inw[:, :, :], inw[:, :, :], const("valid").unsqueeze(1).to_broadcast([P, 2, NT]), ALU.mult)
                        tt(rowq[:, :, :], rowq[:, :, :], rowb[:, :, :], ALU.add)
                        tt(gw[:, :, :], wk[:, :, :], inw[:, :, :], ALU.mult)
                        tt(from_slot[:, :, :], rowq[:, :, :], inw[:, :, :], ALU.mult)
                        do(v.scalar_tensor_tensor(out=rowq[:, :, :], in0=rowq[:, :, :], scalar=-2.0 * NSLOT,
                                                  in1=inw[:, :, :], op0=ALU.add, op1=ALU.mult))
                        do(v.tensor_scalar(woff[:, :], woff[:, :], float(SLOTS), None, ALU.add))
                        v.tensor_scalar(to_slot[:, :, :], rowq[:, :, :], 2.0 * NSLOT, None,
                                        ALU.add).then_inc(index_set, 1)
                        with v.Fori(0, BODIES) as it:
                            n = v.snap(BODIES * w + it)
                            for p in range(2):
                                j = 2 * n + p
                                v.wait_ge(turned, j + 1)
                                v.tensor_copy(xsT[:, p, 4:8, :],
                                              ps[:, TP[1], :].rearrange("p (k s) -> p k s", k=4)).then_inc(xs_dve, 1)
                                for e in range(2):
                                    v.wait_ge(silu_done, 2 * j + e + 1)
                                    if p:
                                        v.wait_ge(w_used[e], n + 1)
                                    else:
                                        v.wait_ge(w_used[2 + e], n)
                                    v.tensor_tensor(hT[:, e, :], sg[:, e, :], ps[:, GU[e], 2 * SLOTS:4 * SLOTS],
                                                    ALU.mult).then_inc(h_done, 1)
                                v.wait_ge(w_used[2 * p + 1], n + 1)
                                v.wait_ge(ys_out[p], 16 * n)
                                v.tensor_copy(ys[:, p, 512:D], ps[:, YB[p][1], :]).then_inc(y_dve, 1)
                        for t in range(NT):
                            for k in range(2):
                                r = ROWS[t]
                                v.wait_ge(got_in[k], 16 * (NT * w + t + 1))
                                v.wait_ge(summed, 2 * NT * w + 2 * t + k)
                                v.scalar_tensor_tensor(out=acc[0:r, t, :], in0=got[0:r, k, :], scalar=gw[0:r, k, t:t + 1],
                                                       in1=acc[0:r, t, :], op0=ALU.mult, op1=ALU.add).then_inc(summed, 1)

        def attention():
            with ExitStack() as att:
                L = buf(att, "L", [P, NT, DQKV])
                kvT = buf(att, "kvT", [P, 2, TOK])
                krT = buf(att, "krT", [ROPE, TOK])
                qlatT = buf(att, "qlatT", [P, 2, AH, TOK])
                qrT = buf(att, "qrT", [ROPE, AH, TOK])
                pages = buf(att, "pages", [1, DEC_B * PAGES], I32)
                w_dqkv = ring[:, 0, 0:KD * DQKV]
                w_uq = ring[:, 1, 0:3 * AH * (NOPE + ROPE)]
                w_ukT = ring[:, 2, 0:AH * KL]
                w_uv = ring[:, 2, AH * KL:2 * AH * KL]
                UQ = AH * (NOPE + ROPE)

                def w_o(k):
                    return ring[:, 3, k * D:(k + 1) * D] if k < 6 else ring[:, 2, (k - 2) * D:(k - 1) * D]

                latents(L, kvT, krT, qlatT, qrT, pages, w_dqkv, w_uq, w_ukT, w_uv, w_o, UQ)
                with ExitStack() as st:
                    olatT = buf(st, "olatT", [P, 2, AH, TOK])
                    prompt_attention(L, kvT, krT, qlatT, qrT, olatT, pages)
                    sample_attention(L, kvT, krT, qlatT, qrT, olatT, pages)
                    attention_output(olatT, w_uv, w_o)

        def latents(L, kvT, krT, qlatT, qrT, pages, w_dqkv, w_uq, w_ukT, w_uv, w_o, UQ):
            with ExitStack() as st:
                s = phase_semaphores(st)
                cqT = buf(st, "cqT", [P, 3, TOK])
                qnT = buf(st, "qnT", [P, 2, TOK])
                qkn = buf(st, "qkn", [P, QL + KL])
                ss = buf(st, "ss", [P, NT, 2])
                sqs = buf(st, "sqs", [P, QL])
                qr = buf(st, "qr", [P, 2, AH, ROPE])
                r4 = buf(st, "r4", [P, 4, AH, ROPE // 2])
                kr4 = buf(st, "kr4", [P, 4, NT, ROPE // 2])
                (dq_in, uq_in, uk_in, small_in, dq_done, l_copied, ss_done, std_done, norm_done, kr_done, turned, tcopied,
                 qn_done, qn_copied, ql_done, ql_copied, qr_done, qr_ready, qrt_done, qrt_copied, out_done, dve) = map(s, [
                     "dq_in", "uq_in", "uk_in", "small_in", "dq_done", "l_copied", "ss_done", "std_done", "norm_done",
                     "kr_done", "turned", "tcopied", "qn_done", "qn_copied", "ql_done", "ql_copied", "qr_done",
                     "qr_ready", "qrt_done", "qrt_copied", "out_done", "dve"])
                block = st.enter_context(nc.Block())

                @block.sync
                def _(sp):
                    sp.dma_start(w_dqkv, a["w_dqkv"]).then_inc(dq_in, 16)
                    sp.dma_start(w_uq, a["w_uq"]).then_inc(uq_in, 16)
                    sp.dma_start(w_ukT, a["w_ukT"]).then_inc(uk_in, 16)
                    sp.dma_start(qkn[:, :], a["qkn"]).then_inc(small_in, 16)
                    sp.dma_start(pages[:, :], a["pages"]).then_inc(small_in, 16)
                    sp.dma_start(w_uv, a["w_uv"]).then_inc(wo_in, 16)
                    sp.dma_start(ring[:, 3, 0:6 * D], a["w_o"][:, 0:6, :]).then_inc(wo_in, 16)
                    sp.dma_start(ring[:, 2, 4 * D:6 * D], a["w_o"][:, 6:8, :]).then_inc(wo_in, 16)
                    sp.wait_ge(norm_done, NT)
                    sp.dma_start(o["lat"], L[:, :, QL:QL + KL]).then_inc(out_done, 16)
                    sp.wait_ge(kr_done, 1)
                    sp.dma_start(o["kr"], L[:, :, QL + KL:DQKV]).then_inc(out_done, 16)
                    sp.wait_ge(out_done, 32)
                    sp.wait_ge(small_in, 32)

                TB = (4, 5)
                turns = [(L, i * P, P, (cqT, i)) for i in range(3)] + [(L, QL + i * P, P, (kvT, i)) for i in range(2)]

                @block.tensor
                def _(pe):
                    pe.wait_ge(dq_in, 16)
                    for t in range(NT):
                        r = ROWS[t]
                        if t == 2:
                            pe.wait_ge(l_copied, 1)
                        for n, (lo, hi) in enumerate(((0, 512), (512, DQKV))):
                            for k in range(KD):
                                mm = pe.matmul(ps[0:r, 2 * (t % 2) + n, 0:hi - lo], XT[:, k, OFF[t]:OFF[t] + r],
                                               w_dqkv[:, k * DQKV + lo:k * DQKV + hi], start=(k == 0), stop=(k == KD - 1))
                        mm.then_inc(dq_done, 1)
                    pe.wait_ge(norm_done, NT)
                    for n in range(6):
                        if n >= 2:
                            pe.wait_ge(tcopied, n - 1)
                        if n == 5:
                            pe.wait_ge(kr_done, 1)
                        lo, w = (n * P, P) if n < 5 else (QL + KL, ROPE)
                        for t in range(NT):
                            r = ROWS[t]
                            tr = pe.transpose(ps[0:w, TB[n % 2], OFF[t]:OFF[t] + r], L[0:r, t, lo:lo + w], ident[0:r, 0:r])
                        tr.then_inc(turned, 1)
                    pe.wait_ge(tcopied, 3)
                    pe.wait_ge(uq_in, 16)
                    pe.wait_ge(l_copied, NT)

                    def nope(h):
                        if h >= 2:
                            pe.wait_ge(qn_copied, h - 1)
                        for k in range(3):
                            mm = pe.matmul(ps[:, h % 2, 0:TOK], w_uq[:, k * UQ + h * NOPE:k * UQ + (h + 1) * NOPE],
                                           cqT[:, k, :], start=(k == 0), stop=(k == 2))
                        mm.then_inc(qn_done, 1)

                    def absorb(h):
                        pe.wait_ge(qn_copied, h + 1)
                        if h == 0:
                            pe.wait_ge(uk_in, 16)
                        else:
                            pe.wait_ge(ql_copied, 2 * h)
                        for c in range(2):
                            pe.matmul(ps[:, 2 + c, 0:TOK], w_ukT[:, h * KL + c * P:h * KL + (c + 1) * P],
                                      qnT[:, h % 2, :], start=True, stop=True).then_inc(ql_done, 1)

                    for h in range(AH):
                        nope(h)
                        if h:
                            absorb(h - 1)
                    absorb(AH - 1)
                    pe.wait_ge(tcopied, 6)

                    def rope_in(t):
                        r = ROWS[t]
                        if t == 2:
                            pe.wait_ge(qr_ready, 1)
                        for k in range(3):
                            mm = pe.matmul(ps[0:r, TB[t % 2], :], cqT[:, k, OFF[t]:OFF[t] + r],
                                           w_uq[:, k * UQ + AH * NOPE:(k + 1) * UQ], start=(k == 0), stop=(k == 2))
                        mm.then_inc(qr_done, 1)

                    def rope_turn(t):
                        r = ROWS[t]
                        pe.wait_ge(qr_ready, t + 1)
                        for half in range(2):
                            if t:
                                pe.wait_ge(qrt_copied, 2 * t + half - 1)
                            for j in range(4):
                                tr = pe.transpose(ps[0:ROPE, 6 + half, j * P:j * P + r], qr[0:r, t % 2, 4 * half + j, :],
                                                  ident[0:r, 0:r])
                            tr.then_inc(qrt_done, 1)

                    rope_in(0)
                    rope_in(1)
                    rope_turn(0)
                    rope_in(2)
                    rope_turn(1)
                    rope_turn(2)

                @block.scalar
                def _(act):
                    for t in range(NT):
                        r = ROWS[t]
                        act.wait_ge(dq_done, t + 1)
                        if t == 2:
                            act.wait_ge(dve, 1)
                        b = 2 * (t % 2)
                        act.activation(L[0:r, t, 0:512], ps[0:r, b, :], ACT.Copy)
                        act.activation(L[0:r, t, 512:DQKV], ps[0:r, b + 1, 0:DQKV - 512], ACT.Copy).then_inc(l_copied, 1)
                    for t in range(NT):
                        r = ROWS[t]
                        act.wait_ge(ss_done, 2 * t + 2)
                        for n, w in enumerate((QL, KL)):
                            ins = act.activation(ss[0:r, t, n:n + 1], ss[0:r, t, n:n + 1], ACT.Sqrt, scale=1.0 / w,
                                                 bias=eps[0:r, 1:2])
                        ins.then_inc(std_done, 1)
                    for n in range(6):
                        act.wait_ge(turned, n + 1)
                        dst = cqT[:, n, :] if n < 3 else kvT[:, n - 3, :] if n < 5 else krT[:, :]
                        w = P if n < 5 else ROPE
                        act.activation(dst, ps[0:w, TB[n % 2], 0:TOK], ACT.Copy).then_inc(tcopied, 1)
                    for h in range(AH):
                        for c in range(2):
                            act.wait_ge(ql_done, 2 * h + c + 1)
                            act.activation(qlatT[:, c, h, :], ps[:, 2 + c, 0:TOK], ACT.Copy).then_inc(ql_copied, 1)
                    for t in range(NT):
                        r = ROWS[t]
                        for half in range(2):
                            act.wait_ge(qrt_done, 2 * t + half + 1)
                            act.activation(qrT[:, 4 * half:4 * half + 4, OFF[t]:OFF[t] + r],
                                           ps[0:ROPE, 6 + half, :].rearrange("p (j s) -> p j s", j=4)[:, :, 0:r],
                                           ACT.Copy).then_inc(qrt_copied, 1)

                @block.vector
                def _(v):
                    step = Tally(dve)
                    step.mark(v.memset(L[64:P, 2, :], 0.0))
                    cos, sin = const3("cos"), const3("sin")
                    for t in range(NT):
                        r = ROWS[t]
                        v.wait_ge(l_copied, t + 1)
                        for n, (lo, w) in enumerate(((0, QL), (QL, KL))):
                            x = L[0:r, t, lo:lo + w]
                            if t + n:
                                v.wait_ge(ss_done, 2 * t + n)
                            v.tensor_tensor_reduce(sqs[0:r, 0:w], x, x, 1.0, 0.0, ALU.mult, ALU.add,
                                                   ss[0:r, t, n:n + 1]).then_inc(ss_done, 1)
                    v.wait_ge(small_in, 32)
                    for t in range(NT):
                        r = ROWS[t]
                        v.wait_ge(std_done, t + 1)
                        step.mark(v.reciprocal(ss[0:r, t, :], ss[0:r, t, :]))
                        step.settle(v)
                        for n, (lo, w) in enumerate(((0, QL), (QL, KL))):
                            x = L[0:r, t, lo:lo + w]
                            ins = v.scalar_tensor_tensor(out=x, in0=x, scalar=ss[0:r, t, n:n + 1], in1=qkn[0:r, lo:lo + w],
                                                         op0=ALU.mult, op1=ALU.mult)
                        ins.then_inc(norm_done, 1)

                    def rotate(out1, out2, x1, x2, c, sn, tmp4):
                        v.tensor_tensor(tmp4[0], x1, c, ALU.mult)
                        v.tensor_tensor(tmp4[1], x2, sn, ALU.mult)
                        v.tensor_tensor(tmp4[2], x2, c, ALU.mult)
                        step.mark(v.tensor_tensor(tmp4[3], x1, sn, ALU.mult))
                        step.settle(v)
                        v.tensor_tensor(out1, tmp4[0], tmp4[1], ALU.subtract)
                        return v.tensor_tensor(out2, tmp4[2], tmp4[3], ALU.add)

                    k1, k2 = L[:, :, QL + KL:QL + KL + 32], L[:, :, QL + KL + 32:DQKV]
                    rotate(k1, k2, k1, k2, cos, sin, [kr4[:, i, :, :] for i in range(4)]).then_inc(kr_done, 1)
                    for h in range(AH):
                        v.wait_ge(qn_done, h + 1)
                        if h >= 2:
                            v.wait_ge(ql_done, 2 * (h - 1))
                        v.tensor_copy(qnT[:, h % 2, :], ps[:, h % 2, 0:TOK]).then_inc(qn_copied, 1)
                    for t in range(NT):
                        r = ROWS[t]
                        v.wait_ge(qr_done, t + 1)
                        if t == 2:
                            v.wait_ge(qrt_done, 2)
                        x = ps[0:r, TB[t % 2], :].rearrange("p (h e) -> p h e", h=AH)
                        cb = cos[0:r, t, :].unsqueeze(1).to_broadcast([r, AH, 32])
                        sb = sin[0:r, t, :].unsqueeze(1).to_broadcast([r, AH, 32])
                        q = qr[0:r, t % 2, :, :]
                        if t:
                            v.wait_ge(qr_ready, t)
                        rotate(q[:, :, 0:32], q[:, :, 32:64], x[:, :, 0:32], x[:, :, 32:64], cb, sb,
                               [r4[0:r, i, :, :] for i in range(4)]).then_inc(qr_ready, 1)

        def load_keys(sp, pages, b, at, wait=None):
            for i in range(PAGES):
                page = sp.value_load(pages[0:1, ds(at + i, 1)], min_val=0, max_val=a["latent"].shape[0] - 1)
                lat = a["latent"][ds(page, 1)].rearrange("a p n -> (a p) n")
                kr = a["krope"][ds(page, 1)].rearrange("a p n -> (a p) n")
                if i == 0 and wait is not None:
                    sp.wait_ge(*wait)
                sp.dma_start(ring[:, b, i * 512:(i + 1) * 512], lat).then_inc(key_in[b], 16)
                sp.dma_start(ring[0:ROPE, b, 4096 + i * PAGE:4096 + (i + 1) * PAGE], kr).then_inc(key_in[b], 16)

        def prompt_attention(L, kvT, krT, qlatT, qrT, olatT, pages):
            with ExitStack() as st:
                s = phase_semaphores(st)
                pr = buf(st, "pr", [P, 2, 2 * P])
                pT = buf(st, "pT", [P, 2, 2, P])
                nm = buf(st, "nm", [P, 2])
                sm = buf(st, "sm", [P, 2])
                sc_done, masked, max_done, exp_done, p_done, pt_done, pt_copied, o_done, o_copied, dve = map(s, [
                    "sc_done", "masked", "max_done", "exp_done", "p_done", "pt_done", "pt_copied", "o_done", "o_copied",
                    "dve"])
                block = st.enter_context(nc.Block())
                units = [(i, h) for i in range(2) for h in range(AH)]
                N = len(units)
                SB, TB, OB = (0, 1), (2, 3), (4, 5)

                @block.sync
                def _(sp):
                    for b in range(2):
                        load_keys(sp, pages, b, b * PAGES)

                @block.tensor
                def _(pe):
                    def scores(u):
                        i, h = units[u]
                        q, nk = slice(i * P, (i + 1) * P), (i + 1) * P
                        if u >= 2:
                            pe.wait_ge(masked, u - 1)
                        out = ps[:, SB[u % 2], 0:nk]
                        for c in range(2):
                            pe.matmul(out, qlatT[:, c, h, q], kvT[:, c, 0:nk], start=(c == 0), stop=False)
                        pe.matmul(out, qrT[:, h, q], krT[:, 0:nk], start=False, stop=True).then_inc(sc_done, 1)

                    def turn(u):
                        i, h = units[u]
                        pe.wait_ge(p_done, u + 1)
                        if u >= 2:
                            pe.wait_ge(pt_copied, u - 1)
                        for k in range(i + 1):
                            tr = pe.transpose(ps[:, TB[u % 2], k * P:(k + 1) * P], pr[:, u % 2, k * P:(k + 1) * P], ident)
                        tr.then_inc(pt_done, 1)

                    def values(u):
                        i, h = units[u]
                        pe.wait_ge(pt_copied, u + 1)
                        if u >= 2:
                            pe.wait_ge(o_copied, u - 1)
                        for c in range(2):
                            for k in range(i + 1):
                                mm = pe.matmul(ps[:, OB[u % 2], c * P:(c + 1) * P], L[:, k, QL + c * P:QL + (c + 1) * P],
                                               pT[:, u % 2, k, :], start=(k == 0), stop=(k == i))
                        mm.then_inc(o_done, 1)

                    for u in range(N + 2):
                        if u < N:
                            scores(u)
                        if 1 <= u <= N:
                            turn(u - 1)
                        if u >= 2:
                            values(u - 2)

                @block.vector
                def _(v):
                    def mask(u):
                        i, h = units[u]
                        nk = (i + 1) * P
                        v.wait_ge(sc_done, u + 1)
                        if u >= 2:
                            v.wait_ge(pt_done, u - 1)
                        v.scalar_tensor_tensor(out=pr[:, u % 2, 0:nk], in0=ps[:, SB[u % 2], 0:nk], scalar=ATT_SCALE,
                                               in1=C[:, CONST["causal"].stop - nk:CONST["causal"].stop],
                                               op0=ALU.mult, op1=ALU.add).then_inc(masked, 1)
                        v.wait_ge(masked, u + 1)
                        v.tensor_reduce(nm[:, u % 2:u % 2 + 1], pr[:, u % 2, 0:nk], X_AXIS, ALU.max,
                                        negate=True).then_inc(max_done, 1)

                    step = Tally(dve)

                    def normalise(u):
                        i, h = units[u]
                        v.wait_ge(exp_done, u + 1)
                        sc = sm[:, u % 2:u % 2 + 1]
                        step.mark(v.reciprocal(sc, sc))
                        step.settle(v)
                        x = pr[:, u % 2, 0:(i + 1) * P]
                        v.tensor_scalar(x, x, sc, None, ALU.mult).then_inc(p_done, 1)

                    for u in range(N + 1):
                        if u < N:
                            mask(u)
                        if u >= 1:
                            normalise(u - 1)

                @block.scalar
                def _(act):
                    for u in range(N + 2):
                        if u < N:
                            i, h = units[u]
                            act.wait_ge(max_done, u + 1)
                            if u >= 2:
                                act.wait_ge(p_done, u - 1)
                            x = pr[:, u % 2, 0:(i + 1) * P]
                            act.activation(x, x, ACT.Exp, bias=nm[:, u % 2:u % 2 + 1],
                                           accum_out=sm[:, u % 2:u % 2 + 1]).then_inc(exp_done, 1)
                        if 1 <= u <= N:
                            i, h = units[u - 1]
                            act.wait_ge(pt_done, u)
                            if u >= 3:
                                act.wait_ge(o_done, u - 2)
                            act.activation(pT[:, (u - 1) % 2, 0:i + 1, :],
                                           ps[:, TB[(u - 1) % 2], 0:(i + 1) * P].rearrange("p (k q) -> p k q", k=i + 1),
                                           ACT.Copy).then_inc(pt_copied, 1)
                        if u >= 2:
                            i, h = units[u - 2]
                            act.wait_ge(o_done, u - 1)
                            act.activation(olatT[:, :, h, i * P:(i + 1) * P],
                                           ps[:, OB[u % 2], 0:2 * P].rearrange("p (c q) -> p c q", c=2),
                                           ACT.Copy).then_inc(o_copied, 1)

        def sample_attention(L, kvT, krT, qlatT, qrT, olatT, pages):
            with ExitStack() as st:
                s = phase_semaphores(st)
                W = PAST + 64
                pr = buf(st, "pr", [64, 2, W])
                qb = buf(st, "qb", [P, 2, 2, 64])
                qrb = buf(st, "qrb", [ROPE, 2, 64])
                small = buf(st, "small", [64, 2, 8])
                q_done, sc_done, sc_read, max_done, exp_done, p_done, pt_done, pt_copied, o_done, o_copied, dve = map(s, [
                    "q_done", "sc_done", "sc_read", "max_done", "exp_done", "p_done", "pt_done", "pt_copied", "o_done",
                    "o_copied", "dve"])
                passed = s("passed")
                block = st.enter_context(nc.Block())
                pTs = [ring[:, b, 5120:5120 + 9 * 64] for b in range(2)]
                SB, TB, NB = ((0, 1, 2), (3, 4, 5)), 6, 7

                def lat(b, i):
                    return ring[:, b, i * 512:i * 512 + KL]

                @block.sync
                def _(sp):
                    with sp.Fori(0, 3) as it:
                        for b in range(2):
                            load_keys(sp, pages, b, sp.snap((2 * it + 2 + b) * PAGES), (o_done, sp.snap(2 * it + b + 1)))

                @block.gpsimd
                def _(pool):
                    with pool.Fori(0, 4) as it:
                        for b in range(2):
                            n = 2 * it + b
                            at = ds(SEQ + DEC_T * n, DEC_T)
                            pool.wait_ge(sc_done, 2 * it)
                            for c in range(2):
                                pool.tensor_copy(qb[:, b, c, :].rearrange("p (t h) -> p t h", h=AH),
                                                 qlatT[:, c, :, at].rearrange("p h t -> p t h"))
                            pool.tensor_copy(qrb[:, b, :].rearrange("p (t h) -> p t h", h=AH),
                                             qrT[:, :, at].rearrange("p h t -> p t h")).then_inc(q_done, 1)

                @block.tensor
                def _(pe):
                    def scores(b, it):
                        n = 2 * it + b
                        pe.wait_ge(q_done, n + 1)
                        pe.wait_ge(key_in[b], 256 * (it + 1))
                        pe.wait_ge(sc_read, 2 * it)
                        for half in range(2):
                            out = ps[0:64, SB[b][half], :]
                            for c in range(2):
                                keys = ring[:, b, half * 2048:(half + 1) * 2048].rearrange("p (i w) -> p i w", w=512)
                                pe.matmul(out, qb[:, b, c, :], keys[:, :, KL + c * PAGE:KL + (c + 1) * PAGE],
                                          start=(c == 0), stop=False)
                            pe.matmul(out, qrb[:, b, :], ring[0:ROPE, b, 4096 + half * 512:4096 + (half + 1) * 512],
                                      start=False, stop=True)
                        out = ps[0:64, SB[b][2], 0:64]
                        for c in range(2):
                            pe.matmul(out, qb[:, b, c, :], kvT[:, c, SAMPLE], start=(c == 0), stop=False)
                        pe.matmul(out, qrb[:, b, :], krT[:, SAMPLE], start=False, stop=True).then_inc(sc_done, 1)

                    def values(b, it):
                        n = 2 * it + b
                        pe.wait_ge(p_done, n + 1)
                        pe.wait_ge(o_copied, n)
                        pe.sem_inc(passed, 1)
                        for i in range(PAGES):
                            pe.transpose(ps[:, TB, i * 64:(i + 1) * 64], pr[:, b, i * P:(i + 1) * P], ident[0:64, 0:64])
                        pe.transpose(ps[0:64, NB, 0:64], pr[:, b, PAST:W], ident[0:64, 0:64]).then_inc(pt_done, 1)
                        pe.wait_ge(pt_copied, n + 1)
                        for c in range(2):
                            out = ps[:, NB, P + c * 64:P + (c + 1) * 64]
                            for i in range(PAGES):
                                pe.matmul(out, lat(b, i)[:, c * P:(c + 1) * P], pTs[b][:, i * 64:(i + 1) * 64],
                                          start=(i == 0), stop=False)
                            mm = pe.matmul(out, L[0:64, 2, QL + c * P:QL + (c + 1) * P], pTs[b][0:64, 512:576],
                                           start=False, stop=True)
                        mm.then_inc(o_done, 1)

                    scores(0, 0)
                    with pe.Fori(0, 3) as it:
                        scores(1, it)
                        values(0, it)
                        scores(0, pe.snap(it + 1))
                        values(1, it)
                    scores(1, 3)
                    values(0, 3)
                    values(1, 3)

                @block.vector
                def _(v):
                    step = Tally(dve)

                    def do(ins):
                        step.mark(ins)
                        step.settle(v)

                    def col(b, i):
                        return small[:, b, i:i + 1]

                    PER = 9
                    with v.Fori(0, 4) as it:
                        for b in range(2):
                            n = v.snap(2 * it + b)
                            step.loop(v.snap(n * PER))
                            v.wait_ge(sc_done, n + 1)
                            v.wait_ge(pt_done, 2 * it)
                            past = ps[0:64, SB[b][0]:SB[b][0] + 2, :].rearrange("p a k -> p (a k)")
                            new = pr[:, b, PAST:W]
                            msk = C[0:64, ds(CONST["smask"].start + n * 64, 64)]
                            do(v.scalar_tensor_tensor(out=new, in0=ps[0:64, SB[b][2], 0:64], scalar=ATT_SCALE, in1=msk,
                                                      op0=ALU.mult, op1=ALU.add))
                            do(v.tensor_reduce(col(b, 0), past, X_AXIS, ALU.max))
                            do(v.tensor_reduce(col(b, 1), new, X_AXIS, ALU.max))
                            do(v.scalar_tensor_tensor(out=col(b, 2), in0=col(b, 0), scalar=ATT_SCALE, in1=col(b, 1),
                                                      op0=ALU.mult, op1=ALU.max))
                            do(v.tensor_scalar(col(b, 3), col(b, 2), -1.0, None, ALU.mult))
                            do(v.tensor_copy(col(b, 6), col(b, 3)))
                            v.tensor_copy(col(b, 7), col(b, 3)).then_inc(max_done, 1)
                            v.wait_ge(exp_done, n + 1)
                            do(v.tensor_tensor(col(b, 4), col(b, 4), col(b, 5), ALU.add))
                            do(v.reciprocal(col(b, 4), col(b, 4)))
                            do(v.tensor_scalar(pr[:, b, :], pr[:, b, :], col(b, 4), None, ALU.mult))
                            v.tensor_copy(col(b, 0), col(b, 4)).then_inc(p_done, 1)

                @block.scalar
                def _(act):
                    with act.Fori(0, 4) as it:
                        for b in range(2):
                            n = act.snap(2 * it + b)
                            past = ps[0:64, SB[b][0]:SB[b][0] + 2, :].rearrange("p a k -> p (a k)")
                            act.wait_ge(max_done, n + 1)
                            act.activation(pr[:, b, 0:PAST], past, ACT.Exp, bias=small[:, b, 3:4], scale=ATT_SCALE,
                                           accum_out=small[:, b, 4:5]).then_inc(sc_read, 1)
                            act.activation(pr[:, b, PAST:W], pr[:, b, PAST:W], ACT.Exp, bias=small[:, b, 3:4],
                                           accum_out=small[:, b, 5:6]).then_inc(exp_done, 1)
                            act.wait_ge(pt_done, n + 1)
                            act.activation(pTs[b][:, 0:512], ps[:, TB, :], ACT.Copy)
                            act.activation(pTs[b][0:64, 512:576], ps[0:64, NB, 0:64], ACT.Copy).then_inc(pt_copied, 1)
                            act.wait_ge(o_done, n + 1)
                            at = ds(SEQ + DEC_T * n, DEC_T)
                            for c in range(2):
                                ins = act.activation(
                                    olatT[:, c, :, at],
                                    ps[:, NB, P + c * 64:P + (c + 1) * 64].rearrange("p (t h) -> p h t", h=AH), ACT.Copy)
                            ins.then_inc(o_copied, 1)

        def attention_output(olatT, w_uv, w_o):
            with ExitStack() as st:
                s = phase_semaphores(st)
                v_done, v_copied = s("v_done"), s("v_copied")
                block = st.enter_context(nc.Block())
                VB = (6, 7)

                @block.tensor
                def _(pe):
                    pe.wait_ge(wo_in, 48)

                    def head(h):
                        if h >= 2:
                            pe.wait_ge(v_copied, h - 1)
                        for c in range(2):
                            mm = pe.matmul(ps[:, VB[h % 2], 0:TOK],
                                           w_uv[:, c * AH * VH + h * VH:c * AH * VH + (h + 1) * VH],
                                           olatT[:, c, h, :], start=(c == 0), stop=(c == 1))
                        mm.then_inc(v_done, 1)

                    def project(h):
                        pe.wait_ge(v_copied, h + 1)
                        for t in range(NT):
                            for n in range(2):
                                pe.matmul(ps[0:ROWS[t], 2 * t + n, :], XT[:, h, OFF[t]:OFF[t] + ROWS[t]],
                                          w_o(h)[:, n * 512:(n + 1) * 512], start=(h == 0), stop=(h == AH - 1))

                    head(0)
                    for h in range(AH):
                        if h + 1 < AH:
                            head(h + 1)
                        project(h)

                @block.scalar
                def _(act):
                    for h in range(AH):
                        act.wait_ge(v_done, h + 1)
                        act.activation(XT[:, h, :], ps[:, VB[h % 2], 0:TOK], ACT.Copy).then_inc(v_copied, 1)

        in_projection()
        for c in range(NT):
            scan_chunk(c)
        sample_states()
        out_projection()
        ssd.close()

        def in_psum(t):
            return ps[0:ROWS[t], 2 * t:2 * t + 2, :].rearrange("p a n -> p (a n)")

        layer_norm("a0", in_psum, 1)
        for layer in range(2):
            if layer == 1:
                attention()
                layer_norm("a1", in_psum, 3)
            with ExitStack() as ffn:
                acc = buf(ffn, "acc", [P, NT, D])
                moe(layer, acc)
                layer_norm(f"f{layer}", lambda t: acc[0:ROWS[t], t, :], 2 * layer + 2)


def _lay_out(i):
    def by_k(w):
        return w.reshape(-1, P, w.shape[-1]).transpose(1, 0, 2)

    x = np.zeros((NT * P, D), np.float32)
    x[:TOK] = np.concatenate([i["x_prompt"].reshape(SEQ, D), i["x_sample"].reshape(-1, D)])
    w_in = i["ssd_w_in"][0]
    cw = i["ssd_conv_w"][0].reshape(4, XBCB, P).transpose(2, 1, 0).reshape(P, 4 * XBCB)
    cb = i["ssd_conv_b"][0].reshape(XBCB, P).T
    nw = i["ssd_norm_w"][0].reshape(ZB, P).T
    dk = np.repeat(i["ssd_d_skip"][0], HP).reshape(ZB, P).T
    conv = i["state_conv"][0].reshape(DEC_B, 3, XBCB, P).transpose(3, 2, 0, 1)
    rows = np.stack([i["ssd_dt_bias"][0], i["ssd_a_log"][0]])
    ln = np.stack([np.stack([i[f"ln_{k}_{g}"][l] for g in "gb"]) for l in range(2) for k in ("mix", "ffn")])
    experts = []
    for l in range(2):
        gate, up = (i[n][l].reshape(EXPERTS, KD, P, FF).transpose(0, 2, 1, 3).reshape(EXPERTS, P, KD * FF)
                    for n in ("moe_w_gate", "moe_w_up"))
        down = i["moe_w_down"][l].reshape(EXPERTS, 2, P, D).transpose(0, 2, 1, 3).reshape(EXPERTS, P, 2 * D)
        experts.append(np.concatenate([gate, up, down], axis=2))
    uq = i["mla_w_uq"][0].reshape(3, P, AH, NOPE + ROPE).transpose(1, 0, 2, 3)
    lat, kr = i["cache_mla_latent"][0], i["cache_mla_krope"][0]
    latT = lat.transpose(0, 2, 1).reshape(-1, 2, P, PAGE).transpose(0, 2, 1, 3).reshape(-1, P, 2 * PAGE)
    out = {
        "xT": by_k(x[:TOK].T),
        "x": x.reshape(NT, P, D).transpose(1, 0, 2),
        "w_in": w_in[:, :INNER + XBCB * P].reshape(KD, P, 10, 512).transpose(2, 1, 0, 3).reshape(10, P, KD * 512),
        "w_dt": by_k(w_in[:, INNER + XBCB * P:]),
        "cols": np.concatenate([cw, cb, nw, dk], axis=1),
        "conv": conv,
        "rows": np.broadcast_to(rows, (P, 2, HEADS)),
        "w_out": by_k(i["ssd_w_out"][0]).reshape(P, 4, 4 * D).transpose(1, 0, 2),
        "state": i["state_ssd"][0].reshape(DEC_B, INNER, STATE).transpose(0, 2, 1),
        "ln": np.broadcast_to(ln[:, None], (4, P, 2, D)),
        "router": np.stack([by_k(i["moe_router"][l]) for l in range(2)]),
        "rbias": np.broadcast_to(i["moe_router_bias"][:, None], (2, P, EXPERTS)),
        "experts": np.concatenate(experts),
        "const": constants(),
        "w_dqkv": by_k(i["mla_w_dqkv"][0]),
        "w_uq": np.concatenate([uq[..., :NOPE].reshape(P, 3, AH * NOPE), uq[..., NOPE:].reshape(P, 3, AH * ROPE)], axis=2),
        "w_ukT": i["mla_w_uk"][0].transpose(2, 1, 0),
        "w_uv": by_k(i["mla_w_uv"][0].reshape(KL, AH * VH)),
        "w_o": by_k(i["mla_w_o"][0]),
        "qkn": np.broadcast_to(np.concatenate([i["mla_q_norm"][0], i["mla_kv_norm"][0]]), (P, QL + KL)),
        "latent": np.concatenate([lat, latT], axis=2),
        "krope": kr.transpose(0, 2, 1),
        "pages": i["page_table"].reshape(1, DEC_B * PAGES),
    }
    return {k: np.ascontiguousarray(v) for k, v in out.items()}


_OUTS = {
    "y": (P, NT, D), "lat": (P, NT, KL), "kr": (P, NT, ROPE), "ssdp": (P, INNER),
    "conv": (P, XBCB, CONVO), "ssds": (DEC_B, P, INNER),
}


def kernel(**inputs):
    import concourse.bacc as bacc
    from concourse.bass_utils import run_bass_kernel_spmd

    arrays = _lay_out({k: np.asarray(v) for k, v in inputs.items()})
    nc = bacc.Bacc("TRN2", target_bir_lowering=False, num_devices=1)
    a = {k: nc.dram_tensor(f"in_{k}", v.shape, mybir.dt.from_np(v.dtype), kind="ExternalInput").ap()
         for k, v in arrays.items()}
    o = {k: nc.dram_tensor(f"out_{k}", s, F32, kind="ExternalOutput").ap() for k, s in _OUTS.items()}
    program(nc, a, o)
    r = run_bass_kernel_spmd(nc, [{f"in_{k}": v for k, v in arrays.items()}], core_ids=[0]).results[0]
    r = {k: r[f"out_{k}"] for k in _OUTS}

    def tokens(v):
        rows = v.transpose(1, 0, 2).reshape(NT * P, -1)
        return rows[:SEQ], rows[SEQ:TOK].reshape(DEC_B, DEC_T, -1)

    yp, ysm = tokens(r["y"])
    lp, lsm = tokens(r["lat"])
    kp, ksm = tokens(r["kr"])
    conv = r["conv"].transpose(2, 1, 0).reshape(CONVO, XBCB * P)
    state = (HEADS, HP, STATE)
    return (yp[None], ysm, lp[None, None], kp[None, None], r["ssdp"].T.reshape(1, 1, *state),
            conv[None, None, :3], lsm[None], ksm[None],
            r["ssds"].transpose(0, 2, 1).reshape(1, DEC_B, *state), conv[3:].reshape(1, DEC_B, 3, XBCB * P))
```

```python
from contextlib import ExitStack

import numpy as np

import concourse.bass as bass
from concourse import mybir

F32 = mybir.dt.float32
I32 = mybir.dt.int32
ALU = mybir.AluOpType
ACT = mybir.ActivationFunctionType
X_AXIS = mybir.AxisListType.X
ds = bass.ds

P = 128
D = 1024
KD = D // P
SEQ, DEC_B, DEC_T = 256, 8, 8
NT = 3
ROWS = [P, P, DEC_B * DEC_T]
OFF = [0, P, 2 * P]
TOK = SEQ + DEC_B * DEC_T
SAMPLE = slice(SEQ, TOK)
PAST, PAGE = 1024, 128
PAGES = PAST // PAGE

INNER = 2048
HEADS, HP, STATE, GROUPS = 32, 64, 128, 4
HG = HEADS // GROUPS
ZB = INNER // P
XBCB = 24
CONVO = 3 + 3 * DEC_B
RMS_EPS, LN_EPS = 1e-6, 1e-5

AH, QL, KL, NOPE, ROPE, VH = 8, 384, 256, 128, 64, 128
DQKV = QL + KL + ROPE
ATT_SCALE = float(NOPE + ROPE) ** -0.5
ALPHA = 4.0 ** 0.25

EXPERTS, MGROUPS, EG, FF = 32, 4, 8, 256
SLOTS = 64
NSLOT = EXPERTS * SLOTS
WEXP = 2 * KD * FF + 2 * D
MAX_WINDOWS = TOK // SLOTS
PHASE_SEMS = 48
NEG = -1e30

_WIDTHS = [("ident", P), ("tri", P), ("strict", P), ("ones", P), ("tri_s", 64), ("same_s", 64),
           ("bmask", DEC_B), ("desc4", MGROUPS), ("desc32", EXPERTS), ("ebase", EXPERTS),
           ("valid", NT), ("causal", 2 * P), ("smask", DEC_B * 64), ("eps", 2), ("cos", NT * 32), ("sin", NT * 32)]
CONST = {}
_at = 0
for _name, _w in _WIDTHS:
    CONST[_name] = slice(_at, _at + _w)
    _at += _w
CONST_W = _at


def constants():
    c = np.zeros((P, CONST_W), np.float32)
    i = np.arange(P)
    s = np.arange(64)
    c[:, CONST["ident"]] = np.eye(P)
    c[:, CONST["tri"]] = i[:, None] <= i[None, :]
    c[:, CONST["strict"]] = i[:, None] < i[None, :]
    c[:, CONST["ones"]] = 1.0
    same = s[:, None] // DEC_T == s[None, :] // DEC_T
    c[:64, CONST["tri_s"]] = same & (s[:, None] <= s[None, :])
    c[:64, CONST["same_s"]] = same
    c[:64, CONST["bmask"]] = s[:, None] // DEC_T == np.arange(DEC_B)[None, :]
    c[:, CONST["desc4"]] = np.arange(MGROUPS, 0, -1)
    c[:, CONST["desc32"]] = np.arange(EXPERTS, 0, -1)
    c[:, CONST["ebase"]] = np.arange(EXPERTS) * SLOTS
    for t in range(NT):
        c[:ROWS[t], CONST["valid"].start + t] = 1.0
    c[:, CONST["causal"].start + P:CONST["causal"].stop] = np.where(i[None, :] <= i[:, None], 0.0, NEG)
    key_b, key_j = s // DEC_T, s % DEC_T
    t_of = s // AH
    ok = (key_b[None, None, :] == np.arange(DEC_B)[None, :, None]) & (key_j[None, None, :] <= t_of[:, None, None])
    c[:64, CONST["smask"]] = np.where(ok, 0.0, NEG).reshape(64, -1)
    c[:, CONST["eps"]] = [LN_EPS, RMS_EPS]
    half = ROPE // 2
    inv = 10000.0 ** (-np.arange(half, dtype=np.float32) / half)
    pos = np.zeros((NT, P), np.float32)
    pos[0], pos[1], pos[2, :64] = i, P + i, PAST + s % DEC_T
    ang = (pos[:, :, None] * inv.astype(np.float32)).transpose(1, 0, 2)
    c[:, CONST["cos"]] = np.cos(ang).reshape(P, -1)
    c[:, CONST["sin"]] = np.sin(ang).reshape(P, -1)
    return c


class Tally:

    def __init__(self, sem):
        self.sem, self.base, self.n = sem, 0, 0

    def mark(self, ins):
        ins.then_inc(self.sem, 1)
        self.n += 1

    def settle(self, eng):
        eng.wait_ge(self.sem, self.base + self.n)

    def loop(self, base):
        self.base, self.n = base, 0


def credit(eng, *sems, by=1):
    for s in sems:
        eng.sem_inc(s, by)


def program(nc, a, o):
    ctx = ExitStack()
    with ctx:
        def sem(name):
            return ctx.enter_context(nc.semaphore(name))

        def sems(name, n):
            return [sem(f"{name}{i}") for i in range(n)]

        free = sorted(nc.free_semaphores)[-2 * PHASE_SEMS:]
        POOLS, turn = (free[:PHASE_SEMS], free[PHASE_SEMS:]), [0]

        def phase_semaphores(stack, tag=""):
            made = []
            stack.callback(nc.clear_and_free_semaphores, made)
            turn[0] ^= 1
            numbers = iter(POOLS[turn[0]])

            def make(name):
                names[name + tag] = names.get(name + tag, 0) + 1
                made.append(nc.alloc_semaphore(f"{name}{tag}_{names[name + tag]}", num=next(numbers)))
                return made[-1]

            return make

        names = {}

        def buf(stack, name, shape, dt=F32):
            names[name] = names.get(name, 0) + 1
            unique = name if names[name] == 1 else f"{name}_{names[name]}"
            return stack.enter_context(nc.sbuf_tensor(unique, shape, dt))

        ring = buf(ctx, "ring", [P, 4, WEXP])
        X = buf(ctx, "X", [P, NT, D])
        XT = buf(ctx, "XT", [P, KD, TOK])
        C = buf(ctx, "C", [P, CONST_W])
        lnp = buf(ctx, "lnp", [P, 2, D])
        ps = ctx.enter_context(nc.psum_tensor("ps", [P, 8, 512], F32))
        xs_dram = nc.dram_tensor("xs_dram", (NSLOT, D), F32).ap()
        ys_dram = nc.dram_tensor("ys_dram", (NSLOT, D), F32).ap()

        def const(name, rows=P):
            return C[0:rows, CONST[name]]

        def const3(name):
            return C[:, CONST[name]].rearrange("p (t i) -> p t i", t=NT)

        ident = const("ident")
        eps = const("eps")
        const_in, x_in, ln_in, cols_in, rows_in, conv_in, wdt_in = map(
            sem, ["const_in", "x_in", "ln_in", "cols_in", "rows_in", "conv_in", "wdt_in"])
        wout_in = sems("wout_in", 4)
        zero_made, zero_out = sem("zero_made"), sem("zero_out")
        state_in = sems("state_in", 4)
        key_in, wo_in = sems("key_in", 3), sem("wo_in")
        router_in = sem("router_in")
        expert_in = [sems(f"expert_in{layer}_", 4) for layer in range(2)]
        router = buf(ctx, "router", [P, KD, EXPERTS])
        rbias = buf(ctx, "rbias", [P, EXPERTS])

        def load_router(sp, layer):
            sp.dma_start(router[:, :, :], a["router"][layer]).then_inc(router_in, 16)
            sp.dma_start(rbias[:, :], a["rbias"][layer]).then_inc(router_in, 16)

        def first_expert(sp, layer, i):
            sp.dma_start(ring[:, i, :], a["experts"][layer * EXPERTS + i]).then_inc(expert_in[layer][i], 16)

        ssd = ExitStack()
        zT = buf(ssd, "zT", [P, ZB, TOK])
        xbcT = buf(ssd, "xbcT", [P, XBCB, TOK])
        cols = buf(ssd, "cols", [P, 152])
        dt = buf(ssd, "dt", [P, NT, HEADS])
        dtA = buf(ssd, "dtA", [P, NT, HEADS])
        convw, convb = cols[:, 0:96], cols[:, 96:120]
        normw, dskip = cols[:, 120:136], cols[:, 136:152]

        def in_projection():
            with ExitStack() as st:
                xpad = buf(st, "xpad", [P, 2, 3 + SEQ])
                spad = buf(st, "spad", [P, 2, DEC_B, 3 + DEC_T])
                conv = buf(st, "conv", [P, 2, TOK])
                cst = buf(st, "cst", [P, XBCB, DEC_B, 3])
                cvo = buf(st, "cvo", [P, XBCB, CONVO])
                wdt = buf(st, "wdt", [P, KD, HEADS])
                rows = buf(st, "rows", [P, 2, HEADS])
                nega = buf(st, "nega", [P, HEADS])
                soft = ring[:, 3, 4 * D:4 * D + 3 * NT * HEADS].rearrange("p (a h) -> p a h", a=3)
                zero = ring[:, 3, 0:D]

                s = phase_semaphores(st)

                chunk_in = [s("chunk_in0"), s("chunk_in1")]
                proj_done, dt_done, conv_done, cvo_out = map(s, ["proj_done", "dt_done", "conv_done", "cvo_out"])
                kept = [s("kept0"), s("kept1")]
                freed = [s(f"freed{q}") for q in range(4)]
                silu_done = [s("silu_done0"), s("silu_done1")]
                dve, soft_in, soft_out = map(s, ["dve_a", "soft_in", "soft_out"])
                block = st.enter_context(nc.Block())

                @block.sync
                def _(sp):
                    sp.dma_start(XT[:, :, :], a["xT"]).then_inc(x_in, 16)
                    for u in range(2):
                        sp.dma_start(ring[:, u, 0:KD * 512], a["w_in"][u]).then_inc(chunk_in[u], 16)
                    sp.dma_start(C[:, :], a["const"]).then_inc(const_in, 16)
                    sp.dma_start(cols[:, :], a["cols"]).then_inc(cols_in, 16)
                    sp.dma_start(cst[:, :, :, :], a["conv"]).then_inc(conv_in, 16)
                    sp.dma_start(wdt[:, :, :], a["w_dt"]).then_inc(wdt_in, 16)
                    sp.dma_start(rows[:, :, :], a["rows"]).then_inc(rows_in, 16)
                    with sp.Fori(0, 4) as it:
                        for u in range(2):
                            src = a["w_in"][ds(sp.snap(2 * it + 2 + u), 1)].rearrange("c p n -> (c p) n")
                            sp.wait_ge(proj_done, 8 * it + 4 * u + 4)
                            sp.dma_start(ring[:, u, 0:KD * 512], src).then_inc(chunk_in[u], 16)
                    for i in (2, 3):
                        if i == 3:
                            sp.wait_ge(zero_out, 16 * (NSLOT // P))
                        sp.dma_start(ring[:, i, 0:4 * D], a["w_out"][i]).then_inc(wout_in[i], 16)
                    for i in range(2):
                        sp.wait_ge(proj_done, 40)
                        sp.dma_start(ring[:, i, 0:4 * D], a["w_out"][i]).then_inc(wout_in[i], 16)
                    for b in range(2):
                        sp.wait_ge(kept[b], XBCB + 1)
                    sp.dma_start(o["conv"], cvo[:, :, :]).then_inc(cvo_out, 16)
                    sp.wait_ge(cvo_out, 16)

                @block.tensor
                def _(pe):
                    pe.wait_ge(x_in, 16)
                    with pe.Fori(0, 5) as it:
                        for u in range(2):
                            pe.wait_ge(chunk_in[u], 16 * (it + 1))
                            for q in range(4):
                                pe.wait_ge(freed[q], 2 * it + u + 1)
                                for k in range(KD):
                                    mm = pe.matmul(ps[:, q, 0:TOK],
                                                   ring[:, u, k * 512 + q * P:k * 512 + (q + 1) * P],
                                                   XT[:, k, :], start=(k == 0), stop=(k == KD - 1))
                                mm.then_inc(proj_done, 1)
                    pe.wait_ge(wdt_in, 16)
                    for t in range(NT):
                        r = ROWS[t]
                        for k in range(KD):
                            mm = pe.matmul(ps[0:r, 4, t * HEADS:(t + 1) * HEADS], XT[:, k, OFF[t]:OFF[t] + r],
                                           wdt[:, k, :], start=(k == 0), stop=(k == KD - 1))
                    mm.then_inc(dt_done, 1)

                @block.scalar
                def _(act):
                    credit(act, *freed, *silu_done)
                    with act.Fori(0, 2) as it:
                        for u in range(2):
                            for q in range(4):
                                blk = 8 * it + 4 * u + q
                                act.wait_ge(proj_done, blk + 1)
                                act.activation(zT[:, ds(blk, 1), :].rearrange("p a t -> p (a t)"),
                                               ps[:, q, 0:TOK], ACT.Silu).then_inc(freed[q], 1)
                    with act.Fori(0, 3) as it:
                        for u in range(2):
                            for q in range(4):
                                blk = 8 * it + 4 * u + q
                                act.wait_ge(conv_done, blk + 1)
                                act.activation(xbcT[:, ds(blk, 1), :].rearrange("p a t -> p (a t)"),
                                               conv[:, q % 2, :], ACT.Silu).then_inc(silu_done[q % 2], 1)
                    act.wait_ge(soft_in, 1)
                    act.activation(soft[:, 1, :], soft[:, 1, :], ACT.Exp).then_inc(soft_out, 1)
                    act.wait_ge(rows_in, 16)
                    act.activation(nega[:, :], rows[:, 1, :], ACT.Exp)
                    act.wait_ge(soft_out, 1)
                    act.activation(soft[:, 1, :], soft[:, 1, :], ACT.Ln, bias=1.0).then_inc(soft_out, 1)

                @block.gpsimd
                def _(pool):
                    credit(pool, *kept)
                    pool.memset(zero, 0.0).then_inc(zero_made, 1)
                    pool.wait_ge(zero_made, 1)
                    for i in range(NSLOT // P):
                        pool.dma_start(xs_dram[i * P:(i + 1) * P, :], zero).then_inc(zero_out, 16)
                    with pool.Fori(0, 12) as it:
                        for v in range(2):
                            blk = 2 * it + v
                            pool.wait_ge(conv_done, blk + 1)
                            pool.tensor_copy(cvo[:, ds(blk, 1), 0:3].rearrange("p a t -> p (a t)"),
                                             xpad[:, v, SEQ:SEQ + 3]).then_inc(kept[v], 1)
                            pool.tensor_copy(
                                cvo[:, ds(blk, 1), 3:CONVO].rearrange("p a (b t) -> p (a b) t", b=DEC_B),
                                spad[:, v, :, DEC_T:DEC_T + 3]).then_inc(kept[v], 1)

                @block.vector
                def _(v):
                    step = Tally(dve)
                    step.mark(v.memset(xpad[:, :, 0:3], 0.0))
                    step.mark(v.memset(soft[:, 0, :], 0.0))
                    v.wait_ge(conv_in, 16)
                    v.wait_ge(cols_in, 16)
                    start = step.n
                    with v.Fori(0, 3) as it:
                        for u in range(2):
                            for q in range(4):
                                b = q % 2
                                m = 4 * u + q
                                blk = 8 * it + m
                                step.loop(start + blk * 3)
                                xo, so = conv[:, b, 0:SEQ], conv[:, b, SEQ:TOK].rearrange("p (b t) -> p b t", b=DEC_B)
                                v.wait_ge(kept[b], 2 * (4 * it + m // 2) + 1)
                                v.wait_ge(proj_done, 16 + blk + 1)
                                v.tensor_copy(xpad[:, b, 3:3 + SEQ], ps[:, q, 0:SEQ])
                                v.tensor_copy(spad[:, b, :, 0:3], cst[:, ds(blk, 1), :, :].rearrange("p a b t -> p (a b) t"))
                                cp = v.tensor_copy(spad[:, b, :, 3:3 + DEC_T],
                                                   ps[:, q, SEQ:TOK].rearrange("p (b t) -> p b t", b=DEC_B))
                                cp.then_inc(freed[q], 1)
                                v.wait_ge(freed[q], 4 + 2 * it + u + 2)
                                v.wait_ge(silu_done[b], 4 * it + 2 * u + q // 2 + 1)
                                for k in range(4):
                                    w = convw[:, ds(4 * blk + k, 1)]
                                    xi, si = xpad[:, b, k:k + SEQ], spad[:, b, :, k:k + DEC_T]
                                    if k == 0:
                                        bias = convb[:, ds(blk, 1)]
                                        v.tensor_scalar(xo, xi, w, bias, ALU.mult, ALU.add)
                                        ins = v.tensor_scalar(so, si, w, bias, ALU.mult, ALU.add)
                                    else:
                                        v.scalar_tensor_tensor(out=xo, in0=xi, scalar=w, in1=xo, op0=ALU.mult, op1=ALU.add)
                                        ins = v.scalar_tensor_tensor(out=so, in0=si, scalar=w, in1=so,
                                                                     op0=ALU.mult, op1=ALU.add)
                                    if k < 3:
                                        step.mark(ins)
                                        step.settle(v)
                                    else:
                                        ins.then_inc(conv_done, 1)
                    step.loop(start + XBCB * 3)
                    v.wait_ge(dt_done, 1)
                    v.wait_ge(rows_in, 16)
                    v.tensor_copy(soft[:, 0, 0:64], ps[:, 4, 0:64])
                    step.mark(v.tensor_copy(soft[0:64, 0, 64:96], ps[0:64, 4, 64:96]))
                    step.settle(v)
                    raw = soft[:, 0, :].rearrange("p (t h) -> p t h", t=NT)
                    bias = rows[:, 0, :].unsqueeze(1).to_broadcast([P, NT, HEADS])
                    step.mark(v.tensor_tensor(raw, raw, bias, ALU.add))
                    step.settle(v)
                    v.scalar_tensor_tensor(out=soft[:, 1, :], in0=soft[:, 0, :], scalar=-1.0, in1=soft[:, 0, :],
                                           op0=ALU.mult, op1=ALU.min).then_inc(soft_in, 1)
                    v.wait_ge(soft_out, 2)
                    dtf = dt[:, :, :].rearrange("p t h -> p (t h)")
                    step.mark(v.scalar_tensor_tensor(out=dtf, in0=soft[:, 0, :], scalar=0.0, in1=soft[:, 1, :],
                                                     op0=ALU.max, op1=ALU.add))
                    step.settle(v)
                    v.scalar_tensor_tensor(out=dtA[:, :, :], in0=dt[:, :, :], scalar=-1.0,
                                           in1=nega[:, :].unsqueeze(1).to_broadcast([P, NT, HEADS]),
                                           op0=ALU.mult, op1=ALU.mult)

        h1 = buf(ssd, "h1", [P, INNER])
        Bt = buf(ssd, "Bt", [P, GROUPS * STATE])
        decS = buf(ssd, "decS", [P, DEC_B, HEADS])
        xdt = ring[:, 0, 4 * D:6 * D]
        xdtw = ring[:, 1, 4 * D:6 * D]
        h0 = [ring[:, 2, 4 * D:6 * D], ring[:, 3, 4 * D:6 * D],
              XT[:, :, :].rearrange("p k t -> p (k t)")[:, 0:INNER], X[:, :, :].rearrange("p t d -> p (t d)")[:, 0:INNER]]

        def load_rows(sp):
            sp.dma_start(X[:, :, :], a["x"]).then_inc(x_in, 16)
            sp.dma_start(lnp[:, :, :], a["ln"][0]).then_inc(ln_in, 16)


        def scan_chunk(c):
            r = ROWS[c]
            carried = c == 1
            mask = const("tri_s", 64) if c == 2 else const("tri")
            same = const("same_s", 64) if c == 2 else const("ones")
            TR, BC, CB, Y, M = (0, 1), (2, 3), 4, (5, 6), 7
            UNITS = 2 * GROUPS

            def by_channel(blk):
                return xbcT[:, blk, OFF[c]:OFF[c] + r]

            with ExitStack() as st:
                s = phase_semaphores(st, f"_c{c}")

                cums = buf(st, "cums", [P, HEADS])
                wS = buf(st, "wS", [P, HEADS])
                dec = buf(st, "dec", [P, HEADS])
                cbm = buf(st, "cbm", [P, 2, P])
                ec = buf(st, "ec", [P, 2, 4, P])
                seg = buf(st, "seg", [P, 2, 4, P])
                tmp = buf(st, "tmp", [P, 2, 2, P])
                (turned, xdt_done, bt_done, cum_done, cums_done, w_in, w_done, xw_done, bc_done, cb_done,
                 cbm_done, ec_done, seg_in, seg_done, mt_done, ct_done, y_done, tmp_done, gated,
                 h_mm, h1_done, h1_scaled, h2_out, dec_done) = map(s, [
                     "turned", "xdt_done", "bt_done", "cum_done", "cums_done", "w_in", "w_done", "xw_done",
                     "bc_done", "cb_done", "cbm_done", "ec_done", "seg_in", "seg_done", "mt_done", "ct_done",
                     "y_done", "tmp_done", "gated", "h_mm", "h1_done", "h1_scaled", "h2_out", "dec_done"])
                block = st.enter_context(nc.Block())

                if c < 2:
                    @block.sync
                    def _(sp):
                        if c == 1:
                            sp.wait_ge(h1_done, GROUPS)
                            sp.dma_start(o["ssdp"], h1[:, :]).then_inc(h2_out, 16)
                            sp.wait_ge(h2_out, 16)
                        else:
                            for b in range(4):
                                sp.dma_start(h0[b], a["state"][b]).then_inc(state_in[b], 16)

                @block.tensor
                def _(pe):
                    for f in range(5):
                        if f >= 2:
                            pe.wait_ge(xdt_done, f - 1)
                        for j in range(4):
                            tr = pe.transpose(ps[0:r, TR[f % 2], j * P:(j + 1) * P], by_channel(4 * f + j), ident)
                        tr.then_inc(turned, 1)
                    pe.matmul(ps[0:r, M, 0:HEADS], mask[0:r, 0:r], dtA[0:r, c, :], start=True, stop=True)
                    mm = pe.matmul(ps[0:P if c < 2 else r, M, HEADS:2 * HEADS], same[0:r, :], dtA[0:r, c, :],
                                   start=True, stop=True)
                    if c == 2:
                        for b in range(DEC_B):
                            at = CONST["bmask"].start + b
                            mm = pe.matmul(ps[:, M, P + b * HEADS:P + (b + 1) * HEADS],
                                           C[0:64, at:at + 1].to_broadcast([64, P]), dtA[0:64, 2, :],
                                           start=True, stop=True)
                    mm.then_inc(cum_done, 1)

                    def spread(u):
                        g, half = divmod(u, 2)
                        if u >= 2:
                            pe.wait_ge(seg_in, u - 1)
                            if c:
                                pe.wait_ge(ec_done, u - 1)
                        for j in range(4):
                            h = HG * g + 4 * half + j
                            mm = pe.matmul(ps[:, BC[u % 2], j * P:j * P + r],
                                           dtA[0:r, c, h:h + 1].to_broadcast([r, P]), mask[0:r, 0:r],
                                           start=True, stop=True)
                        mm.then_inc(bc_done, 1)
                        if half == 0:
                            if g:
                                pe.wait_ge(cbm_done, g)
                            pe.matmul(ps[0:r, CB, 0:r], by_channel(ZB + g), by_channel(ZB + GROUPS + g),
                                      start=True, stop=True).then_inc(cb_done, 1)

                    def output(u):
                        g, half = divmod(u, 2)
                        pe.wait_ge(mt_done, u + 1)
                        if carried:
                            pe.wait_ge(ct_done, u + 1)
                        if u >= 2:
                            pe.wait_ge(tmp_done, u - 1)
                        for j in range(4):
                            h = HG * g + 4 * half + j
                            at = HP * (j % 2)
                            out = ps[at:at + HP, Y[u % 2], (j // 2) * P:(j // 2) * P + r]
                            mm = pe.matmul(out, xdt[0:r, h * HP:(h + 1) * HP], seg[0:r, u % 2, j, 0:r],
                                           start=True, stop=not carried)
                            if carried:
                                mm = pe.matmul(out, h1[:, h * HP:(h + 1) * HP], ec[:, u % 2, j, 0:r],
                                               start=False, stop=True)
                        mm.then_inc(y_done, 1)

                    pe.wait_ge(xdt_done, 4)
                    for u in range(UNITS):
                        spread(u)
                        if u:
                            output(u - 1)
                    output(UNITS - 1)
                    if c < 2:
                        pe.wait_ge(xw_done, 1)
                        pe.wait_ge(bt_done, 1)
                        pe.wait_ge(seg_in, UNITS)
                        if c:
                            pe.wait_ge(ec_done, UNITS)
                        for g in range(GROUPS):
                            pe.matmul(ps[:, g, :], Bt[:, g * STATE:(g + 1) * STATE], xdtw[:, g * 512:(g + 1) * 512],
                                      start=True, stop=True).then_inc(h_mm, 1)

                @block.vector
                def _(v):
                    for f in range(4):
                        v.wait_ge(turned, f + 1)
                        v.tensor_tensor(
                            xdt[0:r, f * 512:(f + 1) * 512].rearrange("p (h e) -> p h e", e=HP),
                            ps[0:r, TR[f % 2], :].rearrange("p (h e) -> p h e", e=HP),
                            dt[0:r, c, HG * f:HG * (f + 1)].unsqueeze(2).to_broadcast([r, HG, HP]),
                            ALU.mult).then_inc(xdt_done, 1)
                    v.wait_ge(cum_done, 1)
                    v.tensor_copy(cums[0:r, :], ps[0:r, M, 0:HEADS]).then_inc(cums_done, 1)
                    v.wait_ge(cums_done, 1)
                    v.tensor_tensor(wS[0:r, :], ps[0:r, M, HEADS:2 * HEADS], cums[0:r, :],
                                    ALU.subtract).then_inc(w_in, 1)

                    def exponents(u):
                        g, half = divmod(u, 2)
                        v.wait_ge(bc_done, u + 1)
                        if u >= 2:
                            v.wait_ge(y_done, u - 1)
                        for j in range(4):
                            h = HG * g + 4 * half + j
                            ins = v.tensor_scalar(seg[0:r, u % 2, j, 0:r], ps[0:r, BC[u % 2], j * P:j * P + r],
                                                  cums[0:r, h:h + 1], 0.0, ALU.subtract, ALU.min)
                        ins.then_inc(seg_in, 1)
                        if half == 0:
                            v.wait_ge(cb_done, g + 1)
                            v.tensor_tensor(cbm[0:r, g % 2, 0:r], ps[0:r, CB, 0:r], mask[0:r, 0:r],
                                            ALU.mult).then_inc(cbm_done, 1)

                    def weights(u):
                        g = u // 2
                        v.wait_ge(seg_done, u + 1)
                        v.wait_ge(cbm_done, g + 1)
                        w = seg[0:r, u % 2, :, 0:r]
                        v.tensor_tensor(w, w, cbm[0:r, g % 2, 0:r].unsqueeze(1).to_broadcast([r, 4, r]),
                                        ALU.mult).then_inc(mt_done, 1)

                    def skip(u):
                        v.wait_ge(y_done, u + 1)
                        if c < 2 and u >= 2:
                            v.wait_ge(gated, u - 1)
                        for i in range(2):
                            blk = 2 * u + i
                            out = tmp[:, u % 2, i, 0:r] if c < 2 else by_channel(blk)
                            ins = v.scalar_tensor_tensor(out=out, in0=by_channel(blk), scalar=dskip[:, blk:blk + 1],
                                                         in1=ps[:, Y[u % 2], i * P:i * P + r], op0=ALU.mult, op1=ALU.add)
                        ins.then_inc(tmp_done, 1)

                    for u in range(UNITS + 2):
                        if u < UNITS:
                            exponents(u)
                        if 1 <= u <= UNITS:
                            weights(u - 1)
                        if u >= 2:
                            skip(u - 2)
                    if c == 1:
                        v.wait_ge(dec_done, 1)
                        hv = h1[:, :].rearrange("p (h e) -> p h e", e=HP)
                        v.tensor_tensor(hv, hv, dec[:, :].unsqueeze(2).to_broadcast([P, HEADS, HP]),
                                        ALU.mult).then_inc(h1_scaled, 1)
                        v.wait_ge(h1_scaled, 1)
                        for g in range(GROUPS):
                            v.wait_ge(h_mm, g + 1)
                            hg = h1[:, g * 512:(g + 1) * 512]
                            v.tensor_tensor(hg, hg, ps[:, g, :], ALU.add).then_inc(h1_done, 1)

                @block.scalar
                def _(act):
                    act.wait_ge(turned, 5)
                    act.activation(Bt[0:r, :], ps[0:r, TR[0], :], ACT.Copy).then_inc(bt_done, 1)
                    act.wait_ge(w_in, 1)
                    act.activation(wS[0:r, :], wS[0:r, :], ACT.Exp).then_inc(w_done, 1)
                    if c == 1:
                        act.activation(dec[:, :], ps[:, M, HEADS:2 * HEADS], ACT.Exp).then_inc(dec_done, 1)
                    if c == 2:
                        act.activation(decS[:, :, :].rearrange("p b h -> p (b h)"), ps[:, M, P:P + DEC_B * HEADS],
                                       ACT.Exp).then_inc(dec_done, 1)
                    for u in range(UNITS):
                        if c:
                            act.wait_ge(seg_in, u + 1)
                            if u >= 2:
                                act.wait_ge(y_done if c == 1 else ct_done, u - 1)
                            act.activation(ec[:, u % 2, :, 0:r],
                                           ps[:, BC[u % 2], :].rearrange("p (j l) -> p j l", j=4)[:, :, 0:r],
                                           ACT.Exp).then_inc(ec_done, 1)
                        act.wait_ge(seg_in, u + 1)
                        w = seg[0:r, u % 2, :, 0:r]
                        act.activation(w, w, ACT.Exp).then_inc(seg_done, 1)
                    if c == 0:
                        for g in range(GROUPS):
                            act.wait_ge(h_mm, g + 1)
                            act.activation(h1[:, g * 512:(g + 1) * 512], ps[:, g, :], ACT.Copy).then_inc(h1_done, 1)

                @block.gpsimd
                def _(pool):
                    def weigh_inputs():
                        pool.wait_ge(w_done, 1)
                        pool.wait_ge(xdt_done, 4)
                        pool.tensor_tensor(xdtw[0:r, :].rearrange("p (h e) -> p h e", e=HP),
                                           xdt[0:r, :].rearrange("p (h e) -> p h e", e=HP),
                                           wS[0:r, :].unsqueeze(2).to_broadcast([r, HEADS, HP]),
                                           ALU.mult).then_inc(xw_done, 1)

                    def gate(u):
                        z = zT[:, 2 * u:2 * u + 2, OFF[c]:OFF[c] + r]
                        pool.wait_ge(tmp_done, u + 1)
                        pool.tensor_tensor(z, z, tmp[:, u % 2, :, 0:r], ALU.mult).then_inc(gated, 1)

                    for u in range(UNITS + 2):
                        if c and u < UNITS:
                            cu = by_channel(ZB + GROUPS + u // 2).unsqueeze(1).to_broadcast([P, 4, r])
                            src = ec[:, u % 2, :, 0:r]
                            dst = src if c == 1 else h1[:, u * 256:(u + 1) * 256].rearrange("p (j l) -> p j l", j=4)
                            pool.wait_ge(ec_done, u + 1)
                            pool.tensor_tensor(dst, src, cu, ALU.mult).then_inc(ct_done, 1)
                        if c < 2 and u >= 2:
                            gate(u - 2)
                        if u == 3:
                            weigh_inputs()

        def sample_states():
            with ExitStack() as st:
                s = phase_semaphores(st)

                Bm = buf(st, "Bm", [64, 2, GROUPS * STATE])
                ct = buf(st, "ct", [P, 2, HEADS, DEC_T])
                bm_done, ys_mm, ys_done, up_mm, scaled, updated = map(
                    s, ["bm_done", "ys_mm", "ys_done", "up_mm", "scaled", "updated"])
                state_out = [s(f"state_out{i}") for i in range(4)]
                block = st.enter_context(nc.Block())
                cts = h1[:, :].rearrange("p (h l) -> p h l", l=64)
                YB, UP = 4, (0, 1, 2, 3)

                @block.sync
                def _(sp):
                    for n in range(DEC_B):
                        b = n % 4
                        sp.wait_ge(updated, GROUPS * (n + 1) + 1)
                        sp.dma_start(o["ssds"][n], h0[b]).then_inc(state_out[b], 16)
                        if n >= 1 and n + 3 < DEC_B:
                            e = (n - 1) % 4
                            sp.wait_ge(state_out[e], 16)
                            sp.dma_start(h0[e], a["state"][n + 3]).then_inc(state_in[e], 16)
                    for b in range(4):
                        sp.wait_ge(state_out[b], 32)
                    load_rows(sp)

                @block.tensor
                def _(pe):
                    credit(pe, up_mm)
                    with pe.Fori(0, DEC_B // 4) as it:
                        for b in range(4):
                            n = 4 * it + b
                            pe.wait_ge(state_in[b], 16 * (it + 1))
                            pe.wait_ge(ys_done, 2 * n + 1)
                            pe.wait_ge(bm_done, n + 1)
                            for j in range(ZB):
                                mm = pe.matmul(ps[:, YB, j * 16:(j + 1) * 16], h0[b][:, j * P:(j + 1) * P],
                                               ct[:, b % 2, 2 * j:2 * j + 2, :], start=True, stop=True)
                            mm.then_inc(ys_mm, 1)
                            pe.wait_ge(updated, GROUPS * n + 1)
                            for g in range(GROUPS):
                                pe.matmul(ps[:, UP[g], :], Bm[:, b % 2, g * STATE:(g + 1) * STATE],
                                          xdtw[0:64, g * 512:(g + 1) * 512], start=True, stop=True).then_inc(up_mm, 1)

                @block.gpsimd
                def _(pool):
                    with pool.Fori(0, DEC_B // 2) as it:
                        for b in range(2):
                            n = 2 * it + b
                            pool.wait_ge(up_mm, GROUPS * 2 * it + 1)
                            pool.tensor_copy(ct[:, b, :, :], cts[:, :, ds(DEC_T * n, DEC_T)])
                            own = C[0:64, ds(CONST["bmask"].start + n, 1)].to_broadcast([64, GROUPS * STATE])
                            pool.tensor_tensor(Bm[:, b, :], Bt[0:64, :], own, ALU.mult).then_inc(bm_done, 1)

                @block.vector
                def _(v):
                    credit(v, ys_done, updated)
                    with v.Fori(0, DEC_B // 4) as it:
                        for b in range(4):
                            n = 4 * it + b
                            v.wait_ge(ys_mm, n + 1)
                            y = ps[:, YB, 0:ZB * 16].rearrange("p (j e) -> p j e", e=16)
                            for half in range(2):
                                at = HP * half
                                ysm = xbcT[at:at + HP, 0:ZB, ds(SEQ + DEC_T * n, DEC_T)]
                                v.tensor_tensor(ysm, ysm, y[at:at + HP, :, DEC_T * half:DEC_T * (half + 1)],
                                                ALU.add).then_inc(ys_done, 1)
                            hv = h0[b].rearrange("p (h e) -> p h e", e=HP)
                            dv = decS[:, ds(n, 1), :].rearrange("p a h -> p (a h)").unsqueeze(2)
                            v.tensor_tensor(hv, hv, dv.to_broadcast([P, HEADS, HP]), ALU.mult).then_inc(scaled, 1)
                            v.wait_ge(scaled, n + 1)
                            for g in range(GROUPS):
                                v.wait_ge(up_mm, GROUPS * n + g + 2)
                                hg = h0[b][:, g * 512:(g + 1) * 512]
                                v.tensor_tensor(hg, hg, ps[:, UP[g], :], ALU.add).then_inc(updated, 1)

        def out_projection():
            with ExitStack() as st:
                s = phase_semaphores(st)

                sq = buf(st, "sq", [P, 2, 4, TOK])
                rstd = h1[:, 0:2 * TOK].rearrange("p (b t) -> p b t", b=2)
                gate_done, sq_done, ms_done, std_done, rstd_done, scaled = map(
                    s, ["gate_done", "sq_done", "ms_done", "std_done", "rstd_done", "scaled"])
                wout_used = s("wout_used")
                block = st.enter_context(nc.Block())
                ms = [6, 7]

                @block.sync
                def _(sp):
                    load_router(sp, 0)
                    for i in range(4):
                        sp.wait_ge(wout_used, i + 1)
                        first_expert(sp, 0, i)

                @block.vector
                def _(v):
                    z = zT[:, :, SAMPLE]
                    v.tensor_tensor(z, z, xbcT[:, 0:ZB, SAMPLE], ALU.mult).then_inc(gate_done, 1)
                    for g in range(GROUPS):
                        v.wait_ge(std_done, g + 1)
                        rs = rstd[:, g % 2, :]
                        v.reciprocal(rs, rs).then_inc(rstd_done, 1)
                        v.wait_ge(rstd_done, g + 1)
                        for i in range(4):
                            blk = 4 * g + i
                            v.scalar_tensor_tensor(out=zT[:, blk, :], in0=zT[:, blk, :], scalar=normw[:, blk:blk + 1],
                                                   in1=rs, op0=ALU.mult, op1=ALU.mult).then_inc(scaled, 1)

                @block.scalar
                def _(act):
                    act.wait_ge(gate_done, 1)
                    for g in range(GROUPS):
                        if g >= 2:
                            act.wait_ge(ms_done, g - 1)
                        act.activation(sq[:, g % 2, :, :], zT[:, 4 * g:4 * g + 4, :], ACT.Square).then_inc(sq_done, 1)
                    for g in range(GROUPS):
                        act.wait_ge(ms_done, g + 1)
                        if g >= 2:
                            act.wait_ge(scaled, 4 * (g - 1))
                        act.activation(rstd[:, g % 2, :], ps[:, ms[g % 2], 0:TOK], ACT.Sqrt,
                                       bias=eps[:, 1:2], scale=1.0 / (4 * P)).then_inc(std_done, 1)

                @block.tensor
                def _(pe):
                    for g in range(GROUPS):
                        pe.wait_ge(sq_done, g + 1)
                        if g >= 2:
                            pe.wait_ge(std_done, g - 1)
                        for i in range(4):
                            mm = pe.matmul(ps[:, ms[g % 2], 0:TOK], const("ones"), sq[:, g % 2, i, :],
                                           start=(i == 0), stop=(i == 3))
                        mm.then_inc(ms_done, 1)
                    for blk in range(ZB):
                        pe.wait_ge(wout_in[blk // 4], 16)
                        pe.wait_ge(scaled, blk + 1)
                        for t in range(NT):
                            for n in range(2):
                                at = (blk % 4) * D + n * 512
                                mm = pe.matmul(ps[0:ROWS[t], 2 * t + n, :], zT[:, blk, OFF[t]:OFF[t] + ROWS[t]],
                                               ring[:, blk // 4, at:at + 512], start=(blk == 0), stop=(blk == ZB - 1))
                        if blk % 4 == 3:
                            mm.then_inc(wout_used, 1)

        def layer_norm(tag, sub, ln_count):
            with ExitStack() as st:
                s = phase_semaphores(st, f"_{tag}")

                stats = buf(st, "stats", [P, NT, 2, 6])
                mv = buf(st, "mv", [P, NT, 2])
                var_done, std_done, gain_done, norm_done, turned, copied, dve, stored = map(
                    s, ["var_done", "std_done", "gain_done", "norm_done", "turned", "copied", "dve", "stored"])
                block = st.enter_context(nc.Block())
                last = tag == "f1"

                @block.vector
                def _(v):
                    step = Tally(dve)
                    if tag == "a0":
                        v.wait_ge(x_in, 32)
                    for t in range(NT):
                        r = ROWS[t]
                        xt = X[0:r, t, :]
                        step.mark(v.scalar_tensor_tensor(out=xt, in0=xt, scalar=ALPHA, in1=sub(t), op0=ALU.mult, op1=ALU.add))
                        step.settle(v)
                        for n in range(2):
                            ins = v.bn_stats(stats[0:r, t, n, :], X[0:r, t, n * 512:(n + 1) * 512])
                        step.mark(ins)
                        step.settle(v)
                        v.bn_aggr(mv[0:r, t, :], stats[0:r, t, :, :].rearrange("p n s -> p (n s)")).then_inc(var_done, 1)
                    v.wait_ge(ln_in, 16 * ln_count)
                    for t in range(NT):
                        r = ROWS[t]
                        xt = X[0:r, t, :]
                        v.wait_ge(std_done, t + 1)
                        step.mark(v.reciprocal(mv[0:r, t, 1:2], mv[0:r, t, 1:2]))
                        step.settle(v)
                        step.mark(v.tensor_scalar(xt, xt, mv[0:r, t, 0:1], mv[0:r, t, 1:2], ALU.subtract, ALU.mult))
                        step.settle(v)
                        v.tensor_tensor(xt, xt, lnp[0:r, 0, :], ALU.mult).then_inc(gain_done, 1)

                @block.gpsimd
                def _(pool):
                    for t in range(NT):
                        r = ROWS[t]
                        pool.wait_ge(gain_done, t + 1)
                        pool.tensor_tensor(X[0:r, t, :], X[0:r, t, :], lnp[0:r, 1, :], ALU.add).then_inc(norm_done, 1)

                @block.scalar
                def _(act):
                    for t in range(NT):
                        act.wait_ge(var_done, t + 1)
                        r = ROWS[t]
                        act.activation(mv[0:r, t, 1:2], mv[0:r, t, 1:2], ACT.Sqrt, bias=eps[0:r, 0:1]).then_inc(std_done, 1)
                    if not last:
                        for t in range(NT):
                            r = ROWS[t]
                            for half in range(2):
                                act.wait_ge(turned, 2 * t + half + 1)
                                act.activation(XT[:, 4 * half:4 * half + 4, OFF[t]:OFF[t] + r],
                                               ps[:, 6 + half, :].rearrange("p (k s) -> p k s", k=4)[:, :, 0:r],
                                               ACT.Copy).then_inc(copied, 1)

                if not last:
                    @block.tensor
                    def _(pe):
                        for t in range(NT):
                            r = ROWS[t]
                            pe.wait_ge(norm_done, t + 1)
                            for half in range(2):
                                if t:
                                    pe.wait_ge(copied, 2 * t + half - 1)
                                for k in range(4):
                                    at = (4 * half + k) * P
                                    tr = pe.transpose(ps[:, 6 + half, k * P:k * P + r], X[0:r, t, at:at + P],
                                                      ident[0:r, 0:r])
                                tr.then_inc(turned, 1)

                @block.sync
                def _(sp):
                    sp.wait_ge(norm_done, NT)
                    if last:
                        sp.dma_start(o["y"], X[:, :, :]).then_inc(stored, 16)
                        sp.wait_ge(stored, 16)
                    elif tag != "f0":
                        sp.dma_start(lnp[:, :, :], a["ln"][ln_count]).then_inc(ln_in, 16)

        def moe(layer, acc, afterwards=None):
            with ExitStack() as st:
                s = phase_semaphores(st, f"_m{layer}")

                def wide(n, w=EXPERTS, dt_=F32):
                    return buf(st, n, [P, NT, w], dt_)

                aff, sel, eq, pick1, pick2, took, pos = map(
                    wide, ["aff", "sel", "eq", "pick1", "pick2", "took", "pos"])
                top = buf(st, "top", [P, NT, MGROUPS, 8])
                gs, geq = wide("gs", MGROUPS), wide("geq", MGROUPS)
                mx = buf(st, "mx", [P, NT])
                rowb, rowp, wk, rowq, inw, gw = (buf(st, n, [P, 2, NT]) for n in
                                                 ["rowb", "rowp", "wk", "rowq", "inw", "gw"])
                to_slot = buf(st, "to_slot", [P, 2, NT], I32)
                from_slot = buf(st, "from_slot", [P, 2, NT], I32)
                count = buf(st, "count", [P, 1])
                windows = buf(st, "windows", [P, 1], I32)
                woff = buf(st, "woff", [P, 1])
                xs = buf(st, "xs", [P, 2, D])
                xsT = buf(st, "xsT", [P, 2, KD, P])
                sg = buf(st, "sg", [P, 2, 2 * SLOTS])
                hT = buf(st, "hT", [P, 2, 2 * SLOTS])
                ys = buf(st, "ys", [P, 2, D])
                got = buf(st, "got", [P, 2, D])

                (logit_done, logit_copied, aff_done, took_done, pos_done, windows_set, index_set, scattered,
                 turned, xs_act, xs_dve, gu_done, silu_done, h_done, y_act, y_dve, summed, passed, dve) = map(s, [
                     "logit_done", "logit_copied", "aff_done", "took_done", "pos_done", "windows_set",
                     "index_set", "scattered", "turned", "xs_act", "xs_dve", "gu_done", "silu_done", "h_done",
                     "y_act", "y_dve", "summed", "passed", "dve"])
                w_in = expert_in[layer]
                w_used = [s(f"w_used{i}") for i in range(4)]
                xs_in = [s("xs_in0"), s("xs_in1")]
                ys_out = [s("ys_out0"), s("ys_out1")]
                got_in = [s(f"got_in{i}") for i in range(2 * NT)]
                places = [got[:, 0, :], got[:, 1, :], xs[:, 0, :], xs[:, 1, :], ys[:, 0, :], ys[:, 1, :]]
                block = st.enter_context(nc.Block())

                LG = 0
                TP, GU, YB = (0, 1), (2, 3), ((4, 5), (6, 7))
                BODIES = EXPERTS // 4

                def load_windows(eng):
                    eng.wait_ge(windows_set, 1)
                    return eng.value_load(windows[0:1, 0:1], min_val=1, max_val=MAX_WINDOWS)

                @block.sync
                def _(sp):
                    n_windows = load_windows(sp)
                    with sp.Fori(0, n_windows) as w:
                        base = sp.snap(BODIES * w)
                        n_scat = sp.snap(2 * NT * 16 * w + 2 * NT * 16)
                        sp.wait_ge(scattered, n_scat)
                        for p in range(2):
                            sp.dma_start(xs[:, p, :], xs_dram[p * P:(p + 1) * P, :]).then_inc(xs_in[p], 16)
                        with sp.Fori(0, BODIES - 1) as it:
                            for p in range(2):
                                src = xs_dram[ds(sp.snap((2 * it + 2 + p) * P), P), :]
                                n_t = sp.snap(2 * (base + it) + p + 1)
                                sp.wait_ge(turned, n_t)
                                sp.dma_start(xs[:, p, :], src).then_inc(xs_in[p], 16)
                                for e in range(2):
                                    i = 2 * p + e
                                    row = a["experts"][ds(sp.snap(layer * EXPERTS + 4 * it + 4 + i), 1)]
                                    n_u = sp.snap(base + it + 2)
                                    sp.wait_ge(w_used[i], n_u)
                                    sp.dma_start(ring[:, i, :], row.rearrange("e p n -> (e p) n")).then_inc(w_in[i], 16)
                        n_u = sp.snap(base + BODIES + 1)
                        with sp.If(w + 1 < n_windows):
                            for i in range(4):
                                sp.wait_ge(w_used[i], n_u)
                                first_expert(sp, layer, i)
                    if afterwards:
                        n_got = sp.snap(n_windows * 16)
                        for got_one in got_in:
                            sp.wait_ge(got_one, n_got)
                        n_all = sp.snap(n_windows * BODIES + 1)
                        afterwards(sp, lambda i: sp.wait_ge(w_used[i], n_all))

                @block.tensor
                def _(pe):
                    pe.wait_ge(router_in, 32 * (layer + 1))
                    for t in range(NT):
                        r = ROWS[t]
                        for k in range(KD):
                            mm = pe.matmul(ps[0:r, LG, t * EXPERTS:(t + 1) * EXPERTS], XT[:, k, OFF[t]:OFF[t] + r],
                                           router[:, k, :], start=(k == 0), stop=(k == KD - 1))
                    mm.then_inc(logit_done, 1)
                    pe.wait_ge(took_done, 1)
                    for t in range(NT):
                        out = ps[:, 1, t * EXPERTS:(t + 1) * EXPERTS]
                        for e in range(t):
                            pe.matmul(out, const("ones"), took[:, e, :], start=(e == 0), stop=False)
                        pe.matmul(out, const("strict"), took[:, t, :], start=(t == 0), stop=True)
                    for t in range(NT):
                        mm = pe.matmul(ps[:, 1, 128:128 + EXPERTS], const("ones"), took[:, t, :],
                                       start=(t == 0), stop=(t == NT - 1))
                    mm.then_inc(pos_done, 1)
                    def turn(n, p):
                        j = 2 * n + p
                        pe.wait_ge(xs_in[p], 16 * n + 16)
                        pe.wait_ge(xs_act, j + 1)
                        pe.wait_ge(xs_dve, j + 1)
                        for k in range(KD):
                            tr = pe.transpose(ps[:, TP[k // 4], (k % 4) * P:(k % 4 + 1) * P],
                                              xs[:, p, k * P:(k + 1) * P], ident)
                        tr.then_inc(turned, 1)

                    def gate_up(n, p):
                        j = 2 * n + p
                        pe.wait_ge(xs_act, j + 2)
                        pe.wait_ge(xs_dve, j + 2)
                        for e in range(2):
                            i = 2 * p + e
                            pe.wait_ge(w_in[i], 16 * n + 16)
                            pe.wait_ge(h_done, 2 * j + 1)
                            for f in range(4):
                                for k in range(KD):
                                    at = (f // 2) * KD * FF + k * FF + (f % 2) * P
                                    mm = pe.matmul(ps[:, GU[e], f * SLOTS:(f + 1) * SLOTS],
                                                   ring[:, i, at:at + P], xsT[:, p, k, e * SLOTS:(e + 1) * SLOTS],
                                                   start=(k == 0), stop=(k == KD - 1))
                            mm.then_inc(gu_done, 1)

                    def down(n, p):
                        j = 2 * n + p
                        pe.wait_ge(y_act, 2 * n + 1)
                        pe.wait_ge(y_dve, 2 * n + 1)
                        for e in range(2):
                            i = 2 * p + e
                            pe.wait_ge(h_done, 2 * j + e + 2)
                            for m in range(2):
                                for f in range(2):
                                    at = 2 * KD * FF + f * D + m * 512
                                    mm = pe.matmul(ps[e * SLOTS:(e + 1) * SLOTS, YB[p][m], :],
                                                   hT[:, e, f * SLOTS:(f + 1) * SLOTS], ring[:, i, at:at + 512],
                                                   start=(f == 0), stop=(f == 1))
                            mm.then_inc(w_used[i], 1)

                    credit(pe, *w_used)
                    with pe.Fori(0, load_windows(pe)) as w:
                        turn(pe.snap(BODIES * w), 0)

                        def body(n, final=False):
                            gate_up(n, 0)
                            turn(n, 1)
                            down(n, 0)
                            gate_up(n, 1)
                            if not final:
                                turn(pe.snap(n + 1), 0)
                            down(n, 1)

                        with pe.Fori(0, BODIES - 1) as it:
                            body(pe.snap(BODIES * w + it))
                        body(pe.snap(BODIES * w + BODIES - 1), final=True)

                @block.scalar
                def _(act):
                    act.wait_ge(logit_copied, 1)
                    act.activation(aff[:, :, :], aff[:, :, :], ACT.Sigmoid).then_inc(aff_done, 1)

                    def rows_in(n, p):
                        act.wait_ge(turned, 2 * n + p + 1)
                        act.activation(xsT[:, p, 0:4, :], ps[:, TP[0], :].rearrange("p (k s) -> p k s", k=4),
                                       ACT.Copy).then_inc(xs_act, 1)

                    def silu(n, p):
                        j = 2 * n + p
                        for e in range(2):
                            act.wait_ge(gu_done, 2 * j + e + 1)
                            act.wait_ge(h_done, 2 * j + 1)
                            act.activation(sg[:, e, :], ps[:, GU[e], 0:2 * SLOTS], ACT.Silu).then_inc(silu_done, 1)

                    def rows_out(n, at, p):
                        act.wait_ge(w_used[2 * p + 1], n + 2)
                        act.wait_ge(ys_out[p], 16 * n + 16)
                        act.activation(ys[:, p, 0:512], ps[:, YB[p][0], :], ACT.Copy).then_inc(y_act, 1)
                        rows = ys_dram[ds(act.snap((2 * at + p) * P), P), :]
                        n_y = act.snap(2 * n + p + 2)
                        act.wait_ge(y_act, n_y)
                        act.wait_ge(y_dve, n_y)
                        act.dma_start(rows, ys[:, p, :]).then_inc(ys_out[p], 16)

                    credit(act, xs_act, y_act)
                    with act.Fori(0, load_windows(act)) as w:
                        rows_in(act.snap(BODIES * w), 0)

                        def body(n, at, final=False):
                            silu(n, 0)
                            rows_in(n, 1)
                            rows_out(n, at, 0)
                            silu(n, 1)
                            if not final:
                                rows_in(act.snap(n + 1), 0)
                            rows_out(n, at, 1)

                        with act.Fori(0, BODIES - 1) as it:
                            body(act.snap(BODIES * w + it), it)
                        body(act.snap(BODIES * w + BODIES - 1), BODIES - 1, final=True)

                @block.gpsimd
                def _(pool):
                    credit(pool, *ys_out, by=16)
                    last_row = pool.to_reg(NSLOT - 1)
                    with pool.Fori(0, load_windows(pool)) as w:
                        pool.wait_ge(index_set, w + 1)
                        pool.sem_inc(passed, 1)
                        for k in range(2):
                            for t in range(NT):
                                r = ROWS[t]
                                pool.indirect_dma_start(
                                    out=xs_dram, out_offset=bass.IndirectOffsetOnAxis(ap=to_slot[0:r, k, t:t + 1], axis=0),
                                    in_=X[0:r, t, :], in_offset=None, bounds_check=last_row,
                                    oob_is_err=False).then_inc(scattered, 16)
                        for p in range(2):
                            pool.wait_ge(ys_out[p], 16 * BODIES * (w + 1) + 16)
                        pool.sem_inc(passed, 1)
                        for k in range(2):
                            for t in range(NT):
                                r = ROWS[t]
                                pool.indirect_dma_start(
                                    out=places[k * NT + t][0:r, :], out_offset=None, in_=ys_dram,
                                    in_offset=bass.IndirectOffsetOnAxis(ap=from_slot[0:r, k, t:t + 1], axis=0),
                                    bounds_check=last_row, oob_is_err=True).then_inc(got_in[k * NT + t], 16)

                @block.vector
                def _(v):
                    step = Tally(dve)

                    def do(ins):
                        step.mark(ins)
                        step.settle(v)

                    def tt(out, x, y, op):
                        do(v.tensor_tensor(out, x, y, op))

                    def spread(x, w):
                        return x.unsqueeze(2).to_broadcast([P, NT, w])

                    v.memset(acc[:, :, :], 0.0)
                    do(v.memset(aff[:, :, :], 0.0))
                    v.wait_ge(logit_done, 1)
                    v.tensor_copy(aff[:, 0:2, :], ps[:, LG, 0:64].rearrange("p (t e) -> p t e", t=2))
                    v.tensor_copy(aff[0:64, 2, :], ps[0:64, LG, 64:96]).then_inc(logit_copied, 1)
                    v.wait_ge(aff_done, 1)
                    v.wait_ge(router_in, 32 * (layer + 1))
                    tt(sel[:, :, :], aff[:, :, :], rbias[:, :].unsqueeze(1).to_broadcast([P, NT, EXPERTS]), ALU.add)
                    for t in range(NT):
                        for g in range(MGROUPS):
                            ins = v.max(top[:, t, g, :], sel[:, t, g * EG:(g + 1) * EG])
                    do(ins)
                    tt(gs[:, :, :], top[:, :, :, 0], top[:, :, :, 1], ALU.add)

                    def first_best(out, values, desc, w):
                        do(v.tensor_reduce(mx[:, :], values, X_AXIS, ALU.max))
                        tt(out, values, spread(mx[:, :], w), ALU.is_ge)
                        tt(out, out, desc.unsqueeze(1).to_broadcast([P, NT, w]), ALU.mult)
                        do(v.tensor_reduce(mx[:, :], out, X_AXIS, ALU.max))
                        tt(out, out, spread(mx[:, :], w), ALU.is_ge)

                    first_best(geq[:, :, :], gs[:, :, :], const("desc4"), MGROUPS)
                    do(v.tensor_scalar(geq[:, :, :], geq[:, :, :], -1.0, -NEG, ALU.add, ALU.mult))
                    sel4 = sel[:, :, :].rearrange("p t (g e) -> p (t g) e", e=EG)
                    g4 = geq[:, :, :].rearrange("p t g -> p (t g)").unsqueeze(2).to_broadcast([P, NT * MGROUPS, EG])
                    tt(sel4, sel4, g4, ALU.add)
                    first_best(pick1[:, :, :], sel[:, :, :], const("desc32"), EXPERTS)
                    do(v.scalar_tensor_tensor(out=sel[:, :, :], in0=pick1[:, :, :], scalar=10 * NEG, in1=sel[:, :, :],
                                              op0=ALU.mult, op1=ALU.add))
                    first_best(pick2[:, :, :], sel[:, :, :], const("desc32"), EXPERTS)
                    tt(took[:, :, :], pick1[:, :, :], pick2[:, :, :], ALU.add)
                    v.tensor_tensor(took[:, :, :], took[:, :, :], spread(const("valid"), EXPERTS),
                                    ALU.mult).then_inc(took_done, 1)
                    picks = [pick1, pick2]

                    def picked(out, table):
                        for k in range(2):
                            tt(eq[:, :, :], picks[k][:, :, :], table, ALU.mult)
                            do(v.tensor_reduce(out[:, k, :], eq[:, :, :], X_AXIS, ALU.add))

                    picked(wk, aff[:, :, :])
                    tt(mx[:, :], wk[:, 0, :], wk[:, 1, :], ALU.add)
                    do(v.reciprocal(mx[:, :], mx[:, :]))
                    tt(wk[:, :, :], wk[:, :, :], mx[:, :].unsqueeze(1).to_broadcast([P, 2, NT]), ALU.mult)
                    picked(rowb, const("ebase").unsqueeze(1).to_broadcast([P, NT, EXPERTS]))
                    v.wait_ge(pos_done, 1)
                    do(v.tensor_copy(pos[:, :, :], ps[:, 1, 0:NT * EXPERTS].rearrange("p (t e) -> p t e", t=NT)))
                    do(v.tensor_reduce(count[:, :], ps[:, 1, 128:128 + EXPERTS], X_AXIS, ALU.max))
                    v.tensor_scalar(windows[:, :], count[:, :], 1.0 / SLOTS, 0.5 - 0.5 / SLOTS,
                                    ALU.mult, ALU.add).then_inc(windows_set, 1)
                    picked(rowp, pos[:, :, :])
                    do(v.memset(woff[:, :], 0.0))
                    credit(v, xs_dve, y_dve, h_done, summed)
                    total = step.n
                    PER_WINDOW = 9
                    with v.Fori(0, load_windows(v)) as w:
                        step.loop(v.snap(w * PER_WINDOW + total))
                        do(v.tensor_scalar(rowq[:, :, :], rowp[:, :, :], woff[:, 0:1], None, ALU.subtract))
                        do(v.tensor_scalar(inw[:, :, :], rowq[:, :, :], 0.0, None, ALU.is_ge))
                        do(v.scalar_tensor_tensor(out=inw[:, :, :], in0=rowq[:, :, :], scalar=float(SLOTS),
                                                  in1=inw[:, :, :], op0=ALU.is_lt, op1=ALU.mult))
                        tt(inw[:, :, :], inw[:, :, :], const("valid").unsqueeze(1).to_broadcast([P, 2, NT]), ALU.mult)
                        tt(rowq[:, :, :], rowq[:, :, :], rowb[:, :, :], ALU.add)
                        tt(gw[:, :, :], wk[:, :, :], inw[:, :, :], ALU.mult)
                        tt(from_slot[:, :, :], rowq[:, :, :], inw[:, :, :], ALU.mult)
                        do(v.scalar_tensor_tensor(out=rowq[:, :, :], in0=rowq[:, :, :], scalar=-2.0 * NSLOT,
                                                  in1=inw[:, :, :], op0=ALU.add, op1=ALU.mult))
                        do(v.tensor_scalar(woff[:, :], woff[:, :], float(SLOTS), None, ALU.add))
                        v.tensor_scalar(to_slot[:, :, :], rowq[:, :, :], 2.0 * NSLOT, None,
                                        ALU.add).then_inc(index_set, 1)
                        def rows_in(n, p):
                            v.wait_ge(turned, 2 * n + p + 1)
                            v.tensor_copy(xsT[:, p, 4:8, :],
                                          ps[:, TP[1], :].rearrange("p (k s) -> p k s", k=4)).then_inc(xs_dve, 1)

                        def hidden(n, p):
                            j = 2 * n + p
                            for e in range(2):
                                v.wait_ge(silu_done, 2 * j + e + 1)
                                if p:
                                    v.wait_ge(w_used[e], n + 2)
                                else:
                                    v.wait_ge(w_used[2 + e], n + 1)
                                v.tensor_tensor(hT[:, e, :], sg[:, e, :], ps[:, GU[e], 2 * SLOTS:4 * SLOTS],
                                                ALU.mult).then_inc(h_done, 1)

                        def rows_out(n, p):
                            v.wait_ge(w_used[2 * p + 1], n + 2)
                            v.wait_ge(ys_out[p], 16 * n + 16)
                            v.tensor_copy(ys[:, p, 512:D], ps[:, YB[p][1], :]).then_inc(y_dve, 1)

                        def body(n, final=False):
                            hidden(n, 0)
                            rows_in(n, 1)
                            rows_out(n, 0)
                            hidden(n, 1)
                            if not final:
                                rows_in(v.snap(n + 1), 0)
                            rows_out(n, 1)

                        rows_in(v.snap(BODIES * w), 0)
                        with v.Fori(0, BODIES - 1) as it:
                            body(v.snap(BODIES * w + it))
                        body(v.snap(BODIES * w + BODIES - 1), final=True)
                        for k in range(2):
                            for t in range(NT):
                                r = ROWS[t]
                                v.wait_ge(got_in[k * NT + t], 16 * (w + 1))
                                if k:
                                    v.wait_ge(summed, 2 * NT * w + t + 2)
                                else:
                                    v.wait_ge(summed, 2 * NT * w + 1)
                                v.scalar_tensor_tensor(out=acc[0:r, t, :], in0=places[k * NT + t][0:r, :],
                                                       scalar=gw[0:r, k, t:t + 1], in1=acc[0:r, t, :],
                                                       op0=ALU.mult, op1=ALU.add).then_inc(summed, 1)

        dq_in, uq_in, uk_in = map(sem, ["dq_in", "uq_in", "uk_in"])
        UQ = AH * (NOPE + ROPE)
        w_dqkv = ring[:, 0, 0:KD * DQKV]
        w_uq = ring[:, 1, 0:3 * UQ]
        w_ukT = ring[:, 2, 0:AH * KL]
        w_uv = ring[:, 2, AH * KL:2 * AH * KL]

        def w_o(k):
            return ring[:, 3, k * D:(k + 1) * D] if k < 6 else ring[:, 2, (k - 2) * D:(k - 1) * D]

        def load_attention(sp, wait):
            wait(0)
            sp.dma_start(w_dqkv, a["w_dqkv"]).then_inc(dq_in, 16)
            wait(1)
            sp.dma_start(w_uq, a["w_uq"]).then_inc(uq_in, 16)
            wait(2)
            sp.dma_start(w_ukT, a["w_ukT"]).then_inc(uk_in, 16)
            sp.dma_start(w_uv, a["w_uv"]).then_inc(wo_in, 16)
            sp.dma_start(ring[:, 2, 4 * D:6 * D], a["w_o"][:, 6:8, :]).then_inc(wo_in, 16)
            wait(3)
            sp.dma_start(ring[:, 3, 0:6 * D], a["w_o"][:, 0:6, :]).then_inc(wo_in, 16)

        def attention():
            with ExitStack() as att:
                L = buf(att, "L", [P, NT, DQKV])
                kvT = buf(att, "kvT", [P, 2, TOK])
                krT = buf(att, "krT", [ROPE, TOK])
                qlatT = buf(att, "qlatT", [P, 2, AH, TOK])
                qrT = buf(att, "qrT", [ROPE, AH, TOK])
                pages = buf(att, "pages", [1, DEC_B * PAGES], I32)
                latents(L, kvT, krT, qlatT, qrT, pages)
                with ExitStack() as st:
                    olatT = buf(st, "olatT", [P, 2, AH, TOK])
                    rope3 = buf(st, "rope3", [ROPE, PAST // 2])
                    slots = [(ring[:, b, 0:2048], ring[:, b, 2048:4096],
                              ring[0:ROPE, b, 4096:4608], ring[0:ROPE, b, 4608:5120]) for b in range(2)]
                    xt = XT[:, :, :].rearrange("p k t -> p (k t)")
                    slots.append((xt[:, 0:2048], lnp[:, :, :].rearrange("p a d -> p (a d)"),
                                  xt[0:ROPE, 2048:2560], rope3[:, :]))
                    prompt_attention(L, kvT, krT, qlatT, qrT, olatT, pages, slots)
                    sample_attention(L, kvT, krT, qlatT, qrT, olatT, pages, slots)
                    attention_output(olatT)

        def latents(L, kvT, krT, qlatT, qrT, pages):
            with ExitStack() as st:
                s = phase_semaphores(st)
                cqT = buf(st, "cqT", [P, 3, TOK])
                qnT = buf(st, "qnT", [P, 2, TOK])
                qkn = buf(st, "qkn", [P, QL + KL])
                ss = buf(st, "ss", [P, NT, 2])
                sqs = buf(st, "sqs", [P, QL])
                qr = buf(st, "qr", [P, 2, AH, ROPE])
                r4 = buf(st, "r4", [P, 4, AH, ROPE // 2])
                kr4 = buf(st, "kr4", [P, 4, NT, ROPE // 2])
                (small_in, dq_done, l_copied, ss_done, std_done, norm_done, kr_done, turned, tcopied,
                 qn_done, qn_copied, ql_done, ql_copied, qr_done, qr_ready, qrt_done, qrt_copied, out_done, dve) = map(s, [
                     "small_in", "dq_done", "l_copied", "ss_done", "std_done", "norm_done",
                     "kr_done", "turned", "tcopied", "qn_done", "qn_copied", "ql_done", "ql_copied", "qr_done",
                     "qr_ready", "qrt_done", "qrt_copied", "out_done", "dve"])
                block = st.enter_context(nc.Block())

                @block.sync
                def _(sp):
                    sp.dma_start(qkn[:, :], a["qkn"]).then_inc(small_in, 16)
                    sp.dma_start(pages[:, :], a["pages"]).then_inc(small_in, 16)
                    load_router(sp, 1)
                    sp.wait_ge(norm_done, NT)
                    sp.dma_start(o["lat"], L[:, :, QL:QL + KL]).then_inc(out_done, 16)
                    sp.wait_ge(kr_done, 1)
                    sp.dma_start(o["kr"], L[:, :, QL + KL:DQKV]).then_inc(out_done, 16)
                    sp.wait_ge(out_done, 32)
                    sp.wait_ge(small_in, 32)

                TB = (4, 5)
                turns = [(L, i * P, P, (cqT, i)) for i in range(3)] + [(L, QL + i * P, P, (kvT, i)) for i in range(2)]

                @block.tensor
                def _(pe):
                    pe.wait_ge(dq_in, 16)
                    for t in range(NT):
                        r = ROWS[t]
                        if t == 2:
                            pe.wait_ge(l_copied, 1)
                        for n, (lo, hi) in enumerate(((0, 512), (512, DQKV))):
                            for k in range(KD):
                                mm = pe.matmul(ps[0:r, 2 * (t % 2) + n, 0:hi - lo], XT[:, k, OFF[t]:OFF[t] + r],
                                               w_dqkv[:, k * DQKV + lo:k * DQKV + hi], start=(k == 0), stop=(k == KD - 1))
                        mm.then_inc(dq_done, 1)
                    pe.wait_ge(norm_done, NT)
                    for n in range(6):
                        if n >= 2:
                            pe.wait_ge(tcopied, n - 1)
                        if n == 5:
                            pe.wait_ge(kr_done, 1)
                        lo, w = (n * P, P) if n < 5 else (QL + KL, ROPE)
                        for t in range(NT):
                            r = ROWS[t]
                            tr = pe.transpose(ps[0:w, TB[n % 2], OFF[t]:OFF[t] + r], L[0:r, t, lo:lo + w], ident[0:r, 0:r])
                        tr.then_inc(turned, 1)
                    pe.wait_ge(tcopied, 3)
                    pe.wait_ge(uq_in, 16)
                    pe.wait_ge(l_copied, NT)

                    def nope(h):
                        if h >= 2:
                            pe.wait_ge(qn_copied, h - 1)
                        for k in range(3):
                            mm = pe.matmul(ps[:, h % 2, 0:TOK], w_uq[:, k * UQ + h * NOPE:k * UQ + (h + 1) * NOPE],
                                           cqT[:, k, :], start=(k == 0), stop=(k == 2))
                        mm.then_inc(qn_done, 1)

                    def absorb(h):
                        pe.wait_ge(qn_copied, h + 1)
                        if h == 0:
                            pe.wait_ge(uk_in, 16)
                        else:
                            pe.wait_ge(ql_copied, 2 * h)
                        for c in range(2):
                            pe.matmul(ps[:, 2 + c, 0:TOK], w_ukT[:, h * KL + c * P:h * KL + (c + 1) * P],
                                      qnT[:, h % 2, :], start=True, stop=True).then_inc(ql_done, 1)

                    for h in range(AH):
                        nope(h)
                        if h:
                            absorb(h - 1)
                    absorb(AH - 1)
                    pe.wait_ge(tcopied, 6)

                    def rope_in(t):
                        r = ROWS[t]
                        if t == 2:
                            pe.wait_ge(qr_ready, 1)
                        for k in range(3):
                            mm = pe.matmul(ps[0:r, TB[t % 2], :], cqT[:, k, OFF[t]:OFF[t] + r],
                                           w_uq[:, k * UQ + AH * NOPE:(k + 1) * UQ], start=(k == 0), stop=(k == 2))
                        mm.then_inc(qr_done, 1)

                    def rope_turn(t):
                        r = ROWS[t]
                        pe.wait_ge(qr_ready, t + 1)
                        for half in range(2):
                            if t:
                                pe.wait_ge(qrt_copied, 2 * t + half - 1)
                            for j in range(4):
                                tr = pe.transpose(ps[0:ROPE, 6 + half, j * P:j * P + r], qr[0:r, t % 2, 4 * half + j, :],
                                                  ident[0:r, 0:r])
                            tr.then_inc(qrt_done, 1)

                    rope_in(0)
                    rope_in(1)
                    rope_turn(0)
                    rope_in(2)
                    rope_turn(1)
                    rope_turn(2)

                @block.scalar
                def _(act):
                    for t in range(NT):
                        r = ROWS[t]
                        act.wait_ge(dq_done, t + 1)
                        if t == 2:
                            act.wait_ge(dve, 1)
                        b = 2 * (t % 2)
                        act.activation(L[0:r, t, 0:512], ps[0:r, b, :], ACT.Copy)
                        act.activation(L[0:r, t, 512:DQKV], ps[0:r, b + 1, 0:DQKV - 512], ACT.Copy).then_inc(l_copied, 1)
                    for t in range(NT):
                        r = ROWS[t]
                        act.wait_ge(ss_done, 2 * t + 2)
                        for n, w in enumerate((QL, KL)):
                            ins = act.activation(ss[0:r, t, n:n + 1], ss[0:r, t, n:n + 1], ACT.Sqrt, scale=1.0 / w,
                                                 bias=eps[0:r, 1:2])
                        ins.then_inc(std_done, 1)
                    for n in range(6):
                        act.wait_ge(turned, n + 1)
                        dst = cqT[:, n, :] if n < 3 else kvT[:, n - 3, :] if n < 5 else krT[:, :]
                        w = P if n < 5 else ROPE
                        act.activation(dst, ps[0:w, TB[n % 2], 0:TOK], ACT.Copy).then_inc(tcopied, 1)
                    for h in range(AH):
                        for c in range(2):
                            act.wait_ge(ql_done, 2 * h + c + 1)
                            act.activation(qlatT[:, c, h, :], ps[:, 2 + c, 0:TOK], ACT.Copy).then_inc(ql_copied, 1)
                    for t in range(NT):
                        r = ROWS[t]
                        for half in range(2):
                            act.wait_ge(qrt_done, 2 * t + half + 1)
                            act.activation(qrT[:, 4 * half:4 * half + 4, OFF[t]:OFF[t] + r],
                                           ps[0:ROPE, 6 + half, :].rearrange("p (j s) -> p j s", j=4)[:, :, 0:r],
                                           ACT.Copy).then_inc(qrt_copied, 1)

                @block.vector
                def _(v):
                    step = Tally(dve)
                    step.mark(v.memset(L[64:P, 2, :], 0.0))
                    cos, sin = const3("cos"), const3("sin")
                    for t in range(NT):
                        r = ROWS[t]
                        v.wait_ge(l_copied, t + 1)
                        for n, (lo, w) in enumerate(((0, QL), (QL, KL))):
                            x = L[0:r, t, lo:lo + w]
                            if t + n:
                                v.wait_ge(ss_done, 2 * t + n)
                            v.tensor_tensor_reduce(sqs[0:r, 0:w], x, x, 1.0, 0.0, ALU.mult, ALU.add,
                                                   ss[0:r, t, n:n + 1]).then_inc(ss_done, 1)
                    v.wait_ge(small_in, 32)
                    for t in range(NT):
                        r = ROWS[t]
                        v.wait_ge(std_done, t + 1)
                        step.mark(v.reciprocal(ss[0:r, t, :], ss[0:r, t, :]))
                        step.settle(v)
                        for n, (lo, w) in enumerate(((0, QL), (QL, KL))):
                            x = L[0:r, t, lo:lo + w]
                            ins = v.scalar_tensor_tensor(out=x, in0=x, scalar=ss[0:r, t, n:n + 1], in1=qkn[0:r, lo:lo + w],
                                                         op0=ALU.mult, op1=ALU.mult)
                        ins.then_inc(norm_done, 1)

                    def rotate(out1, out2, x1, x2, c, sn, tmp4):
                        v.tensor_tensor(tmp4[0], x1, c, ALU.mult)
                        v.tensor_tensor(tmp4[1], x2, sn, ALU.mult)
                        v.tensor_tensor(tmp4[2], x2, c, ALU.mult)
                        step.mark(v.tensor_tensor(tmp4[3], x1, sn, ALU.mult))
                        step.settle(v)
                        v.tensor_tensor(out1, tmp4[0], tmp4[1], ALU.subtract)
                        return v.tensor_tensor(out2, tmp4[2], tmp4[3], ALU.add)

                    k1, k2 = L[:, :, QL + KL:QL + KL + 32], L[:, :, QL + KL + 32:DQKV]
                    rotate(k1, k2, k1, k2, cos, sin, [kr4[:, i, :, :] for i in range(4)]).then_inc(kr_done, 1)
                    for h in range(AH):
                        v.wait_ge(qn_done, h + 1)
                        if h >= 2:
                            v.wait_ge(ql_done, 2 * (h - 1))
                        v.tensor_copy(qnT[:, h % 2, :], ps[:, h % 2, 0:TOK]).then_inc(qn_copied, 1)
                    for t in range(NT):
                        r = ROWS[t]
                        v.wait_ge(qr_done, t + 1)
                        if t == 2:
                            v.wait_ge(qrt_done, 2)
                        x = ps[0:r, TB[t % 2], :].rearrange("p (h e) -> p h e", h=AH)
                        cb = cos[0:r, t, :].unsqueeze(1).to_broadcast([r, AH, 32])
                        sb = sin[0:r, t, :].unsqueeze(1).to_broadcast([r, AH, 32])
                        q = qr[0:r, t % 2, :, :]
                        if t:
                            v.wait_ge(qr_ready, t)
                        rotate(q[:, :, 0:32], q[:, :, 32:64], x[:, :, 0:32], x[:, :, 32:64], cb, sb,
                               [r4[0:r, i, :, :] for i in range(4)]).then_inc(qr_ready, 1)

        def load_keys(sp, pages, slot, n, wait=None):
            numbers = [sp.value_load(pages[0:1, n * PAGES + i:n * PAGES + i + 1], min_val=0, max_val=a["latent"].shape[0] - 1)
                       for i in range(PAGES)]
            if wait is not None:
                sp.wait_ge(*wait)
            for i, page in enumerate(numbers):
                lat = a["latent"][ds(page, 1)].rearrange("a p n -> (a p) n")
                kr = a["krope"][ds(page, 1)].rearrange("a p n -> (a p) n")
                sp.dma_start(slot[i // 4][:, i % 4 * 512:(i % 4 + 1) * 512], lat).then_inc(key_in[n % 3], 16)
                sp.dma_start(slot[2 + i // 4][:, i % 4 * PAGE:(i % 4 + 1) * PAGE], kr).then_inc(key_in[n % 3], 16)

        def prompt_attention(L, kvT, krT, qlatT, qrT, olatT, pages, slots):
            with ExitStack() as st:
                s = phase_semaphores(st)
                pr = buf(st, "pr", [P, 2, 2 * P])
                pT = buf(st, "pT", [P, 2, 2, P])
                nm = buf(st, "nm", [P, 2])
                sm = buf(st, "sm", [P, 2])
                sc_done, masked, max_done, exp_done, p_done, pt_done, pt_copied, o_done, o_copied, dve = map(s, [
                    "sc_done", "masked", "max_done", "exp_done", "p_done", "pt_done", "pt_copied", "o_done", "o_copied",
                    "dve"])
                block = st.enter_context(nc.Block())
                units = [(i, h) for i in range(2) for h in range(AH)]
                N = len(units)
                SB, TB, OB = (0, 1), (2, 3), (4, 5)

                @block.sync
                def _(sp):
                    for n in range(3):
                        load_keys(sp, pages, slots[n], n)

                @block.tensor
                def _(pe):
                    def scores(u):
                        i, h = units[u]
                        q, nk = slice(i * P, (i + 1) * P), (i + 1) * P
                        if u >= 2:
                            pe.wait_ge(masked, u - 1)
                        out = ps[:, SB[u % 2], 0:nk]
                        for c in range(2):
                            pe.matmul(out, qlatT[:, c, h, q], kvT[:, c, 0:nk], start=(c == 0), stop=False)
                        pe.matmul(out, qrT[:, h, q], krT[:, 0:nk], start=False, stop=True).then_inc(sc_done, 1)

                    def turn(u):
                        i, h = units[u]
                        pe.wait_ge(p_done, u + 1)
                        if u >= 2:
                            pe.wait_ge(pt_copied, u - 1)
                        for k in range(i + 1):
                            tr = pe.transpose(ps[:, TB[u % 2], k * P:(k + 1) * P], pr[:, u % 2, k * P:(k + 1) * P], ident)
                        tr.then_inc(pt_done, 1)

                    def values(u):
                        i, h = units[u]
                        pe.wait_ge(pt_copied, u + 1)
                        if u >= 2:
                            pe.wait_ge(o_copied, u - 1)
                        for c in range(2):
                            for k in range(i + 1):
                                mm = pe.matmul(ps[:, OB[u % 2], c * P:(c + 1) * P], L[:, k, QL + c * P:QL + (c + 1) * P],
                                               pT[:, u % 2, k, :], start=(k == 0), stop=(k == i))
                        mm.then_inc(o_done, 1)

                    for u in range(N + 2):
                        if u < N:
                            scores(u)
                        if 1 <= u <= N:
                            turn(u - 1)
                        if u >= 2:
                            values(u - 2)

                @block.vector
                def _(v):
                    def mask(u):
                        i, h = units[u]
                        nk = (i + 1) * P
                        v.wait_ge(sc_done, u + 1)
                        if u >= 2:
                            v.wait_ge(pt_done, u - 1)
                        v.scalar_tensor_tensor(out=pr[:, u % 2, 0:nk], in0=ps[:, SB[u % 2], 0:nk], scalar=ATT_SCALE,
                                               in1=C[:, CONST["causal"].stop - nk:CONST["causal"].stop],
                                               op0=ALU.mult, op1=ALU.add).then_inc(masked, 1)
                        v.wait_ge(masked, u + 1)
                        v.tensor_reduce(nm[:, u % 2:u % 2 + 1], pr[:, u % 2, 0:nk], X_AXIS, ALU.max,
                                        negate=True).then_inc(max_done, 1)

                    step = Tally(dve)

                    def normalise(u):
                        i, h = units[u]
                        v.wait_ge(exp_done, u + 1)
                        sc = sm[:, u % 2:u % 2 + 1]
                        step.mark(v.reciprocal(sc, sc))
                        step.settle(v)
                        x = pr[:, u % 2, 0:(i + 1) * P]
                        v.tensor_scalar(x, x, sc, None, ALU.mult).then_inc(p_done, 1)

                    for u in range(N + 1):
                        if u < N:
                            mask(u)
                        if u >= 1:
                            normalise(u - 1)

                @block.scalar
                def _(act):
                    for u in range(N + 2):
                        if u < N:
                            i, h = units[u]
                            act.wait_ge(max_done, u + 1)
                            if u >= 2:
                                act.wait_ge(p_done, u - 1)
                            x = pr[:, u % 2, 0:(i + 1) * P]
                            act.activation(x, x, ACT.Exp, bias=nm[:, u % 2:u % 2 + 1],
                                           accum_out=sm[:, u % 2:u % 2 + 1]).then_inc(exp_done, 1)
                        if 1 <= u <= N:
                            i, h = units[u - 1]
                            act.wait_ge(pt_done, u)
                            if u >= 3:
                                act.wait_ge(o_done, u - 2)
                            act.activation(pT[:, (u - 1) % 2, 0:i + 1, :],
                                           ps[:, TB[(u - 1) % 2], 0:(i + 1) * P].rearrange("p (k q) -> p k q", k=i + 1),
                                           ACT.Copy).then_inc(pt_copied, 1)
                        if u >= 2:
                            i, h = units[u - 2]
                            act.wait_ge(o_done, u - 1)
                            act.activation(olatT[:, :, h, i * P:(i + 1) * P],
                                           ps[:, OB[u % 2], 0:2 * P].rearrange("p (c q) -> p c q", c=2),
                                           ACT.Copy).then_inc(o_copied, 1)

        def sample_attention(L, kvT, krT, qlatT, qrT, olatT, pages, slots):
            with ExitStack() as st:
                s = phase_semaphores(st)
                W = PAST + 64
                pr = buf(st, "pr", [64, 2, W])
                qb = buf(st, "qb", [P, 2, 2, 64])
                qrb = ring[0:ROPE, 0:2, 5696:5760]
                small = buf(st, "small", [64, 2, 8])
                q_done, sc_done, sc_read, max_done, exp_done, p_done, pt_done, pt_copied, o_done, o_copied, dve = map(s, [
                    "q_done", "sc_done", "sc_read", "max_done", "exp_done", "p_done", "pt_done", "pt_copied", "o_done",
                    "o_copied", "dve"])
                passed = s("passed")
                block = st.enter_context(nc.Block())
                pTs = [ring[:, b, 5120:5120 + 9 * 64] for b in range(2)]
                SB, TB, NB = ((0, 1, 2), (3, 4, 5)), 6, 7

                def lat(n, i):
                    return slots[n % 3][i // 4][:, i % 4 * 512:i % 4 * 512 + KL]

                @block.sync
                def _(sp):
                    for n in range(3, DEC_B):
                        load_keys(sp, pages, slots[n % 3], n, (o_done, n - 2))

                @block.gpsimd
                def _(pool):
                    with pool.Fori(0, 4) as it:
                        for b in range(2):
                            n = 2 * it + b
                            at = ds(SEQ + DEC_T * n, DEC_T)
                            pool.wait_ge(sc_done, 2 * it + 1)
                            for c in range(2):
                                pool.tensor_copy(qb[:, b, c, :].rearrange("p (t h) -> p t h", h=AH),
                                                 qlatT[:, c, :, at].rearrange("p h t -> p t h"))
                            pool.tensor_copy(qrb[:, b, :].rearrange("p (t h) -> p t h", h=AH),
                                             qrT[:, :, at].rearrange("p h t -> p t h")).then_inc(q_done, 1)

                @block.tensor
                def _(pe):
                    def scores(n):
                        b, slot = n % 2, slots[n % 3]
                        pe.wait_ge(q_done, n + 1)
                        pe.wait_ge(key_in[n % 3], 256 * (n // 3 + 1))
                        if n >= 2:
                            pe.wait_ge(sc_read, n)
                        for half in range(2):
                            out = ps[0:64, SB[b][half], :]
                            for c in range(2):
                                keys = slot[half].rearrange("p (i w) -> p i w", w=512)
                                pe.matmul(out, qb[:, b, c, :], keys[:, :, KL + c * PAGE:KL + (c + 1) * PAGE],
                                          start=(c == 0), stop=False)
                            pe.matmul(out, qrb[:, b, :], slot[2 + half],
                                      start=False, stop=True)
                        out = ps[0:64, SB[b][2], 0:64]
                        for c in range(2):
                            pe.matmul(out, qb[:, b, c, :], kvT[:, c, SAMPLE], start=(c == 0), stop=False)
                        pe.matmul(out, qrb[:, b, :], krT[:, SAMPLE], start=False, stop=True).then_inc(sc_done, 1)

                    def values(n):
                        b = n % 2
                        pe.wait_ge(p_done, n + 1)
                        pe.wait_ge(o_copied, n + 1)
                        pe.sem_inc(passed, 1)
                        for i in range(PAGES):
                            pe.transpose(ps[:, TB, i * 64:(i + 1) * 64], pr[:, b, i * P:(i + 1) * P], ident[0:64, 0:64])
                        pe.transpose(ps[0:64, NB, 0:64], pr[:, b, PAST:W], ident[0:64, 0:64]).then_inc(pt_done, 1)
                        pe.wait_ge(pt_copied, n + 1)
                        for c in range(2):
                            out = ps[:, NB, P + c * 64:P + (c + 1) * 64]
                            for i in range(PAGES):
                                pe.matmul(out, lat(n, i)[:, c * P:(c + 1) * P], pTs[b][:, i * 64:(i + 1) * 64],
                                          start=(i == 0), stop=False)
                            mm = pe.matmul(out, L[0:64, 2, QL + c * P:QL + (c + 1) * P], pTs[b][0:64, 512:576],
                                           start=False, stop=True)
                        mm.then_inc(o_done, 1)

                    credit(pe, sc_done, pt_done)
                    scores(0)
                    for n in range(DEC_B):
                        if n + 1 < DEC_B:
                            scores(n + 1)
                        values(n)

                @block.vector
                def _(v):
                    step = Tally(dve)

                    def do(ins):
                        step.mark(ins)
                        step.settle(v)

                    def col(b, i):
                        return small[:, b, i:i + 1]

                    PER = 6
                    with v.Fori(0, 4) as it:
                        for b in range(2):
                            n = v.snap(2 * it + b)
                            step.loop(v.snap(n * PER))
                            v.wait_ge(sc_done, n + 2)
                            v.wait_ge(pt_done, 2 * it + 1)
                            past = ps[0:64, SB[b][0]:SB[b][0] + 2, :].rearrange("p a k -> p (a k)")
                            new = pr[:, b, PAST:W]
                            msk = C[0:64, ds(CONST["smask"].start + n * 64, 64)]
                            do(v.scalar_tensor_tensor(out=new, in0=ps[0:64, SB[b][2], 0:64], scalar=ATT_SCALE, in1=msk,
                                                      op0=ALU.mult, op1=ALU.add))
                            do(v.tensor_reduce(col(b, 0), past, X_AXIS, ALU.max))
                            do(v.tensor_reduce(col(b, 1), new, X_AXIS, ALU.max))
                            do(v.scalar_tensor_tensor(out=col(b, 2), in0=col(b, 0), scalar=ATT_SCALE, in1=col(b, 1),
                                                      op0=ALU.mult, op1=ALU.max))
                            v.tensor_scalar(col(b, 3), col(b, 2), -1.0, None, ALU.mult).then_inc(max_done, 1)
                            v.wait_ge(exp_done, n + 1)
                            do(v.tensor_tensor(col(b, 4), col(b, 4), col(b, 5), ALU.add))
                            do(v.reciprocal(col(b, 4), col(b, 4)))
                            v.tensor_scalar(pr[:, b, :], pr[:, b, :], col(b, 4), None, ALU.mult).then_inc(p_done, 1)

                @block.scalar
                def _(act):
                    credit(act, sc_read, o_copied)
                    with act.Fori(0, 4) as it:
                        for b in range(2):
                            n = act.snap(2 * it + b)
                            past = ps[0:64, SB[b][0]:SB[b][0] + 2, :].rearrange("p a k -> p (a k)")
                            act.wait_ge(max_done, n + 1)
                            act.activation(pr[:, b, 0:PAST], past, ACT.Exp, bias=small[:, b, 3:4], scale=ATT_SCALE,
                                           accum_out=small[:, b, 4:5]).then_inc(sc_read, 1)
                            act.activation(pr[:, b, PAST:W], pr[:, b, PAST:W], ACT.Exp, bias=small[:, b, 3:4],
                                           accum_out=small[:, b, 5:6]).then_inc(exp_done, 1)
                            act.wait_ge(pt_done, n + 2)
                            act.activation(pTs[b][:, 0:512], ps[:, TB, :], ACT.Copy)
                            act.activation(pTs[b][0:64, 512:576], ps[0:64, NB, 0:64], ACT.Copy).then_inc(pt_copied, 1)
                            act.wait_ge(o_done, n + 1)
                            at = ds(SEQ + DEC_T * n, DEC_T)
                            for c in range(2):
                                ins = act.activation(
                                    olatT[:, c, :, at],
                                    ps[:, NB, P + c * 64:P + (c + 1) * 64].rearrange("p (t h) -> p h t", h=AH), ACT.Copy)
                            ins.then_inc(o_copied, 1)

        def attention_output(olatT):
            with ExitStack() as st:
                s = phase_semaphores(st)
                v_done, v_copied, wo_used = s("v_done"), s("v_copied"), s("wo_used")
                block = st.enter_context(nc.Block())

                @block.sync
                def _(sp):
                    sp.dma_start(lnp[:, :, :], a["ln"][2]).then_inc(ln_in, 16)
                    first_expert(sp, 1, 0)
                    first_expert(sp, 1, 1)
                    sp.wait_ge(wo_used, 6)
                    first_expert(sp, 1, 3)
                    sp.wait_ge(wo_used, 8)
                    first_expert(sp, 1, 2)
                VB = (6, 7)

                @block.tensor
                def _(pe):
                    pe.wait_ge(wo_in, 48)

                    def head(h):
                        if h >= 2:
                            pe.wait_ge(v_copied, h - 1)
                        for c in range(2):
                            mm = pe.matmul(ps[:, VB[h % 2], 0:TOK],
                                           w_uv[:, c * AH * VH + h * VH:c * AH * VH + (h + 1) * VH],
                                           olatT[:, c, h, :], start=(c == 0), stop=(c == 1))
                        mm.then_inc(v_done, 1)

                    def project(h):
                        pe.wait_ge(v_copied, h + 1)
                        for t in range(NT):
                            for n in range(2):
                                mm = pe.matmul(ps[0:ROWS[t], 2 * t + n, :], XT[:, h, OFF[t]:OFF[t] + ROWS[t]],
                                               w_o(h)[:, n * 512:(n + 1) * 512], start=(h == 0), stop=(h == AH - 1))
                        mm.then_inc(wo_used, 1)

                    head(0)
                    for h in range(AH):
                        if h + 1 < AH:
                            head(h + 1)
                        project(h)

                @block.scalar
                def _(act):
                    for h in range(AH):
                        act.wait_ge(v_done, h + 1)
                        act.activation(XT[:, h, :], ps[:, VB[h % 2], 0:TOK], ACT.Copy).then_inc(v_copied, 1)

        in_projection()
        for c in range(NT):
            scan_chunk(c)
        sample_states()
        out_projection()
        ssd.close()

        def in_psum(t):
            return ps[0:ROWS[t], 2 * t:2 * t + 2, :].rearrange("p a n -> p (a n)")

        layer_norm("a0", in_psum, 1)
        for layer in range(2):
            if layer == 1:
                attention()
                layer_norm("a1", in_psum, 3)
            with ExitStack() as ffn:
                acc = buf(ffn, "acc", [P, NT, D])
                moe(layer, acc, None if layer else load_attention)
                layer_norm(f"f{layer}", lambda t: acc[0:ROWS[t], t, :], 2 * layer + 2)


def _lay_out(i):
    def by_k(w):
        return w.reshape(-1, P, w.shape[-1]).transpose(1, 0, 2)

    x = np.zeros((NT * P, D), np.float32)
    x[:TOK] = np.concatenate([i["x_prompt"].reshape(SEQ, D), i["x_sample"].reshape(-1, D)])
    w_in = i["ssd_w_in"][0]
    cw = i["ssd_conv_w"][0].reshape(4, XBCB, P).transpose(2, 1, 0).reshape(P, 4 * XBCB)
    cb = i["ssd_conv_b"][0].reshape(XBCB, P).T
    nw = i["ssd_norm_w"][0].reshape(ZB, P).T
    dk = np.repeat(i["ssd_d_skip"][0], HP).reshape(ZB, P).T
    conv = i["state_conv"][0].reshape(DEC_B, 3, XBCB, P).transpose(3, 2, 0, 1)
    rows = np.stack([i["ssd_dt_bias"][0], i["ssd_a_log"][0]])
    ln = np.stack([np.stack([i[f"ln_{k}_{g}"][l] for g in "gb"]) for l in range(2) for k in ("mix", "ffn")])
    experts = []
    for l in range(2):
        gate, up = (i[n][l].reshape(EXPERTS, KD, P, FF).transpose(0, 2, 1, 3).reshape(EXPERTS, P, KD * FF)
                    for n in ("moe_w_gate", "moe_w_up"))
        down = i["moe_w_down"][l].reshape(EXPERTS, 2, P, D).transpose(0, 2, 1, 3).reshape(EXPERTS, P, 2 * D)
        experts.append(np.concatenate([gate, up, down], axis=2))
    uq = i["mla_w_uq"][0].reshape(3, P, AH, NOPE + ROPE).transpose(1, 0, 2, 3)
    lat, kr = i["cache_mla_latent"][0], i["cache_mla_krope"][0]
    latT = lat.transpose(0, 2, 1).reshape(-1, 2, P, PAGE).transpose(0, 2, 1, 3).reshape(-1, P, 2 * PAGE)
    out = {
        "xT": by_k(x[:TOK].T),
        "x": x.reshape(NT, P, D).transpose(1, 0, 2),
        "w_in": w_in[:, :INNER + XBCB * P].reshape(KD, P, 10, 512).transpose(2, 1, 0, 3).reshape(10, P, KD * 512),
        "w_dt": by_k(w_in[:, INNER + XBCB * P:]),
        "cols": np.concatenate([cw, cb, nw, dk], axis=1),
        "conv": conv,
        "rows": np.broadcast_to(rows, (P, 2, HEADS)),
        "w_out": by_k(i["ssd_w_out"][0]).reshape(P, 4, 4 * D).transpose(1, 0, 2),
        "state": i["state_ssd"][0].reshape(DEC_B, INNER, STATE).transpose(0, 2, 1),
        "ln": np.broadcast_to(ln[:, None], (4, P, 2, D)),
        "router": np.stack([by_k(i["moe_router"][l]) for l in range(2)]),
        "rbias": np.broadcast_to(i["moe_router_bias"][:, None], (2, P, EXPERTS)),
        "experts": np.concatenate(experts),
        "const": constants(),
        "w_dqkv": by_k(i["mla_w_dqkv"][0]),
        "w_uq": np.concatenate([uq[..., :NOPE].reshape(P, 3, AH * NOPE), uq[..., NOPE:].reshape(P, 3, AH * ROPE)], axis=2),
        "w_ukT": i["mla_w_uk"][0].transpose(2, 1, 0),
        "w_uv": by_k(i["mla_w_uv"][0].reshape(KL, AH * VH)),
        "w_o": by_k(i["mla_w_o"][0]),
        "qkn": np.broadcast_to(np.concatenate([i["mla_q_norm"][0], i["mla_kv_norm"][0]]), (P, QL + KL)),
        "latent": np.concatenate([lat, latT], axis=2),
        "krope": kr.transpose(0, 2, 1),
        "pages": i["page_table"].reshape(1, DEC_B * PAGES),
    }
    return {k: np.ascontiguousarray(v) for k, v in out.items()}


_OUTS = {
    "y": (P, NT, D), "lat": (P, NT, KL), "kr": (P, NT, ROPE), "ssdp": (P, INNER),
    "conv": (P, XBCB, CONVO), "ssds": (DEC_B, P, INNER),
}


def kernel(**inputs):
    import concourse.bacc as bacc
    from concourse.bass_utils import run_bass_kernel_spmd

    arrays = _lay_out({k: np.asarray(v) for k, v in inputs.items()})
    nc = bacc.Bacc("TRN2", target_bir_lowering=False, num_devices=1)
    a = {k: nc.dram_tensor(f"in_{k}", v.shape, mybir.dt.from_np(v.dtype), kind="ExternalInput").ap()
         for k, v in arrays.items()}
    o = {k: nc.dram_tensor(f"out_{k}", s, F32, kind="ExternalOutput").ap() for k, s in _OUTS.items()}
    program(nc, a, o)
    r = run_bass_kernel_spmd(nc, [{f"in_{k}": v for k, v in arrays.items()}], core_ids=[0]).results[0]
    r = {k: r[f"out_{k}"] for k in _OUTS}

    def tokens(v):
        rows = v.transpose(1, 0, 2).reshape(NT * P, -1)
        return rows[:SEQ], rows[SEQ:TOK].reshape(DEC_B, DEC_T, -1)

    yp, ysm = tokens(r["y"])
    lp, lsm = tokens(r["lat"])
    kp, ksm = tokens(r["kr"])
    conv = r["conv"].transpose(2, 1, 0).reshape(CONVO, XBCB * P)
    state = (HEADS, HP, STATE)
    return (yp[None], ysm, lp[None, None], kp[None, None], r["ssdp"].T.reshape(1, 1, *state),
            conv[None, None, :3], lsm[None], ksm[None],
            r["ssds"].transpose(0, 2, 1).reshape(1, DEC_B, *state), conv[3:].reshape(1, DEC_B, 3, XBCB * P))
```
